# Optimizing a Trainium2 kernel written in Bass

```python
import jax, jax.numpy as jnp
from jax import lax
import numpy as np

D_MODEL = 1024
BATCH = 1
SEQ = 512
DEPTH = 2

ALPHA = (2 * DEPTH) ** 0.25
BETA = (8 * DEPTH) ** -0.25
LN_EPS = 1e-5
A_HEADS = 8
A_HEAD_DIM = 64
IDX_HEADS = 8
IDX_DIM = 64
TOPK_MAX = 256
Q_BLOCK = 128
G_HEADS = 4
G_DK = 128
G_DV = 128
G_RANK = 16
G_TAU = 16.0
G_CHUNK = 64
M_INNER = 2 * D_MODEL
M_HEADS = 4
M_DH = M_INNER // M_HEADS
M_CONV = 4
M_QKV_BLOCK = 4
M_CHUNK = 64
D_FF = 4 * D_MODEL

A_WIDTH = A_HEADS * A_HEAD_DIM
G_WIDTH = G_HEADS * G_DV
EVEN_SPLITS = (A_HEADS * A_HEAD_DIM, A_HEAD_DIM, A_HEAD_DIM,
               IDX_HEADS * IDX_DIM, IDX_DIM, IDX_HEADS,
               G_HEADS * G_DK, G_HEADS * G_DK, G_HEADS * G_DV, G_HEADS * G_DV, G_RANK)
EVEN_COLS = sum(EVEN_SPLITS)

kernel_name = "hybrid_dsa_gla_mlstm_deepnorm"

def layer_norm(x, g, b):
    xf = x.astype(jnp.float32)
    mu = jnp.mean(xf, axis=-1, keepdims=True)
    var = jnp.mean(jnp.square(xf - mu), axis=-1, keepdims=True)
    return ((xf - mu) * lax.rsqrt(var + LN_EPS) * g + b).astype(x.dtype)

def head_norm(x, g):
    xf = x.astype(jnp.float32)
    mu = jnp.mean(xf, axis=-1, keepdims=True)
    var = jnp.mean(jnp.square(xf - mu), axis=-1, keepdims=True)
    return (xf - mu) * lax.rsqrt(var + LN_EPS) * g

def to_chunks(t, L):
    B, H, S = t.shape[:3]
    return jnp.moveaxis(t.reshape(B, H, S // L, L, *t.shape[3:]), 2, 0)

def from_chunks(t):
    t = jnp.moveaxis(t, 0, 2)
    B, H, NC, L = t.shape[:4]
    return t.reshape(B, H, NC * L, *t.shape[4:])

def dsa_attention(q, k, v, qi, ki, wi):
    B, S = q.shape[:2]
    topk = min(TOPK_MAX, S // 4)
    nb = S // Q_BLOCK
    key_pos = jnp.arange(S)

    def block(args):
        qb, qib, wib, start = args
        qpos = start + jnp.arange(Q_BLOCK)
        causal = key_pos[None, :] <= qpos[:, None]
        logits = jnp.einsum('bqhd,bsd->bqhs', qib, ki) * IDX_DIM ** -0.5
        score = jnp.einsum('bqh,bqhs->bqs', wib * IDX_HEADS ** -0.5, jax.nn.relu(logits))
        score = jnp.where(causal[None], score.astype(jnp.float32), -jnp.inf)
        _, idx = lax.top_k(score, topk)
        valid = idx <= qpos[None, :, None]
        kg = jax.vmap(lambda kk, ii: kk[ii])(k, idx)
        vg = jax.vmap(lambda vv, ii: vv[ii])(v, idx)
        s = jnp.einsum('bqhd,bqkd->bqhk', qb, kg).astype(jnp.float32) * A_HEAD_DIM ** -0.5
        s = jnp.where(valid[:, :, None, :], s, -jnp.inf)
        p = jax.nn.softmax(s, axis=-1).astype(vg.dtype)
        return jnp.einsum('bqhk,bqkd->bqhd', p, vg)

    def blocks(t):
        return jnp.moveaxis(t.reshape(B, nb, Q_BLOCK, *t.shape[2:]), 1, 0)

    starts = jnp.arange(nb) * Q_BLOCK
    out = lax.map(block, (blocks(q), blocks(qi), blocks(wi), starts))
    return jnp.moveaxis(out, 0, 1).reshape(B, S, A_HEADS * A_HEAD_DIM)

def gla_chunked(q, k, v, log_a):
    B, H = q.shape[:2]
    tri = jnp.tril(jnp.ones((G_CHUNK, G_CHUNK), bool))

    def step(state, inp):
        qc, kc, vc, ac = inp
        bcum = jnp.cumsum(ac, axis=2)
        o_inter = jnp.einsum('bhld,bhde->bhle', qc * jnp.exp(bcum), state)
        diff = bcum[:, :, :, None, :] - bcum[:, :, None, :, :]
        diff = jnp.where(tri[None, None, :, :, None], diff, -jnp.inf)
        att = jnp.einsum('bhtd,bhsd,bhtsd->bhts', qc, kc, jnp.exp(diff))
        o_intra = jnp.einsum('bhts,bhse->bhte', att, vc)
        g = bcum[:, :, -1]
        kd = kc * jnp.exp(g[:, :, None, :] - bcum)
        state = jnp.exp(g)[..., None] * state + jnp.einsum('bhsd,bhse->bhde', kd, vc)
        return state, o_inter + o_intra

    s0 = jnp.zeros((B, H, G_DK, G_DV), jnp.float32)
    _, o = lax.scan(step, s0, (to_chunks(q, G_CHUNK), to_chunks(k, G_CHUNK),
                               to_chunks(v, G_CHUNK), to_chunks(log_a, G_CHUNK)))
    return from_chunks(o)

def mlstm_chunked(q, k, v, li, lf):
    B, H = q.shape[:2]
    tri = jnp.tril(jnp.ones((M_CHUNK, M_CHUNK), bool))

    def step(carry, inp):
        C, n, m = carry
        qc, kc, vc, lic, lfc = inp
        b = jnp.cumsum(lfc, axis=-1)
        D = b[..., :, None] - b[..., None, :] + lic[..., None, :]
        D = jnp.where(tri, D, -jnp.inf)
        inter = b + m[..., None]
        m_t = jnp.maximum(inter, jnp.max(D, axis=-1))
        w_inter = jnp.exp(inter - m_t)
        P = jnp.exp(D - m_t[..., None]) * jnp.einsum('bhtd,bhsd->bhts', qc, kc)
        num = w_inter[..., None] * jnp.einsum('bhtd,bhde->bhte', qc, C) + jnp.einsum('bhts,bhse->bhte', P, vc)
        den = w_inter * jnp.einsum('bhtd,bhd->bht', qc, n) + jnp.sum(P, axis=-1)
        h = num / jnp.maximum(jnp.abs(den), jnp.exp(-m_t))[..., None]
        g = b[..., -1]
        d_end = g[..., None] - b + lic
        m_new = jnp.maximum(g + m, jnp.max(d_end, axis=-1))
        wk = jnp.exp(d_end - m_new[..., None])
        decay = jnp.exp(g + m - m_new)
        C = decay[..., None, None] * C + jnp.einsum('bhs,bhsd,bhse->bhde', wk, kc, vc)
        n = decay[..., None] * n + jnp.einsum('bhs,bhsd->bhd', wk, kc)
        return (C, n, m_new), h

    init = (jnp.zeros((B, H, M_DH, M_DH), jnp.float32), jnp.zeros((B, H, M_DH), jnp.float32),
            jnp.zeros((B, H), jnp.float32))
    _, h = lax.scan(step, init, (to_chunks(q, M_CHUNK), to_chunks(k, M_CHUNK), to_chunks(v, M_CHUNK),
                                 to_chunks(li, M_CHUNK), to_chunks(lf, M_CHUNK)))
    return from_chunks(h)

def causal_conv(x, w):
    return lax.conv_general_dilated(x, w[:, None, :].astype(x.dtype), window_strides=(1,),
                                    padding=[(w.shape[0] - 1, 0)],
                                    dimension_numbers=('NWC', 'WIO', 'NWC'),
                                    feature_group_count=x.shape[-1])

def even_mixer(x, w_in, g_w2, g_b2, g_norm, w_out):
    B, S, _ = x.shape
    split_idx = np.cumsum(EVEN_SPLITS)[:-1].tolist()
    (a_q, a_k, a_v, i_q, i_k, i_w,
     g_q, g_k, g_v, g_r, g_lr) = jnp.split(x @ w_in, split_idx, axis=-1)
    a_out = dsa_attention(a_q.reshape(B, S, A_HEADS, A_HEAD_DIM), a_k, a_v,
                          i_q.reshape(B, S, IDX_HEADS, IDX_DIM), i_k, i_w)
    log_a = jax.nn.log_sigmoid((g_lr @ g_w2 + g_b2).astype(jnp.float32)) / G_TAU

    def heads(t, d):
        return t.reshape(B, S, G_HEADS, d).transpose(0, 2, 1, 3).astype(jnp.float32)

    o = gla_chunked(heads(g_q, G_DK) * G_DK ** -0.5, heads(g_k, G_DK), heads(g_v, G_DV), heads(log_a, G_DK))
    o = head_norm(o.transpose(0, 2, 1, 3), g_norm).reshape(B, S, G_WIDTH).astype(x.dtype)
    o = o * jax.nn.silu(g_r)
    return jnp.concatenate([a_out, o], axis=-1) @ w_out

def odd_mixer(x, w_in, conv_w, conv_b, w_q, w_k, w_v, w_gate, b_gate, skip, norm_g, w_out):
    B, S, _ = x.shape
    x_m, o_pre = jnp.split(x @ w_in, 2, axis=-1)
    x_c = jax.nn.silu(causal_conv(x_m, conv_w) + conv_b)

    def blockdiag(t, w):
        t = t.reshape(B, S, M_INNER // M_QKV_BLOCK, M_QKV_BLOCK)
        return jnp.einsum('bsnd,nde->bsne', t, w).reshape(B, S, M_INNER)

    q = blockdiag(x_c, w_q)
    k = blockdiag(x_c, w_k)
    v = blockdiag(x_m, w_v)
    gates = (jnp.concatenate([q, k, v], axis=-1) @ w_gate + b_gate).astype(jnp.float32)
    i_pre, f_pre = jnp.split(gates.transpose(0, 2, 1), 2, axis=1)

    def heads(t):
        return t.reshape(B, S, M_HEADS, M_DH).transpose(0, 2, 1, 3).astype(jnp.float32)

    h = mlstm_chunked(heads(q), heads(k) * M_DH ** -0.5, heads(v), i_pre, jax.nn.log_sigmoid(f_pre))
    h = h.transpose(0, 2, 1, 3) * jax.nn.sigmoid(o_pre.astype(jnp.float32)).reshape(B, S, M_HEADS, M_DH)
    y = head_norm(h, norm_g).reshape(B, S, M_INNER) + skip * x_c.astype(jnp.float32)
    return y.astype(x.dtype) @ w_out

def sqrelu_mlp(x, w1, w2):
    h = jax.nn.relu(x @ w1)
    return (h * h) @ w2

def setup_inputs(seed: int = 0) -> dict:
    key = jax.random.key(seed)
    ks = iter(jax.random.split(key, 32))

    def nrm(shape, scale):
        return jax.random.normal(next(ks), shape, jnp.float32) * scale

    NE = (DEPTH + 1) // 2
    NO = DEPTH // 2
    nblk = M_INNER // M_QKV_BLOCK
    f_bias = jnp.linspace(3.0, 6.0, M_HEADS, dtype=jnp.float32)[None, :] + nrm((NO, M_HEADS), 0.01)
    i_bias = nrm((NO, M_HEADS), 0.1)
    return {
        "x": nrm((BATCH, SEQ, D_MODEL), 1.0),
        "ev_w_in": nrm((NE, D_MODEL, EVEN_COLS), D_MODEL ** -0.5),
        "ev_g_w2": nrm((NE, G_RANK, G_HEADS * G_DK), G_RANK ** -0.5),
        "ev_g_b2": nrm((NE, G_HEADS * G_DK), 0.1),
        "ev_g_norm": 1.0 + nrm((NE, G_HEADS, G_DV), 0.02),
        "ev_w_out": nrm((NE, A_WIDTH + G_WIDTH, D_MODEL), (A_WIDTH + G_WIDTH) ** -0.5 * BETA),
        "od_w_in": nrm((NO, D_MODEL, 2 * M_INNER), D_MODEL ** -0.5),
        "od_conv_w": nrm((NO, M_CONV, M_INNER), M_CONV ** -0.5),
        "od_conv_b": nrm((NO, M_INNER), 0.02),
        "od_w_q": nrm((NO, nblk, M_QKV_BLOCK, M_QKV_BLOCK), M_QKV_BLOCK ** -0.5),
        "od_w_k": nrm((NO, nblk, M_QKV_BLOCK, M_QKV_BLOCK), M_QKV_BLOCK ** -0.5),
        "od_w_v": nrm((NO, nblk, M_QKV_BLOCK, M_QKV_BLOCK), M_QKV_BLOCK ** -0.5),
        "od_w_gate": nrm((NO, 3 * M_INNER, 2 * M_HEADS), (3 * M_INNER) ** -0.5),
        "od_b_gate": jnp.concatenate([i_bias, f_bias], axis=-1),
        "od_skip": 1.0 + nrm((NO, M_INNER), 0.02),
        "od_norm": 1.0 + nrm((NO, M_HEADS, M_DH), 0.02),
        "od_w_out": nrm((NO, M_INNER, D_MODEL), M_INNER ** -0.5 * BETA),
        "ln1_g": 1.0 + nrm((DEPTH, D_MODEL), 0.02),
        "ln1_b": nrm((DEPTH, D_MODEL), 0.02),
        "ln2_g": 1.0 + nrm((DEPTH, D_MODEL), 0.02),
        "ln2_b": nrm((DEPTH, D_MODEL), 0.02),
        "mlp_w1": nrm((DEPTH, D_MODEL, D_FF), D_MODEL ** -0.5),
        "mlp_w2": nrm((DEPTH, D_FF, D_MODEL), D_FF ** -0.5 * BETA),
    }

def reference(x, ev_w_in, ev_g_w2, ev_g_b2, ev_g_norm, ev_w_out,
              od_w_in, od_conv_w, od_conv_b, od_w_q, od_w_k, od_w_v, od_w_gate, od_b_gate,
              od_skip, od_norm, od_w_out,
              ln1_g, ln1_b, ln2_g, ln2_b, mlp_w1, mlp_w2):
    for l in range(DEPTH):
        j = l // 2
        if l % 2 == 0:
            h = even_mixer(x, ev_w_in[j], ev_g_w2[j], ev_g_b2[j], ev_g_norm[j], ev_w_out[j])
        else:
            h = odd_mixer(x, od_w_in[j], od_conv_w[j], od_conv_b[j], od_w_q[j], od_w_k[j], od_w_v[j],
                          od_w_gate[j], od_b_gate[j], od_skip[j], od_norm[j], od_w_out[j])
        x = layer_norm(ALPHA * x + h, ln1_g[l], ln1_b[l])
        x = layer_norm(ALPHA * x + sqrelu_mlp(x, mlp_w1[l], mlp_w2[l]), ln2_g[l], ln2_b[l])
    return x


_drawn_inputs = setup_inputs


def setup_inputs(seed=0):
    import zlib

    import numpy as np

    out = dict(_drawn_inputs(seed))
    spreads = {}
    factors = {'ev_g_w2': 3.042,
     'ev_g_b2': 7.019,
     'ev_g_norm': 8.0,
     'od_conv_b': 4.598,
     'od_skip': 8.0,
     'od_norm': 8.0}
    for name, (base, spread) in spreads.items():
        noise = np.random.default_rng([zlib.crc32(name.encode()), seed]).standard_normal(out[name].shape)
        drawn = base * np.exp(spread * noise) if base else spread * noise
        out[name] = __import__('jax').numpy.asarray(drawn.astype(out[name].dtype))
    for name, factor in factors.items():
        out[name] = (out[name] * factor).astype(out[name].dtype)
    return out
```

```python
from contextlib import ExitStack

import concourse.bass as bass
from concourse import mybir

F32 = mybir.dt.float32
F32R = mybir.dt.float32r
U32 = mybir.dt.uint32
ALU = mybir.AluOpType
ACT = mybir.ActivationFunctionType
AX = mybir.AxisListType

P = 128
SLOTS = 8
WIDE = 512
NEG = -3.0e38
MASKED = -1.0e30
LN_EPS = 1e-5

A_HEADS, A_DIM, TOPK = 8, 64, 128
G_HEADS, G_DIM, G_RANK, G_TAU = 4, 128, 16, 16.0
M_HEADS, M_CONV, M_BLK = 4, 4, 4


def hybrid_trunk(nc, x, ev_w_in, ev_g_w2, ev_g_b2, ev_g_norm, ev_w_out, od_w_in, od_conv_w, od_conv_b,
                 od_w_q, od_w_k, od_w_v, od_w_gate, od_b_gate, od_skip, od_norm, od_w_out,
                 ln1_g, ln1_b, ln2_g, ln2_b, mlp_w1, mlp_w2, out):
    _, S, D = x.shape
    T = S // P
    KD = D // P
    DEPTH = ln1_g.shape[0]
    ALPHA = (2 * DEPTH) ** 0.25
    FF = mlp_w1.shape[2]
    CH = FF // WIDE
    INNER = od_w_out.shape[1]
    DH = INNER // M_HEADS
    CT = DH // P
    assert (S, D, KD, T, DH) == (512, 1024, SLOTS, 4, WIDE)

    AQ, AK, AV = 0, 512, 576
    IQ, IK, IW = 640, 1152, 1216
    GQ, GK, GV, GR, GLR = 1224, 1736, 2248, 2760, 3272
    w_in = ev_w_in[0]

    def column_lap(w, c0, width, row0=0):
        return lambda k: [(0, w[row0 + k * P:row0 + (k + 1) * P, c0:c0 + width])]

    def doubled_lap(c0, width):
        return lambda k: [(0, w_in[k * P:(k + 1) * P, c0:c0 + 64]), (64, w_in[k * P:(k + 1) * P, c0:c0 + width])]

    def row_lap(w, r0):
        return lambda k: [(0, w[bass.ds(r0 + (k % 4) * P, P), (k // 4) * WIDE:(k // 4 + 1) * WIDE])]

    def up_lap(layer, c):
        return lambda k: [(0, mlp_w1[layer, k * P:(k + 1) * P, bass.ds(c * WIDE, WIDE)])]

    LAPS = [column_lap(w_in, IQ, 512), doubled_lap(IK, 72), column_lap(w_in, AQ, 512), doubled_lap(AK, 128),
            column_lap(w_in, GLR, 16), column_lap(w_in, GQ, 512), column_lap(w_in, GK, 512),
            column_lap(w_in, GV, 512), column_lap(w_in, GR, 512),
            column_lap(ev_w_out[0], 0, WIDE), column_lap(ev_w_out[0], WIDE, WIDE)]
    L_IQ, L_IK, L_AQ, L_AK, L_LR, L_GQ, L_GK, L_GV, L_GR, L_WO = range(10)
    WIDTHS = {L_IK: 136, L_AK: 192, L_LR: 16}
    DOUBLED = (L_IK, L_AK)

    def add_mlp(layer):
        base = len(LAPS)
        LAPS.append(up_lap(layer, 0))
        for c in range(CH):
            if c + 1 < CH:
                LAPS.append(up_lap(layer, c + 1))
            LAPS.append(row_lap(mlp_w2[layer], c * WIDE))
        return base

    L_MLP0 = add_mlp(0)
    L_XM = len(LAPS)
    for h in range(M_HEADS):
        LAPS.append(column_lap(od_w_in[0], h * WIDE, WIDE))
    L_HEAD = len(LAPS)
    for h in range(M_HEADS):
        LAPS.append(column_lap(od_w_in[0], INNER + h * WIDE, WIDE))
        LAPS.append(row_lap(od_w_out[0], h * WIDE))
    L_MLP1 = add_mlp(1)
    N_LAPS = len(LAPS)

    top = ExitStack()

    def sem(name):
        return top.enter_context(nc.semaphore(name))

    def sbuf(scope, name, shape, dt=F32):
        return scope.enter_context(nc.sbuf_tensor(name, shape, dt))

    with top:
        resid = sbuf(top, "resid", [P, T, D])
        xT_hi = sbuf(top, "xT_hi", [P, KD, S], F32R)
        xT_lo = sbuf(top, "xT_lo", [P, KD, S], F32R)
        w_raw = sbuf(top, "w_raw", [P, SLOTS, WIDE])
        w_hi = sbuf(top, "w_hi", [P, SLOTS, WIDE], F32R)
        w_lo = sbuf(top, "w_lo", [P, SLOTS, WIDE], F32R)
        ident = sbuf(top, "ident", [P, P])
        eps = sbuf(top, "eps", [P, 1])
        ones = sbuf(top, "ones", [P, P])
        ps = top.enter_context(nc.psum_tensor("ps", [P, 8, WIDE], F32))

        w_landed = [sem(f"w_landed{k}") for k in range(SLOTS)]
        w_rounded = sem("w_rounded")
        w_split = sem("w_split")
        w_used = sem("w_used")
        xp_done = sem("xp_done")
        xp_hi = sem("xp_hi")
        xp_lo = sem("xp_lo")
        added = sem("added")
        consts = sem("consts")
        dve_step = sem("dve_step")
        act_step = sem("act_step")
        pool_step = sem("pool_step")
        n_step = {"dve": 0, "act": 0, "pool": 0}
        n_added = [0]
        n_xp = [0]

        def stepper(eng, name, semaphore):
            def step(ins):
                n_step[name] += 1
                ins.then_inc(semaphore, 1)
                eng.wait_ge(semaphore, n_step[name])
            return step

        def load_tile(sp, lap, k, parts):
            if not (isinstance(lap, int) and lap == 0):
                sp.wait_ge(w_split, lap * SLOTS + k - SLOTS + 1)
            for col, src in parts:
                sp.dma_start(w_raw[:, k, col:col + src.shape[1]], src).then_inc(w_landed[k], 16)

        def load_lap(sp, lap):
            if lap < N_LAPS:
                for k in range(SLOTS):
                    load_tile(sp, lap, k, LAPS[lap](k))

        def landed(lap):
            extra = sum(1 for d in DOUBLED if d <= lap) if isinstance(lap, int) else len(DOUBLED)
            return (lap + 1 + extra) * 16

        def round_tile(act, lap, k, width=WIDE):
            act.wait_ge(w_landed[k], landed(lap))
            if not (isinstance(lap, int) and lap == 0):
                act.wait_ge(w_used, lap * SLOTS + k - SLOTS + 1)
            act.activation(w_hi[:, k, 0:width], w_raw[:, k, 0:width], ACT.Copy).then_inc(w_rounded, 1)

        def split_tile(dve, lap, k, width=WIDE):
            dve.wait_ge(w_rounded, lap * SLOTS + k + 1)
            dve.tensor_tensor(w_lo[:, k, 0:width], w_raw[:, k, 0:width], w_hi[:, k, 0:width].bitcast(F32),
                              ALU.subtract).then_inc(w_split, 1)

        def round_lap(act, lap):
            if not isinstance(lap, int) or lap < N_LAPS:
                for k in range(SLOTS):
                    round_tile(act, lap, k, WIDTHS.get(lap, WIDE) if isinstance(lap, int) else WIDE)

        def split_lap(dve, lap, ks=range(SLOTS)):
            if not isinstance(lap, int) or lap < N_LAPS:
                for k in ks:
                    split_tile(dve, lap, k, WIDTHS.get(lap, WIDE) if isinstance(lap, int) else WIDE)

        def tile_T(pe, k, a_hi, a_lo, outs, first, last):
            for dst, c0, cn in outs:
                pe.matmul(dst, w_hi[:, k, c0:c0 + cn], a_hi, start=first, stop=False)
                pe.matmul(dst, w_hi[:, k, c0:c0 + cn], a_lo, start=False, stop=False)
                mm = pe.matmul(dst, w_lo[:, k, c0:c0 + cn], a_hi, start=False, stop=last)
            mm.then_inc(w_used, 1)

        def tile_N(pe, k, a_hi, a_lo, bank0, first, last):
            for t in range(T):
                ts = slice(t * P, (t + 1) * P)
                pe.matmul(ps[:, bank0 + t, :], a_hi[:, ts], w_hi[:, k, :], start=first, stop=False)
                pe.matmul(ps[:, bank0 + t, :], a_hi[:, ts], w_lo[:, k, :], start=False, stop=False)
                mm = pe.matmul(ps[:, bank0 + t, :], a_lo[:, ts], w_hi[:, k, :], start=False, stop=last)
            mm.then_inc(w_used, 1)

        def lap_T(pe, lap, outs):
            for k in range(SLOTS):
                pe.wait_ge(w_split, lap * SLOTS + k + 1)
                tile_T(pe, k, xT_hi[:, k, :], xT_lo[:, k, :], outs, k == 0, k == SLOTS - 1)

        def lap_N(pe, lap, bank0):
            for k in range(SLOTS):
                pe.wait_ge(w_split, lap * SLOTS + k + 1)
                tile_N(pe, k, xT_hi[:, k, :], xT_lo[:, k, :], bank0, k == 0, k == SLOTS - 1)

        def lap_rows(pe, lap, a_hi, a_lo, bank_left, bank_right, before_left, before_right):
            for half, bank0, before in ((0, bank_left, before_left), (1, bank_right, before_right)):
                before()
                for kk in range(4):
                    pe.wait_ge(w_split, lap * SLOTS + half * 4 + kk + 1)
                    tile_N(pe, half * 4 + kk, a_hi(kk), a_lo(kk), bank0, kk == 0, kk == 3)

        def full_banks(bank0):
            return [(ps[:, bank0 + j, :], j * P, P) for j in range(4)]

        def lap_done(lap):
            return (lap + 1) * SLOTS

        def add_half(dve, half, bank0):
            for t in range(T):
                r = resid[:, t, half * WIDE:(half + 1) * WIDE]
                dve.tensor_tensor(r, ps[:, bank0 + t, :], r, ALU.add).then_inc(added, 1)

        def transpose_pe(pe, src, t):
            for half in range(2):
                for j in range(4):
                    c = (4 * half + j) * P
                    mm = pe.transpose(ps[:, 2 * t + half, j * P:(j + 1) * P], src[:, t, c:c + P], ident[:])
                mm.then_inc(xp_done, 1)

        def bank_as_tiles(b):
            return ps[:, b, :].rearrange("p (k q) -> p k q", k=4)

        def transpose_act(act, base, t):
            for half in range(2):
                act.wait_ge(xp_done, base + 2 * t + half + 1)
                act.activation(xT_hi[:, 4 * half:4 * half + 4, t * P:(t + 1) * P], bank_as_tiles(2 * t + half),
                               ACT.Copy).then_inc(xp_hi, 1)

        def transpose_dve(dve, base, t):
            for half in range(2):
                ap = (slice(None), slice(4 * half, 4 * half + 4), slice(t * P, (t + 1) * P))
                dve.wait_ge(xp_hi, base + 2 * t + half + 1)
                dve.tensor_tensor(xT_lo[ap], bank_as_tiles(2 * t + half), xT_hi[ap].bitcast(F32),
                                  ALU.subtract).then_inc(xp_lo, 1)

        even = ExitStack()
        level_mask = sbuf(even, "level_mask", [P, 8, P])
        tri_tau = sbuf(even, "tri_tau", [P, P])
        g_w2 = sbuf(even, "g_w2", [G_RANK, WIDE])
        g_b2 = sbuf(even, "g_b2", [1, WIDE])
        x_landed, params = sem("x_landed"), sem("params")
        with nc.Block() as block:
            @block.sync
            def _(sp):
                for t in range(T):
                    sp.dma_start(resid[:, t, :], x[0, t * P:(t + 1) * P, :]).then_inc(x_landed, 16)
                load_lap(sp, 0)
                load_lap(sp, 1)

            @block.gpsimd
            def _(pool):
                step = stepper(pool, "pool", pool_step)
                step(pool.memset(ident[:], 0.0))
                pool.affine_select(out=ident[:], in_=ident[:], compare_op=ALU.not_equal, fill=1.0, base=0,
                                   pattern=[[-1, P]], channel_multiplier=1).then_inc(consts, 1)
                pool.memset(eps[:], LN_EPS)
                pool.memset(ones[:], 1.0)
                step(pool.memset(tri_tau[:], 1.0 / G_TAU))
                step(pool.affine_select(out=tri_tau[:], in_=tri_tau[:], compare_op=ALU.is_ge, fill=0.0, base=0,
                                        pattern=[[1, P]], channel_multiplier=-1))
                step(pool.memset(level_mask[:], 0.0))
                for lev in range(7):
                    half = 64 >> lev
                    nb = P // (2 * half)
                    v = level_mask[:, lev, :].rearrange("p (b j) -> p b j", b=nb)[:, :, half:2 * half]
                    step(pool.memset(v, 1.0))
                    step(pool.affine_select(out=v, in_=v, compare_op=ALU.is_ge, fill=0.0, base=0,
                                            pattern=[[-2 * half, nb], [0, half]], channel_multiplier=1))
                    step(pool.affine_select(out=v, in_=v, compare_op=ALU.is_ge, fill=0.0, base=half - 1,
                                            pattern=[[2 * half, nb], [0, half]], channel_multiplier=-1))
                step(pool.affine_select(out=level_mask[:, 7, :], in_=level_mask[:, 7, :], compare_op=ALU.not_equal,
                                        fill=1.0, base=0, pattern=[[-1, P]], channel_multiplier=1))

            @block.tensor
            def _(pe):
                pe.wait_ge(consts, 1)
                pe.wait_ge(x_landed, 16 * T)
                for t in range(T):
                    transpose_pe(pe, resid, t)

            @block.scalar
            def _(act):
                act.dma_start(g_w2[:], ev_g_w2[0]).then_inc(params, 16)
                act.dma_start(g_b2[:], ev_g_b2[0:1, :]).then_inc(params, 16)
                for t in range(T):
                    transpose_act(act, 0, t)
                    act.mul(resid[:, t, :], resid[:, t, :], ALPHA)
                round_lap(act, 0)

            @block.vector
            def _(dve):
                for t in range(T):
                    transpose_dve(dve, 0, t)
                split_lap(dve, 0)
        n_xp[0] = 8

        gla_in = ExitStack()
        gqT = sbuf(gla_in, "gqT", [P, G_HEADS, S])
        gkT = sbuf(gla_in, "gkT", [P, G_HEADS, S])
        gv = sbuf(gla_in, "gv", [P, T, WIDE])
        gr = sbuf(gla_in, "gr", [P, T, WIDE])
        lrT = sbuf(gla_in, "lrT", [G_RANK, S])
        cat = sbuf(gla_in, "cat", [P, T, D])
        dsa_in = ExitStack()
        aqT = sbuf(dsa_in, "aqT", [P, 4, S])
        akT = sbuf(dsa_in, "akT", [P, S])
        av = sbuf(dsa_in, "av", [P, T, A_DIM])
        key_mask = sbuf(dsa_in, "key_mask", [P, T, S])
        idx = ExitStack()
        iqT = sbuf(idx, "iqT", [P, 4, S])
        ikT = sbuf(idx, "ikT", [P, S])
        iwT = sbuf(idx, "iwT", [8, S])
        iw = sbuf(idx, "iw", [P, T, 8])
        avT = sbuf(idx, "avT", [A_DIM, S])
        relu_buf = sbuf(idx, "relu_buf", [P, 4, S])
        score = sbuf(idx, "score", [P, 3, S])
        left = sbuf(idx, "left", [P, S])
        best8 = sbuf(idx, "best8", [P, 8])

        proj_out = sem("proj_out")
        iw_turned = sem("iw_turned")
        av_turned = sem("av_turned")
        logits_done, relu_done, score_added = sem("logits_done"), sem("relu_done"), sem("score_added")
        causal_done, chosen, mask_ready = sem("causal_done"), sem("chosen"), sem("mask_ready")
        ITEMS = [(b, h) for b in range(1, T) for h in range(A_HEADS)]
        O_IQ, O_IK, O_IW, O_AQ, O_AK, O_AV, O_LR, O_GQ, O_GK, O_GV, O_GR = 4, 6, 7, 11, 13, 14, 15, 19, 23, 27, 31

        with nc.Block() as block:
            @block.sync
            def _(sp):
                for lap in range(L_IQ + 2, L_GR + 3):
                    load_lap(sp, lap)

            @block.tensor
            def _(pe):
                pe.wait_ge(xp_lo, n_xp[0])
                lap_T(pe, L_IQ, full_banks(0))
                lap_T(pe, L_IK, [(ps[:, 4, :], 0, P), (ps[0:8, 5, :], P, 8)])
                pe.wait_ge(proj_out, O_IK)
                for t in range(T):
                    mm = pe.transpose(ps[:, 6, 8 * t:8 * t + 8], iwT[:, t * P:(t + 1) * P], ident[0:8, 0:8])
                mm.then_inc(iw_turned, 1)
                for u, (b, h) in enumerate(ITEMS):
                    if u >= 4:
                        pe.wait_ge(relu_done, u - 3)
                    r = slice(64 * (h % 2), 64 * (h % 2) + 64)
                    pe.matmul(ps[:, u % 4, 0:(b + 1) * P], iqT[r, h // 2, b * P:(b + 1) * P],
                              ikT[r, 0:(b + 1) * P], start=True, stop=True).then_inc(logits_done, 1)
                pe.wait_ge(proj_out, O_IW)
                lap_T(pe, L_AQ, full_banks(4))
                pe.wait_ge(relu_done, len(ITEMS))
                lap_T(pe, L_AK, [(ps[:, 0, :], 0, P), (ps[0:64, 1, :], P, 64)])
                lap_T(pe, L_LR, [(ps[0:G_RANK, 3, :], 0, G_RANK)])
                pe.wait_ge(proj_out, O_AK)
                for t in range(T):
                    mm = pe.transpose(ps[:, 2, 64 * t:64 * t + 64], avT[:, t * P:(t + 1) * P], ident[0:64, 0:64])
                mm.then_inc(av_turned, 1)
                pe.wait_ge(proj_out, O_AQ)
                lap_T(pe, L_GQ, full_banks(4))
                pe.wait_ge(proj_out, O_LR)
                lap_T(pe, L_GK, full_banks(0))
                pe.wait_ge(proj_out, O_GQ)
                lap_N(pe, L_GV, 4)
                pe.wait_ge(proj_out, O_GK)
                lap_N(pe, L_GR, 0)

            @block.scalar
            def _(act):
                def copy_out(dst, src, scale=1.0):
                    act.activation(dst, src, ACT.Copy, scale=scale).then_inc(proj_out, 1)

                def copy_banks(dst, bank0, scale=1.0):
                    for j in range(4):
                        copy_out(dst[:, j, :], ps[:, bank0 + j, :], scale)

                round_lap(act, L_IK)
                act.wait_ge(w_used, lap_done(L_IQ))
                copy_banks(iqT, 0)
                round_lap(act, L_AQ)
                act.wait_ge(w_used, lap_done(L_IK))
                copy_out(ikT[:], ps[:, 4, :])
                copy_out(iwT[:], ps[0:8, 5, :])
                act.wait_ge(iw_turned, 1)
                copy_out(iw[:].rearrange("p t h -> p (t h)"), ps[:, 6, 0:8 * T], A_HEADS ** -0.5)
                for u, (b, h) in enumerate(ITEMS):
                    act.wait_ge(logits_done, u + 1)
                    if u >= 4:
                        act.wait_ge(score_added, u - 3)
                    act.activation(relu_buf[:, u % 4, 0:(b + 1) * P], ps[:, u % 4, 0:(b + 1) * P], ACT.Relu,
                                   scale=A_DIM ** -0.5).then_inc(relu_done, 1)
                round_lap(act, L_AK)
                act.wait_ge(w_used, lap_done(L_AQ))
                copy_banks(aqT, 4)
                round_lap(act, L_LR)
                act.wait_ge(w_used, lap_done(L_AK))
                copy_out(akT[:], ps[:, 0, :])
                copy_out(avT[:], ps[0:64, 1, :])
                round_lap(act, L_GQ)
                act.wait_ge(av_turned, 1)
                copy_out(av[:].rearrange("p t d -> p (t d)"), ps[:, 2, 0:64 * T])
                act.wait_ge(w_used, lap_done(L_LR))
                copy_out(lrT[:], ps[0:G_RANK, 3, :])
                round_lap(act, L_GK)
                act.wait_ge(w_used, lap_done(L_GQ))
                copy_banks(gqT, 4, G_DIM ** -0.5)
                round_lap(act, L_GV)
                act.wait_ge(w_used, lap_done(L_GK))
                copy_banks(gkT, 0)
                round_lap(act, L_GR)
                act.wait_ge(w_used, lap_done(L_GV))
                copy_banks(gv, 4)
                round_lap(act, L_WO)
                act.wait_ge(w_used, lap_done(L_GR))
                copy_banks(gr, 0)

            @block.vector
            def _(dve):
                step = stepper(dve, "dve", dve_step)
                split_lap(dve, L_IK)
                split_lap(dve, L_AQ)
                dve.wait_ge(proj_out, O_IW)
                for u, (b, h) in enumerate(ITEMS):
                    n = (b + 1) * P
                    dve.wait_ge(relu_done, u + 1)
                    if h == 0:
                        ins = dve.tensor_scalar(score[:, b - 1, 0:n], relu_buf[:, u % 4, 0:n], iw[:, b, 0:1], None,
                                                ALU.mult)
                    else:
                        dve.wait_ge(score_added, u)
                        ins = dve.scalar_tensor_tensor(out=score[:, b - 1, 0:n], in0=relu_buf[:, u % 4, 0:n],
                                                       scalar=iw[:, b, h:h + 1], in1=score[:, b - 1, 0:n],
                                                       op0=ALU.mult, op1=ALU.add)
                    ins.then_inc(score_added, 1)
                tiles = [(lap, k) for lap in range(L_AK, L_WO + 1) for k in range(SLOTS)]
                for b in range(1, T):
                    n = (b + 1) * P
                    dve.wait_ge(causal_done, b)
                    for r in range(TOPK // 8):
                        src = score[:, b - 1, 0:n] if r == 0 else left[:, 0:n]
                        step(dve.max(best8[:], src))
                        step(dve.match_replace(out=left[:, 0:n], in_to_replace=best8[:], in_values=src, imm_value=NEG))
                        lap, k = tiles.pop(0)
                        split_tile(dve, lap, k, WIDTHS.get(lap, WIDE))
                    dve.tensor_scalar(key_mask[:, b, 0:n], left[:, 0:n], NEG / 3, MASKED, ALU.is_gt,
                                      ALU.mult).then_inc(chosen, 1)
                for lap, k in tiles:
                    split_tile(dve, lap, k, WIDTHS.get(lap, WIDE))

            @block.gpsimd
            def _(pool):
                step = stepper(pool, "pool", pool_step)

                def causal(ap, fill):
                    return pool.affine_select(out=ap, in_=ap, compare_op=ALU.is_ge, fill=fill, base=0,
                                              pattern=[[-1, P]], channel_multiplier=1)

                step(pool.memset(key_mask[:, 0, 0:P], 0.0))
                causal(key_mask[:, 0, 0:P], MASKED).then_inc(mask_ready, 1)
                for b in range(1, T):
                    pool.wait_ge(score_added, b * A_HEADS)
                    causal(score[:, b - 1, b * P:(b + 1) * P], NEG).then_inc(causal_done, 1)
                for b in range(1, T):
                    pool.wait_ge(chosen, b)
                    causal(key_mask[:, b, b * P:(b + 1) * P], MASKED).then_inc(mask_ready, 1)
        idx.close()

        att = ExitStack()
        s_neg = sbuf(att, "s_neg", [P, 2, S])
        prob = sbuf(att, "prob", [P, 2, S])
        probT = sbuf(att, "probT", [P, 2, S])
        min_neg = sbuf(att, "min_neg", [P, T * A_HEADS])
        row_sum = sbuf(att, "row_sum", [P, T * A_HEADS])
        row_inv = sbuf(att, "row_inv", [P, T * A_HEADS])
        s_done, s_masked, exp_done = sem("s_done"), sem("s_masked"), sem("exp_done")
        pt_done, pt_out, pv_done, o_out = sem("pt_done"), sem("pt_out"), sem("pv_done"), sem("o_out")
        QH = [(b, h) for b in range(T) for h in range(A_HEADS)]
        with nc.Block() as block:
            @block.tensor
            def _(pe):
                def scores(i):
                    b, h = QH[i]
                    r = slice(64 * (h % 2), 64 * (h % 2) + 64)
                    if i >= 2:
                        pe.wait_ge(s_masked, i - 1)
                    pe.matmul(ps[:, i % 2, 0:(b + 1) * P], aqT[r, h // 2, b * P:(b + 1) * P], akT[r, 0:(b + 1) * P],
                              start=True, stop=True).then_inc(s_done, 1)

                def turn(i):
                    b, h = QH[i]
                    pe.wait_ge(exp_done, i + 1)
                    if i >= 2:
                        pe.wait_ge(pt_out, i - 1)
                    for kt in range(b + 1):
                        mm = pe.transpose(ps[:, 2 + i % 2, kt * P:(kt + 1) * P], prob[:, i % 2, kt * P:(kt + 1) * P],
                                          ident[:])
                    mm.then_inc(pt_done, 1)

                def values(i):
                    b, h = QH[i]
                    pe.wait_ge(pt_out, i + 1)
                    if b >= 2 and h == 0:
                        pe.wait_ge(o_out, b - 1)
                    for kt in range(b + 1):
                        mm = pe.matmul(ps[:, 4 + b % 2, h * A_DIM:(h + 1) * A_DIM],
                                       probT[:, i % 2, kt * P:(kt + 1) * P], av[:, kt, :],
                                       start=(kt == 0), stop=(kt == b))
                    mm.then_inc(pv_done, 1)

                for i in range(len(QH) + 2):
                    if i < len(QH):
                        scores(i)
                    if 1 <= i <= len(QH):
                        turn(i - 1)
                    if i >= 2:
                        values(i - 2)

            @block.vector
            def _(dve):
                step = stepper(dve, "dve", dve_step)

                def normalise(b):
                    dve.wait_ge(pv_done, (b + 1) * A_HEADS)
                    hs = slice(b * A_HEADS, (b + 1) * A_HEADS)
                    step(dve.reciprocal(row_inv[:, hs], row_sum[:, hs]))
                    dve.tensor_tensor(cat[:, b, 0:A_HEADS * A_DIM].rearrange("p (h d) -> p h d", h=A_HEADS),
                                      ps[:, 4 + b % 2, :].rearrange("p (h d) -> p h d", h=A_HEADS),
                                      row_inv[:, hs].unsqueeze(2).broadcast_to([P, A_HEADS, A_DIM]),
                                      ALU.mult).then_inc(o_out, 1)

                for i, (b, h) in enumerate(QH):
                    n = (b + 1) * P
                    dve.wait_ge(s_done, i + 1)
                    if i >= 2:
                        dve.wait_ge(exp_done, i - 1)
                    dve.tensor_tensor_reduce(out=s_neg[:, i % 2, 0:n], in0=ps[:, i % 2, 0:n], in1=key_mask[:, b, 0:n],
                                             scale=-A_DIM ** -0.5, scalar=3.0e38, op0=ALU.add, op1=ALU.min,
                                             accum_out=min_neg[:, i:i + 1]).then_inc(s_masked, 1)
                    if b >= 1 and h == 3:
                        normalise(b - 1)
                normalise(T - 1)

            @block.scalar
            def _(act):
                def copy_pt(i):
                    n = (QH[i][0] + 1) * P
                    act.wait_ge(pt_done, i + 1)
                    if i >= 2:
                        act.wait_ge(pv_done, i - 1)
                    act.activation(probT[:, i % 2, 0:n], ps[:, 2 + i % 2, 0:n], ACT.Copy).then_inc(pt_out, 1)

                for i, (b, h) in enumerate(QH):
                    n = (b + 1) * P
                    act.wait_ge(s_masked, i + 1)
                    if i >= 2:
                        act.wait_ge(pt_done, i - 1)
                    act.activation(prob[:, i % 2, 0:n], s_neg[:, i % 2, 0:n], ACT.Exp, scale=-1.0,
                                   bias=min_neg[:, i:i + 1], accum_out=row_sum[:, i:i + 1]).then_inc(exp_done, 1)
                    if i >= 1:
                        copy_pt(i - 1)
                copy_pt(len(QH) - 1)
        att.close()
        dsa_in.close()

        gla = ExitStack()
        loga = sbuf(gla, "loga", [P, T, WIDE])
        bcum = sbuf(gla, "bcum", [P, G_HEADS, S])
        ebcum = sbuf(gla, "ebcum", [P, G_HEADS, S])
        diff = sbuf(gla, "diff", [P, 2, S])
        expd = diff
        q_lev = sbuf(gla, "q_lev", [P, 2, S])
        k_lev = sbuf(gla, "k_lev", [P, 2, S])
        k_end = k_lev[:, (8 - 1) % 2, :]
        k_endT = sbuf(gla, "k_endT", [P, 3 * P])
        attT = sbuf(gla, "attT", [P, 2, S])
        state = sbuf(gla, "state", [P, G_HEADS, 3, G_DIM])
        g_norm = sbuf(gla, "g_norm", [P, WIDE])
        o_norm = diff[:, 0, :]
        g_stat = sbuf(gla, "g_stat", [P, G_HEADS, 6])
        g_mv = sbuf(gla, "g_mv", [P, G_HEADS, 2])
        g_std = sbuf(gla, "g_std", [P, 2, G_HEADS])
        gate_mm, ln_done, loga_done = sem("gate_mm"), sem("ln_done"), sem("loga_done")
        cum_done, b_ready, eb_ready, qe_ready = sem("cum_done"), sem("b_ready"), sem("eb_ready"), sem("qe_ready")
        diff_ready, expd_ready, lev_ready = sem("diff_ready"), sem("expd_ready"), sem("lev_ready")
        lev_mm, lev_kept = sem("lev_mm"), sem("lev_kept")
        kend_turned, kend_out = sem("kend_turned"), sem("kend_out")
        su_mm, s_ready, o_mm = sem("su_mm"), sem("s_ready"), sem("o_mm")
        zeroed, gr_ready, sg_ready, var_ready, std_ready = (sem("zeroed"), sem("gr_ready"), sem("sg_ready"),
                                                            sem("var_ready"), sem("std_ready"))
        g_norm_landed = sem("g_norm_landed")
        LEV = 8
        def blocks_of(ap, half):
            return ap.rearrange("p (b j) -> p b j", j=2 * half)

        with nc.Block() as block:
            @block.sync
            def _(sp):
                sp.dma_start(g_norm[:], ev_g_norm[0:1].rearrange("o h d -> o (h d)").broadcast_to([P, WIDE])
                             ).then_inc(g_norm_landed, 16)

            @block.tensor
            def _(pe):
                pe.wait_ge(params, 32)
                for c in range(T):
                    pe.matmul(ps[:, c, :], lrT[:, c * P:(c + 1) * P], g_w2[:], start=True, stop=False)
                    pe.matmul(ps[:, c, :], ones[0:1, :], g_b2[:], start=False, stop=True).then_inc(gate_mm, 1)
                pe.wait_ge(loga_done, T)
                for h in range(G_HEADS):
                    for c in range(T):
                        mm = pe.matmul(ps[:, 4 + h, c * P:(c + 1) * P], loga[:, c, h * P:(h + 1) * P], tri_tau[:],
                                       start=True, stop=True)
                    mm.then_inc(cum_done, 1)
                for h in range(G_HEADS):
                    for lev in range(LEV):
                        n = h * LEV + lev
                        pe.wait_ge(lev_ready, n + 1)
                        if n >= 2:
                            pe.wait_ge(lev_kept, n - 1)
                        for c in range(T):
                            cs = slice(c * P, (c + 1) * P)
                            kk, qq = (k_lev[:, n % 2, cs], q_lev[:, n % 2, cs]) if lev < 7 else (gkT[:, h, cs], gqT[:, h, cs])
                            mm = pe.matmul(ps[:, n % 2, cs], kk, qq, start=True, stop=True)
                        mm.then_inc(lev_mm, 1)
                    if h >= 1:
                        pe.wait_ge(kend_out, h)
                    for c in range(T - 1):
                        mm = pe.transpose(ps[:, 2, c * P:(c + 1) * P], k_end[:, c * P:(c + 1) * P], ident[:])
                    mm.then_inc(kend_turned, 1)
                    if h == 0:
                        pe.wait_ge(b_ready, G_HEADS)
                        pe.wait_ge(qe_ready, G_HEADS)
                    pe.wait_ge(kend_out, h + 1)
                    pe.wait_ge(lev_kept, (h + 1) * LEV)
                    for c in range(T):
                        cs, hs = slice(c * P, (c + 1) * P), slice(h * P, (h + 1) * P)
                        if c >= 1:
                            pe.wait_ge(s_ready, h * 3 + c)
                        elif h >= 1:
                            pe.wait_ge(s_ready, h * 3)
                        if c < T - 1:
                            pe.matmul(ps[:, 3, cs], k_endT[:, cs], gv[:, c, hs], start=True,
                                      stop=True).then_inc(su_mm, 1)
                        mm = pe.matmul(ps[:, 4 + c, hs], attT[:, h % 2, cs], gv[:, c, hs], start=True, stop=(c == 0))
                        if c >= 1:
                            mm = pe.matmul(ps[:, 4 + c, hs], loga[:, h, cs], state[:, h, c - 1, :], start=False,
                                           stop=True)
                        mm.then_inc(o_mm, 1)

            @block.scalar
            def _(act):
                step = stepper(act, "act", act_step)

                def copy_kend(h):
                    act.wait_ge(kend_turned, h + 1)
                    if h >= 1:
                        act.wait_ge(su_mm, 3 * h)
                    act.activation(k_endT[:], ps[:, 2, 0:3 * P], ACT.Copy).then_inc(kend_out, 1)

                for c in range(T):
                    act.wait_ge(gate_mm, c + 1)
                    ins = act.activation(loga[:, c, :], ps[:, c, :], ACT.Abs)
                step(ins)
                step(act.activation(loga[:], loga[:], ACT.Exp, scale=-1.0))
                act.activation(loga[:], loga[:], ACT.Ln, bias=1.0).then_inc(ln_done, 1)
                for h in range(G_HEADS):
                    act.wait_ge(cum_done, h + 1)
                    act.activation(bcum[:, h, :], ps[:, 4 + h, :], ACT.Copy).then_inc(b_ready, 1)
                act.wait_ge(b_ready, G_HEADS)
                for h in range(G_HEADS):
                    act.activation(ebcum[:, h, :], bcum[:, h, :], ACT.Exp).then_inc(eb_ready, 1)
                for h in range(G_HEADS):
                    for lev in range(LEV):
                        n = h * LEV + lev
                        act.wait_ge(diff_ready, n + 1)
                        if lev < 7:
                            half = 64 >> lev
                            d, e = blocks_of(diff[:, n % 2, :], half), blocks_of(expd[:, n % 2, :], half)
                            act.activation(e[:, :, half:], d[:, :, half:], ACT.Exp)
                            act.activation(e[:, :, :half], d[:, :, :half], ACT.Exp, scale=-1.0).then_inc(expd_ready, 1)
                        else:
                            act.activation(expd[:, n % 2, :], diff[:, n % 2, :], ACT.Exp, scale=-1.0).then_inc(expd_ready, 1)
                        if lev == 1 and h >= 1:
                            copy_kend(h - 1)
                copy_kend(G_HEADS - 1)
                act.activation(gr[:], gr[:], ACT.Silu).then_inc(gr_ready, 1)
                for c in range(T):
                    act.wait_ge(var_ready, c + 1)
                    act.activation(g_std[:, c % 2, :], g_mv[:, :, 1], ACT.Sqrt, bias=eps[:, 0:1]).then_inc(std_ready, 1)

            @block.gpsimd
            def _(pool):
                pool.memset(q_lev[:], 0.0).then_inc(zeroed, 1)
                pool.memset(k_lev[:], 0.0).then_inc(zeroed, 1)
                pool.wait_ge(zeroed, 2)
                for h in range(G_HEADS):
                    for lev in range(LEV):
                        n = h * LEV + lev
                        pool.wait_ge(expd_ready, n + 1)
                        if n >= 2:
                            pool.wait_ge(lev_mm, n - 1)
                        if lev == 1 and h >= 1:
                            pool.wait_ge(kend_turned, h)
                        if lev < 7:
                            half = 64 >> lev
                            e = blocks_of(expd[:, n % 2, :], half)
                            pool.tensor_tensor(blocks_of(q_lev[:, n % 2, :], half)[:, :, half:],
                                               blocks_of(gqT[:, h, :], half)[:, :, half:], e[:, :, half:], ALU.mult)
                            pool.tensor_tensor(blocks_of(k_lev[:, n % 2, :], half)[:, :, :half],
                                               blocks_of(gkT[:, h, :], half)[:, :, :half], e[:, :, :half],
                                               ALU.mult).then_inc(lev_ready, 1)
                        else:
                            pool.tensor_tensor(k_end, gkT[:, h, :], expd[:, n % 2, :], ALU.mult).then_inc(lev_ready, 1)
                pool.wait_ge(gr_ready, 1)
                pool.wait_ge(g_norm_landed, 16)
                for c in range(T):
                    pool.tensor_tensor(gr[:, c, :], gr[:, c, :], g_norm[:], ALU.mult).then_inc(sg_ready, 1)

            @block.vector
            def _(dve):
                step = stepper(dve, "dve", dve_step)
                step(dve.memset(attT[:], 0.0))
                dve.wait_ge(ln_done, 1)
                for c in range(T):
                    dve.scalar_tensor_tensor(out=loga[:, c, :], in0=ps[:, c, :], scalar=0.0, in1=loga[:, c, :],
                                             op0=ALU.min, op1=ALU.subtract).then_inc(loga_done, 1)

                def make_diff(n):
                    h, lev = divmod(n, LEV)
                    dve.wait_ge(b_ready, h + 1)
                    if n >= 2:
                        dve.wait_ge(lev_ready, n - 1)
                    half, ref = (64 >> lev, (64 >> lev) - 1) if lev < 7 else (64, 127)
                    b = blocks_of(bcum[:, h, :], half)
                    dve.tensor_tensor(blocks_of(diff[:, n % 2, :], half), b,
                                      b[:, :, ref:ref + 1].broadcast_to([P, S // (2 * half), 2 * half]),
                                      ALU.subtract).then_inc(diff_ready, 1)

                def keep(n):
                    h, lev = divmod(n, LEV)
                    dve.wait_ge(lev_mm, n + 1)
                    if lev == 0 and h >= 2:
                        dve.wait_ge(o_mm, (h - 1) * T)
                    if n >= 1:
                        dve.wait_ge(lev_kept, n)
                    dve.copy_predicated(attT[:, h % 2, :].rearrange("p (c t) -> p c t", c=T),
                                        level_mask[:, lev, :].bitcast(U32).unsqueeze(1).broadcast_to([P, T, P]),
                                        ps[:, n % 2, :].rearrange("p (c t) -> p c t", c=T)).then_inc(lev_kept, 1)

                def states(h):
                    for c in range(T - 1):
                        dve.wait_ge(su_mm, h * 3 + c + 1)
                        if c == 0:
                            ins = dve.tensor_copy(state[:, h, 0, :], ps[:, 3, 0:P])
                        else:
                            dve.wait_ge(s_ready, h * 3 + c)
                            ins = dve.scalar_tensor_tensor(out=state[:, h, c, :], in0=state[:, h, c - 1, :],
                                                           scalar=ebcum[:, h, (c + 1) * P - 1:(c + 1) * P],
                                                           in1=ps[:, 3, c * P:(c + 1) * P], op0=ALU.mult, op1=ALU.add)
                        ins.then_inc(s_ready, 1)

                make_diff(0)
                make_diff(1)
                dve.wait_ge(cum_done, G_HEADS)
                for h in range(G_HEADS):
                    dve.wait_ge(eb_ready, h + 1)
                    dve.tensor_tensor(loga[:, h, :], gqT[:, h, :], ebcum[:, h, :], ALU.mult).then_inc(qe_ready, 1)
                for n in range(G_HEADS * LEV):
                    if n + 2 < G_HEADS * LEV:
                        make_diff(n + 2)
                    keep(n)
                    if n % LEV == LEV - 1:
                        states(n // LEV)
                dve.wait_ge(o_mm, G_HEADS * T)
                for c in range(T):
                    for h in range(G_HEADS):
                        ins = dve.bn_stats(g_stat[:, h, :], ps[:, 4 + c, h * P:(h + 1) * P])
                    step(ins)
                    if c >= 1:
                        dve.wait_ge(std_ready, c)
                    for h in range(G_HEADS):
                        ins = dve.bn_aggr(g_mv[:, h, :], g_stat[:, h, :])
                    ins.then_inc(var_ready, 1)
                    dve.wait_ge(std_ready, c + 1)
                    dve.wait_ge(var_ready, c + 1)
                    step(dve.reciprocal(g_std[:, c % 2, :], g_std[:, c % 2, :]))
                    for h in range(G_HEADS):
                        hs = slice(h * P, (h + 1) * P)
                        ins = dve.tensor_scalar(diff[:, 0, hs], ps[:, 4 + c, hs], g_mv[:, h, 0:1],
                                                g_std[:, c % 2, h:h + 1], ALU.subtract, ALU.mult)
                    step(ins)
                    dve.wait_ge(sg_ready, c + 1)
                    step(dve.tensor_tensor(cat[:, c, WIDE:], o_norm, gr[:, c, :], ALU.mult))
        gla.close()

        base = n_xp[0]
        with nc.Block() as block:
            @block.sync
            def _(sp):
                load_lap(sp, L_MLP0)
                load_lap(sp, L_MLP0 + 1)

            @block.tensor
            def _(pe):
                for t in range(T):
                    transpose_pe(pe, cat, t)
                pe.wait_ge(xp_lo, base + 8)
                lap_N(pe, L_WO, 0)
                lap_N(pe, L_WO + 1, 4)

            @block.scalar
            def _(act):
                for t in range(T):
                    transpose_act(act, base, t)
                round_lap(act, L_WO + 1)
                round_lap(act, L_MLP0)

            @block.vector
            def _(dve):
                for t in range(T):
                    transpose_dve(dve, base, t)
                split_lap(dve, L_WO + 1)
                dve.wait_ge(w_used, lap_done(L_WO))
                add_half(dve, 0, 0)
                split_lap(dve, L_MLP0)
                dve.wait_ge(w_used, lap_done(L_WO + 1))
                add_half(dve, 1, 4)
        n_xp[0] += 8
        n_added[0] += 8
        gla_in.close()
        even.close()

        gb_landed, norm_var, norm_std, norm_scaled, norm_y = (sem("gb_landed"), sem("norm_var"), sem("norm_std"),
                                                              sem("norm_scaled"), sem("norm_y"))
        out_stored = sem("out_stored")
        n_norm = [0]

        def norm_stage(g_row, b_row, last=False):
            own = ExitStack()
            i = n_norm[0]
            g_all = sbuf(own, f"ln_g{i}", [P, D])
            b_all = sbuf(own, f"ln_b{i}", [P, D])
            stat = sbuf(own, f"ln_stat{i}", [P, T, 2, 6])
            mv = sbuf(own, f"ln_mv{i}", [P, T, 2])
            rstd = sbuf(own, f"ln_rstd{i}", [P, T])
            base, done = n_xp[0], i * T
            with nc.Block() as block:
                @block.sync
                def _(sp):
                    sp.dma_start(g_all[:], g_row.broadcast_to([P, D])).then_inc(gb_landed, 16)
                    sp.dma_start(b_all[:], b_row.broadcast_to([P, D])).then_inc(gb_landed, 16)
                    if last:
                        for t in range(T):
                            sp.wait_ge(norm_y, done + t + 1)
                            sp.dma_start(out[0, t * P:(t + 1) * P, :], resid[:, t, :]).then_inc(out_stored, 16)
                        sp.wait_ge(out_stored, 16 * T)

                @block.vector
                def _(dve):
                    step = stepper(dve, "dve", dve_step)

                    def statistics(t):
                        dve.bn_stats(stat[:, t, 0, :], resid[:, t, 0:WIDE])
                        step(dve.bn_stats(stat[:, t, 1, :], resid[:, t, WIDE:]))
                        dve.bn_aggr(mv[:, t, :], stat[:, t, :, :].rearrange("p a b -> p (a b)")).then_inc(norm_var, 1)

                    def scale(t):
                        dve.wait_ge(norm_std, done + t + 1)
                        step(dve.reciprocal(rstd[:, t:t + 1], rstd[:, t:t + 1]))
                        step(dve.tensor_scalar(resid[:, t, :], resid[:, t, :], mv[:, t, 0:1], rstd[:, t:t + 1],
                                               ALU.subtract, ALU.mult))
                        dve.wait_ge(gb_landed, 32 * (i + 1))
                        dve.tensor_tensor(resid[:, t, :], resid[:, t, :], g_all[:], ALU.mult).then_inc(norm_scaled, 1)

                    statistics(0)
                    dve.wait_ge(norm_var, done + 1)
                    for t in range(T):
                        if t + 1 < T:
                            statistics(t + 1)
                        scale(t)
                        if t >= 2 and not last:
                            transpose_dve(dve, base, t - 2)
                    if not last:
                        transpose_dve(dve, base, T - 2)
                        transpose_dve(dve, base, T - 1)

                @block.gpsimd
                def _(pool):
                    for t in range(T):
                        pool.wait_ge(norm_scaled, done + t + 1)
                        pool.tensor_tensor(resid[:, t, :], resid[:, t, :], b_all[:], ALU.add).then_inc(norm_y, 1)

                @block.scalar
                def _(act):
                    for t in range(T):
                        act.wait_ge(norm_var, done + t + 1)
                        act.activation(rstd[:, t:t + 1], mv[:, t, 1:2], ACT.Sqrt, bias=eps[:, 0:1]).then_inc(norm_std, 1)
                    if not last:
                        for t in range(T):
                            transpose_act(act, base, t)
                            act.mul(resid[:, t, :], resid[:, t, :], ALPHA)

                if not last:
                    @block.tensor
                    def _(pe):
                        for t in range(T):
                            pe.wait_ge(norm_y, done + t + 1)
                            transpose_pe(pe, resid, t)
            own.close()
            n_norm[0] += 1
            if not last:
                n_xp[0] += 8

        h_relu, h_rounded, h_sq, h_ready = sem("h_relu"), sem("h_rounded"), sem("h_sq"), sem("h_ready")
        n_mlp = [0]

        def mlp_stage(layer, L0):
            own = ExitStack()
            m = n_mlp[0]
            r_buf = sbuf(own, f"r_buf{m}", [P, 4, S])
            h_hi = sbuf(own, f"h_hi{m}", [P, 2, 4, S], F32R)
            h_lo = sbuf(own, f"h_lo{m}", [P, 2, 4, S], F32R)
            HB = m * CH * 4
            AB = n_added[0]
            up = lambda c: L0 + 2 * c - 1
            down = lambda c: L0 + 2 * c + 2
            last = CH - 1
            DOWN_LAST = L0 + 2 * CH - 1
            assert CH % 2 == 0

            with nc.Block() as block:
                @block.sync
                def _(sp):
                    with sp.Fori(0, CH - 2) as c:
                        for k in range(SLOTS):
                            load_tile(sp, down(c), k, row_lap(mlp_w2[layer], c * WIDE)(k))
                        for k in range(SLOTS):
                            load_tile(sp, up(c + 2), k, up_lap(layer, c + 2)(k))
                    for lap in (down(CH - 2), DOWN_LAST, DOWN_LAST + 1, DOWN_LAST + 2):
                        load_lap(sp, lap)

                @block.tensor
                def _(pe):
                    def up_chunk(c, lap, bank0):
                        for k in range(SLOTS):
                            pe.wait_ge(w_split, lap * SLOTS + k + 1)
                            tile_T(pe, k, xT_hi[:, k, :], xT_lo[:, k, :], full_banks(bank0), k == 0, k == SLOTS - 1)

                    def down_chunk(c, lap, par, bank_left, left_free, right_free):
                        pe.wait_ge(h_ready, HB + c * 4 + 4)
                        lap_rows(pe, lap, lambda kk: h_hi[:, par, kk, :], lambda kk: h_lo[:, par, kk, :],
                                 bank_left, 4 - bank_left, left_free, right_free)

                    def both(c, par, first=False):
                        if not first:
                            pe.wait_ge(added, AB + (c - 1) * 8 + 4)
                        up_chunk(c + 1, up(c + 1), 4 - 4 * par)
                        down_chunk(c, down(c), par, 4 * par,
                                   (lambda: None) if first else (lambda: pe.wait_ge(added, AB + c * 8)),
                                   lambda: pe.wait_ge(h_relu, HB + c * 4 + 8))

                    pe.wait_ge(xp_lo, n_xp[0])
                    up_chunk(0, L0, 0)
                    both(0, 0, first=True)
                    with pe.Fori(0, CH // 2 - 1) as i:
                        both(i * 2 + 1, 1)
                        both(i * 2 + 2, 0)
                    down_chunk(last, DOWN_LAST, 1, 0, lambda: pe.wait_ge(added, AB + last * 8 - 4),
                               lambda: pe.wait_ge(added, AB + last * 8))

                @block.scalar
                def _(act):
                    def squares(c, lap, par, bank0, deep=True):
                        act.wait_ge(w_used, lap * SLOTS + SLOTS)
                        act.wait_ge(h_ready, HB + c * 4) if not isinstance(c, int) or HB + c else None
                        for j in range(4):
                            act.activation(r_buf[:, j, :], ps[:, bank0 + j, :], ACT.Relu).then_inc(h_relu, 1)
                        if deep:
                            act.wait_ge(w_used, (lap - 1) * SLOTS)
                        for j in range(4):
                            act.wait_ge(h_relu, HB + c * 4 + j + 1)
                            act.activation(h_hi[:, par, j, :], r_buf[:, j, :], ACT.Square).then_inc(h_rounded, 1)

                    def both(c, par):
                        round_lap(act, down(c))
                        squares(c + 1, up(c + 1), 1 - par, 4 - 4 * par)
                        round_lap(act, up(c + 2))

                    round_lap(act, L0 + 1)
                    squares(0, L0, 0, 0, deep=False)
                    both(0, 0)
                    with act.Fori(0, CH // 2 - 1) as i:
                        both(i * 2 + 1, 1)
                        both(i * 2 + 2, 0)
                    round_lap(act, DOWN_LAST + 1)

                @block.vector
                def _(dve):
                    def rest(c, par):
                        for j in range(4):
                            dve.wait_ge(h_rounded, HB + c * 4 + j + 1)
                            dve.tensor_tensor(r_buf[:, j, :], r_buf[:, j, :], r_buf[:, j, :], ALU.mult).then_inc(h_sq, 1)
                        for j in range(4):
                            dve.wait_ge(h_sq, HB + c * 4 + j + 1)
                            dve.tensor_tensor(h_lo[:, par, j, :], r_buf[:, j, :], h_hi[:, par, j, :].bitcast(F32),
                                              ALU.subtract).then_inc(h_ready, 1)

                    def add_down(half, lap, bank0):
                        dve.wait_ge(w_used, lap * SLOTS + 4 + 4 * half)
                        add_half(dve, half, bank0)

                    def both(c, par):
                        split_lap(dve, down(c))
                        rest(c + 1, 1 - par)
                        split_lap(dve, up(c + 2), range(4))
                        add_down(0, down(c), 4 * par)
                        split_lap(dve, up(c + 2), range(4, 8))
                        add_down(1, down(c), 4 - 4 * par)

                    split_lap(dve, L0 + 1)
                    rest(0, 0)
                    both(0, 0)
                    with dve.Fori(0, CH // 2 - 1) as i:
                        both(i * 2 + 1, 1)
                        both(i * 2 + 2, 0)
                    split_lap(dve, DOWN_LAST + 1, range(4))
                    add_down(0, DOWN_LAST, 0)
                    split_lap(dve, DOWN_LAST + 1, range(4, 8))
                    add_down(1, DOWN_LAST, 4)
            own.close()
            n_mlp[0] += 1
            n_added[0] += 8 * CH

        norm_stage(ln1_g[0:1], ln1_b[0:1])
        mlp_stage(0, L_MLP0)
        norm_stage(ln2_g[0:1], ln2_b[0:1])

        odd = ExitStack()
        NC = INNER // P
        xcT = sbuf(odd, "xcT", [P, NC, S])
        val = sbuf(odd, "val", [P, T, INNER])
        blk = sbuf(odd, "blk", [P, 3, NC, M_BLK])
        bd_mask = sbuf(odd, "bd_mask", [P, P // M_BLK, M_BLK])
        conv_w = sbuf(odd, "conv_w", [P, M_CONV, NC])
        conv_b = sbuf(odd, "conv_b", [P, NC])
        skip_c = sbuf(odd, "skip_c", [P, NC])
        norm_c = sbuf(odd, "norm_c", [P, NC])
        gate_b = sbuf(odd, "gate_b", [36, 1])
        gate_x = sbuf(odd, "gate_x", [36, S])
        pre = ExitStack()
        xm = sbuf(pre, "xm", [P, 2, CT, M_CONV - 1 + S])
        conv = sbuf(pre, "conv", [P, 2, S])
        bd_v = sbuf(pre, "bd_v", [P, 2, P])
        g_rows = sbuf(pre, "g_rows", [P, 3, NC, M_BLK * 8])
        g_prod = sbuf(pre, "g_prod", [P, NC, 8, M_BLK])
        g_fold = sbuf(pre, "g_fold", [P, 2, NC, 8])
        g_mat = sbuf(pre, "g_mat", [P, 2, NC, 36])
        od_params, od_zero, fold_done = sem("od_params"), sem("od_zero"), sem("fold_done")
        xm_out, conv0, conv_done, xc_ready = sem("xm_out"), sem("conv0"), sem("conv_done"), sem("xc_ready")
        bd_ready, v_mm, v_out, gates_mm, gate_out = (sem("bd_ready"), sem("v_mm"), sem("v_out"), sem("gates_mm"),
                                                     sem("gate_out"))
        PAD = M_CONV - 1
        n_odd_params = [0]
        with nc.Block() as block:
            @block.sync
            def _(sp):
                def param(dst, src):
                    with nc.allow_non_contiguous_dma("small parameters, by channel"):
                        sp.dma_start(dst, src).then_inc(od_params, 16)
                    n_odd_params[0] += 16
                for i, w in enumerate((od_w_q, od_w_k, od_w_v)):
                    param(blk[:, i, :, :], w[0].rearrange("(t j) d e -> (j d) t e", t=NC))
                for d in range(M_CONV):
                    param(conv_w[:, d, :], od_conv_w[0, d].rearrange("(t p) -> p t", p=P))
                param(conv_b[:], od_conv_b[0].rearrange("(t p) -> p t", p=P))
                param(skip_c[:], od_skip[0].rearrange("(t p) -> p t", p=P))
                param(norm_c[:], od_norm[0].rearrange("h (t p) -> p (h t)", p=P))
                param(gate_b[0:4, :], od_b_gate[0, 0:4].rearrange("(g o) -> g o", o=1))
                param(gate_b[32:36, :], od_b_gate[0, 4:8].rearrange("(g o) -> g o", o=1))
                for i in range(3):
                    rows = od_w_gate[0, i * INNER:(i + 1) * INNER].rearrange("(t j e) g -> j t (e g)", t=NC, e=M_BLK)
                    for d in range(M_BLK):
                        param(g_rows[d:P:M_BLK, i, :, :], rows)
                for lap in range(L_XM + 2, L_HEAD + 2):
                    load_lap(sp, lap)

            @block.gpsimd
            def _(pool):
                step = stepper(pool, "pool", pool_step)
                pool.memset(xm[:, :, :, 0:PAD], 0.0).then_inc(od_zero, 1)
                pool.memset(g_mat[:], 0.0).then_inc(od_zero, 1)
                step(pool.memset(bd_mask[:], 1.0))
                step(pool.affine_select(out=bd_mask[:], in_=bd_mask[:], compare_op=ALU.is_ge, fill=0.0, base=0,
                                        pattern=[[-M_BLK, P // M_BLK], [0, M_BLK]], channel_multiplier=1))
                step(pool.affine_select(out=bd_mask[:], in_=bd_mask[:], compare_op=ALU.is_ge, fill=0.0, base=M_BLK - 1,
                                        pattern=[[M_BLK, P // M_BLK], [0, M_BLK]], channel_multiplier=-1))
                pool.wait_ge(od_params, 16 * 24)
                for ct in range(NC):
                    if ct >= 2:
                        pool.wait_ge(v_mm, ct - 1)
                    pool.tensor_tensor(bd_v[:, ct % 2, :].rearrange("p (j e) -> p j e", e=M_BLK), bd_mask[:],
                                       blk[:, 2, ct, :].unsqueeze(1).broadcast_to([P, P // M_BLK, M_BLK]),
                                       ALU.mult).then_inc(bd_ready, 1)

            @block.tensor
            def _(pe):
                def from_group(g):
                    pe.wait_ge(xm_out, CT * (g + 1))
                    for j in range(CT):
                        ct = g * CT + j
                        pe.wait_ge(bd_ready, ct + 1)
                        for t in range(T - 1):
                            pe.matmul(ps[:, 4 + t, j * P:(j + 1) * P],
                                      xm[:, g % 2, j, PAD + t * P:PAD + (t + 1) * P], bd_v[:, ct % 2, :],
                                      start=True, stop=True)
                        mm = pe.matmul(ps[:, 3, j * P:(j + 1) * P],
                                       xm[:, g % 2, j, PAD + (T - 1) * P:PAD + T * P], bd_v[:, ct % 2, :],
                                       start=True, stop=True)
                        mm.then_inc(v_mm, 1)
                    if g == 0:
                        pe.wait_ge(fold_done, 2)
                    for j in range(CT):
                        ct = g * CT + j
                        pe.matmul(ps[0:36, 7, :], g_mat[:, 1, ct, :], xm[:, g % 2, j, PAD:], start=(ct == 0), stop=False)
                        pe.wait_ge(xc_ready, ct + 1)
                        mm = pe.matmul(ps[0:36, 7, :], g_mat[:, 0, ct, :], xcT[:, ct, :], start=False,
                                       stop=(ct == NC - 1))
                    mm.then_inc(gates_mm, 1)

                pe.wait_ge(xp_lo, n_xp[0])
                for g in range(M_HEADS):
                    if g >= 1:
                        pe.wait_ge(xm_out, CT * g)
                        pe.wait_ge(conv0, CT * g)
                        pe.wait_ge(v_out, g)
                    lap_T(pe, L_XM + g, full_banks(0))
                    pe.wait_ge(conv0, CT * (g + 1))
                    from_group(g)

            @block.scalar
            def _(act):
                def silu(ct):
                    act.wait_ge(conv_done, ct + 1)
                    act.activation(xcT[:, ct, :], conv[:, ct % 2, :], ACT.Silu).then_inc(xc_ready, 1)

                act.wait_ge(od_params, 16 * 24)
                for g in range(M_HEADS):
                    round_lap(act, L_XM + g + 1)
                    act.wait_ge(w_used, lap_done(L_XM + g))
                    if g == 0:
                        act.wait_ge(od_zero, 2)
                    if g >= 2:
                        act.wait_ge(gates_mm, g - 1)
                        act.wait_ge(conv_done, CT * (g - 1))
                    for j in range(CT):
                        act.activation(xm[:, g % 2, j, PAD:], ps[:, j, :], ACT.Copy).then_inc(xm_out, 1)
                    for j in range(CT):
                        ct = g * CT + j
                        if ct >= 2:
                            act.wait_ge(conv_done, ct - 1)
                            act.wait_ge(xc_ready, ct - 1)
                        act.activation(conv[:, ct % 2, :], ps[:, j, :], ACT.Identity, bias=conv_b[:, ct:ct + 1],
                                       scale=conv_w[:, PAD, ct:ct + 1]).then_inc(conv0, 1)
                        if j >= 1:
                            silu(ct - 1)
                    silu(g * CT + CT - 1)
                act.wait_ge(gates_mm, M_HEADS)
                act.activation(gate_x[0:36, :], ps[0:36, 7, :], ACT.Copy).then_inc(gate_out, 1)

            @block.vector
            def _(dve):
                step = stepper(dve, "dve", dve_step)
                dve.wait_ge(od_params, 16 * 24)
                dve.wait_ge(od_zero, 2)
                for i, dst in ((0, 0), (1, None), (2, 1)):
                    step(dve.tensor_tensor(g_prod[:], blk[:, i, :, :].unsqueeze(2).broadcast_to([P, NC, 8, M_BLK]),
                                           g_rows[:, i, :, :].rearrange("p t (e g) -> p t g e", e=M_BLK), ALU.mult))
                    if i == 0:
                        step(dve.tensor_reduce(g_fold[:, 0, :, :], g_prod[:], AX.X, ALU.add))
                    else:
                        step(dve.tensor_reduce(g_fold[:, 1, :, :], g_prod[:], AX.X, ALU.add))
                        if i == 1:
                            step(dve.tensor_tensor(g_fold[:, 0, :, :], g_fold[:, 0, :, :], g_fold[:, 1, :, :], ALU.add))
                dve.tensor_copy(g_mat[:, :, :, 0:4], g_fold[:, :, :, 0:4]).then_inc(fold_done, 1)
                dve.tensor_copy(g_mat[:, :, :, 32:36], g_fold[:, :, :, 4:8]).then_inc(fold_done, 1)
                for g in range(M_HEADS):
                    split_lap(dve, L_XM + g + 1)
                    for j in range(CT):
                        ct = g * CT + j
                        dve.wait_ge(conv0, ct + 1)
                        for tap in range(PAD):
                            ins = dve.scalar_tensor_tensor(out=conv[:, ct % 2, :], in0=xm[:, g % 2, j, tap:tap + S],
                                                           scalar=conv_w[:, tap, ct:ct + 1], in1=conv[:, ct % 2, :],
                                                           op0=ALU.mult, op1=ALU.add)
                            if tap < PAD - 1:
                                step(ins)
                        ins.then_inc(conv_done, 1)
                    dve.wait_ge(v_mm, CT * (g + 1))
                    for t in range(T):
                        ins = dve.tensor_copy(val[:, t, g * DH:(g + 1) * DH], ps[:, 4 + t if t < T - 1 else 3, :])
                    ins.then_inc(v_out, 1)
        n_xp_odd = n_xp[0]
        pre.close()

        rows = ExitStack()
        a_col = sbuf(odd, "a_col", [P, 2, T, M_HEADS])
        neg_M = sbuf(odd, "neg_M", [4, S])
        sel = sbuf(odd, "sel", [4, M_HEADS, P])
        above = sbuf(odd, "above", [P, P])
        i_row = sbuf(rows, "i_row", [4, S])
        f_rows = sbuf(rows, "f_rows", [36, 2, S])
        lf_row = sbuf(rows, "lf_row", [4, S])
        b_row = sbuf(rows, "b_row", [4, S])
        a_row = sbuf(rows, "a_row", [4, S])
        m_row = sbuf(rows, "m_row", [4, S])
        m_max = sbuf(rows, "m_max", [4, S])
        one_row = sbuf(rows, "one_row", [4, S])
        f_ready, row_const, a_ready, em_ready, m_done, cols_done = (sem("f_ready"), sem("row_const"), sem("a_ready"),
                                                                    sem("em_ready"), sem("m_done"), sem("cols_done"))
        with nc.Block() as block:
            @block.gpsimd
            def _(pool):
                step = stepper(pool, "pool", pool_step)
                pool.memset(one_row[:], 1.0).then_inc(row_const, 1)
                step(pool.memset(sel[:], 1.0))
                step(pool.affine_select(out=sel[:], in_=sel[:], compare_op=ALU.is_equal, fill=0.0, base=0,
                                        pattern=[[-1, M_HEADS], [0, P]], channel_multiplier=1))
                step(pool.memset(above[:], 0.0))
                step(pool.affine_select(out=above[:], in_=above[:], compare_op=ALU.is_ge, fill=MASKED, base=0,
                                        pattern=[[1, P]], channel_multiplier=-1))

            @block.scalar
            def _(act):
                step = stepper(act, "act", act_step)
                act.activation(i_row[:], gate_x[0:4, :], ACT.Identity, bias=gate_b[0:4, :])
                step(act.activation(f_rows[32:36, 0, :], gate_x[32:36, :], ACT.Identity, bias=gate_b[32:36, :]))
                step(act.activation(f_rows[32:36, 1, :], f_rows[32:36, 0, :], ACT.Abs))
                step(act.activation(f_rows[32:36, 1, :], f_rows[32:36, 1, :], ACT.Exp, scale=-1.0))
                act.activation(f_rows[32:36, 1, :], f_rows[32:36, 1, :], ACT.Ln, bias=1.0).then_inc(f_ready, 1)
                act.wait_ge(m_done, 1)
                act.activation(m_row[:], m_row[:], ACT.Exp, scale=-1.0).then_inc(em_ready, 1)

            @block.vector
            def _(dve):
                step = stepper(dve, "dve", dve_step)
                dve.wait_ge(f_ready, 1)
                dve.wait_ge(row_const, 1)
                step(dve.scalar_tensor_tensor(out=lf_row[:], in0=f_rows[32:36, 0, :], scalar=0.0,
                                              in1=f_rows[32:36, 1, :], op0=ALU.min, op1=ALU.subtract))
                step(dve.tensor_tensor_scan(b_row[:], one_row[:], lf_row[:], 0.0, ALU.mult, ALU.add))
                dve.tensor_tensor(a_row[:], i_row[:], b_row[:], ALU.subtract).then_inc(a_ready, 1)
                dve.wait_ge(a_ready, 1)
                step(dve.tensor_tensor_scan(m_max[:], a_row[:], a_row[:], 0.0, ALU.max, ALU.max))
                step(dve.tensor_tensor(m_row[:], b_row[:], m_max[:], ALU.add))
                dve.tensor_scalar(neg_M[:], m_max[:], -1.0, None, ALU.mult).then_inc(m_done, 1)
                dve.wait_ge(cols_done, 1)
                step(dve.tensor_copy(a_col[:].rearrange("p a t h -> p (a t h)"), ps[:, 0, 0:2 * T * M_HEADS]))

            @block.tensor
            def _(pe):
                pe.wait_ge(a_ready, 1)
                for t in range(T):
                    pe.transpose(ps[:, 0, t * 4:t * 4 + 4], a_row[:, t * P:(t + 1) * P], ident[0:4, 0:4])
                pe.wait_ge(em_ready, 1)
                for t in range(T):
                    mm = pe.transpose(ps[:, 0, (T + t) * 4:(T + t) * 4 + 4], m_row[:, t * P:(t + 1) * P],
                                      ident[0:4, 0:4])
                mm.then_inc(cols_done, 1)
        rows.close()

        heads = ExitStack()
        bd_qk = sbuf(heads, "bd_qk", [P, 2, CT, P])
        neg_all = sbuf(heads, "neg_all", [P, S])
        diag = sbuf(heads, "diag", [P, T, P])
        OFF = [sum((T - j) * P for j in range(i)) for i in range(T)]
        wts = sbuf(heads, "wts", [P, OFF[-1] + P])
        hg = sbuf(heads, "hg", [P, T, DH])
        den = sbuf(heads, "den", [P, 2, T])
        h_stat = sbuf(heads, "h_stat", [P, T, 6])
        h_mv = sbuf(heads, "h_mv", [P, T, 2])
        h_std = sbuf(heads, "h_std", [P, T])
        qk_scope = ExitStack()
        qT = sbuf(qk_scope, "qT", [P, CT, S])
        kT = sbuf(qk_scope, "kT", [P, CT, S])
        qk_scope.close()
        y_hi = sbuf(heads, "y_hi", [P, CT, S], F32R)
        y_lo = sbuf(heads, "y_lo", [P, CT, S], F32R)
        bdqk_ready, qk_mm, qk_out, m_bc, m_bc_out = (sem("bdqk_ready"), sem("qk_mm"), sem("qk_out"), sem("m_bc"),
                                                     sem("m_bc_out"))
        diag_ready, wexp, dot_mm, w_ready = sem("diag_ready"), sem("wexp"), sem("dot_mm"), sem("w_ready")
        sig_ready, num_mm, h_gated, h_var, h_stdr, h_normed = (sem("sig_ready"), sem("num_mm"), sem("h_gated"),
                                                               sem("h_var"), sem("h_stdr"), sem("h_normed"))
        hT_mm, xs_ready, y_f32, y_rounded, y_ready = (sem("hT_mm"), sem("xs_ready"), sem("y_f32"), sem("y_rounded"),
                                                      sem("y_ready"))
        AB = n_added[0]
        with nc.Block() as block:
            @block.sync
            def _(sp):
                for lap in range(L_HEAD + 2, L_MLP1 + 2):
                    load_lap(sp, lap)

            @block.gpsimd
            def _(pool):
                for h in range(M_HEADS):
                    if h >= 1:
                        pool.wait_ge(qk_mm, 2 * h)
                    for i in range(2):
                        for j in range(CT):
                            ins = pool.tensor_tensor(
                                bd_qk[:, i, j, :].rearrange("p (j e) -> p j e", e=M_BLK), bd_mask[:],
                                blk[:, i, h * CT + j, :].unsqueeze(1).broadcast_to([P, P // M_BLK, M_BLK]), ALU.mult)
                    ins.then_inc(bdqk_ready, 1)

            @block.tensor
            def _(pe):
                for h in range(M_HEADS):
                    pe.wait_ge(bdqk_ready, h + 1)
                    if h >= 1:
                        pe.wait_ge(added, AB + 8 * h)
                        pe.wait_ge(w_used, lap_done(L_HEAD + 2 * h - 1))
                    for i in range(2):
                        for j in range(CT):
                            mm = pe.matmul(ps[:, 4 * i + j, :], bd_qk[:, i, j, :], xcT[:, h * CT + j, :],
                                           start=True, stop=True)
                        mm.then_inc(qk_mm, 1)
                    pe.wait_ge(qk_out, 8 * h + 4)
                    pe.matmul(ps[:, 0, :], sel[:, h, :], neg_M[:], start=True, stop=True).then_inc(m_bc, 1)
                    pe.wait_ge(qk_out, 8 * h + 8)
                    lap_N(pe, L_HEAD + 2 * h, 4)
                    pe.wait_ge(m_bc_out, h + 1)
                    for i in range(T):
                        n = (T - i) * P
                        for j in range(CT):
                            mm = pe.matmul(ps[:, i, 0:n], kT[:, j, i * P:(i + 1) * P], qT[:, j, i * P:],
                                           start=(j == 0), stop=(j == CT - 1))
                        mm.then_inc(dot_mm, 1)
                    pe.wait_ge(sig_ready, T * (h + 1))
                    pe.wait_ge(w_ready, T * (h + 1))
                    for t in range(T):
                        for i in range(t + 1):
                            lhs = wts[:, OFF[i] + (t - i) * P:OFF[i] + (t - i + 1) * P]
                            pe.matmul(ps[:, t, :], lhs, val[:, i, h * DH:(h + 1) * DH], start=(i == 0), stop=(i == t))
                    for t in range(T):
                        for i in range(t + 1):
                            lhs = wts[:, OFF[i] + (t - i) * P:OFF[i] + (t - i + 1) * P]
                            mm = pe.matmul(ps[:, 4, t:t + 1], lhs, ones[:, 0:1], start=(i == 0), stop=(i == t))
                    mm.then_inc(num_mm, 1)
                    pe.wait_ge(h_normed, T * (h + 1))
                    for j in range(CT):
                        for t in range(T):
                            mm = pe.transpose(ps[:, 4 + j, t * P:(t + 1) * P], hg[:, t, j * P:(j + 1) * P], ident[:])
                        mm.then_inc(hT_mm, 1)
                    pe.wait_ge(y_ready, CT * (h + 1))
                    lap_rows(pe, L_HEAD + 2 * h + 1, lambda kk: y_hi[:, kk, :], lambda kk: y_lo[:, kk, :], 0, 4,
                             lambda: None, lambda: None)

            @block.scalar
            def _(act):
                for h in range(M_HEADS):
                    lap_o, lap_w = L_HEAD + 2 * h, L_HEAD + 2 * h + 1
                    act.wait_ge(qk_mm, 2 * h + 1)
                    for j in range(CT):
                        act.activation(qT[:, j, :], ps[:, j, :], ACT.Copy).then_inc(qk_out, 1)
                    act.wait_ge(qk_mm, 2 * h + 2)
                    for j in range(CT):
                        act.activation(kT[:, j, :], ps[:, 4 + j, :], ACT.Copy).then_inc(qk_out, 1)
                    act.wait_ge(m_bc, h + 1)
                    act.activation(neg_all[:], ps[:, 0, :], ACT.Copy).then_inc(m_bc_out, 1)
                    act.wait_ge(m_bc_out, h + 1)
                    act.wait_ge(diag_ready, h + 1)
                    for i in range(T):
                        bias = a_col[:, 0, i, h:h + 1]
                        if i < T - 1:
                            act.activation(wts[:, OFF[i] + P:OFF[i] + (T - i) * P], neg_all[:, (i + 1) * P:], ACT.Exp,
                                           bias=bias)
                        act.activation(wts[:, OFF[i]:OFF[i] + P], diag[:, i, :], ACT.Exp, bias=bias).then_inc(wexp, 1)
                    round_lap(act, lap_w)
                    for j in range(CT):
                        ct = h * CT + j
                        act.activation(xcT[:, ct, :], xcT[:, ct, :], ACT.Copy, scale=skip_c[:, ct:ct + 1]).then_inc(xs_ready, 1)
                    act.wait_ge(w_used, lap_done(lap_o))
                    for t in range(T):
                        act.activation(hg[:, t, :], ps[:, 4 + t, :], ACT.Sigmoid).then_inc(sig_ready, 1)
                    act.wait_ge(h_var, h + 1)
                    act.activation(h_std[:], h_mv[:, :, 1], ACT.Sqrt, bias=eps[:, 0:1]).then_inc(h_stdr, 1)
                    for j in range(CT):
                        act.wait_ge(y_f32, CT * h + j + 1)
                        act.activation(y_hi[:, j, :], hg[:, j, :], ACT.Copy).then_inc(y_rounded, 1)
                    round_lap(act, lap_w + 1)

            @block.vector
            def _(dve):
                step = stepper(dve, "dve", dve_step)
                for h in range(M_HEADS):
                    lap_w = L_HEAD + 2 * h + 1
                    dve.wait_ge(m_bc_out, h + 1)
                    dve.tensor_tensor(diag[:], neg_all[:].rearrange("p (t q) -> p t q", t=T),
                                      above[:].unsqueeze(1).broadcast_to([P, T, P]), ALU.add).then_inc(diag_ready, 1)
                    split_lap(dve, lap_w)
                    for i in range(T):
                        n = (T - i) * P
                        dve.wait_ge(wexp, T * h + i + 1)
                        dve.wait_ge(dot_mm, T * h + i + 1)
                        w = wts[:, OFF[i]:OFF[i] + n]
                        dve.scalar_tensor_tensor(out=w, in0=ps[:, i, 0:n], scalar=DH ** -0.5, in1=w, op0=ALU.mult,
                                                 op1=ALU.mult).then_inc(w_ready, 1)
                    dve.wait_ge(num_mm, h + 1)
                    step(dve.tensor_scalar(den[:, 0, :], ps[:, 4, 0:T], -1.0, None, ALU.mult))
                    step(dve.tensor_tensor(den[:, 0, :], ps[:, 4, 0:T], den[:, 0, :], ALU.max))
                    step(dve.tensor_tensor(den[:, 0, :], den[:, 0, :], a_col[:, 1, :, h], ALU.max))
                    step(dve.reciprocal(den[:, 1, :], den[:, 0, :]))
                    dve.wait_ge(sig_ready, T * (h + 1))
                    for t in range(T):
                        ins = dve.scalar_tensor_tensor(out=hg[:, t, :], in0=ps[:, t, :], scalar=den[:, 1, t:t + 1],
                                                       in1=hg[:, t, :], op0=ALU.mult, op1=ALU.mult)
                    step(ins)
                    for t in range(T):
                        ins = dve.bn_stats(h_stat[:, t, :], hg[:, t, :])
                    step(ins)
                    for t in range(T):
                        ins = dve.bn_aggr(h_mv[:, t, :], h_stat[:, t, :])
                    ins.then_inc(h_var, 1)
                    dve.wait_ge(h_stdr, h + 1)
                    step(dve.reciprocal(h_std[:], h_std[:]))
                    for t in range(T):
                        dve.tensor_scalar(hg[:, t, :], hg[:, t, :], h_mv[:, t, 0:1], h_std[:, t:t + 1],
                                          ALU.subtract, ALU.mult).then_inc(h_normed, 1)
                    dve.wait_ge(hT_mm, CT * (h + 1))
                    dve.wait_ge(xs_ready, CT * (h + 1))
                    for j in range(CT):
                        ct = h * CT + j
                        dve.scalar_tensor_tensor(out=hg[:, j, :], in0=ps[:, 4 + j, :], scalar=norm_c[:, ct:ct + 1],
                                                 in1=xcT[:, ct, :], op0=ALU.mult, op1=ALU.add).then_inc(y_f32, 1)
                    for j in range(CT):
                        dve.wait_ge(y_rounded, CT * h + j + 1)
                        dve.tensor_tensor(y_lo[:, j, :], hg[:, j, :], y_hi[:, j, :].bitcast(F32),
                                          ALU.subtract).then_inc(y_ready, 1)
                    split_lap(dve, lap_w + 1, range(4))
                    dve.wait_ge(w_used, lap_w * SLOTS + 4)
                    add_half(dve, 0, 0)
                    split_lap(dve, lap_w + 1, range(4, 8))
                    dve.wait_ge(w_used, lap_w * SLOTS + 8)
                    add_half(dve, 1, 4)
        n_added[0] += 8 * M_HEADS
        heads.close()
        odd.close()

        norm_stage(ln1_g[1:2], ln1_b[1:2])
        mlp_stage(1, L_MLP1)
        norm_stage(ln2_g[1:2], ln2_b[1:2], last=True)


_INS = ["x", "ev_w_in", "ev_g_w2", "ev_g_b2", "ev_g_norm", "ev_w_out", "od_w_in", "od_conv_w", "od_conv_b",
        "od_w_q", "od_w_k", "od_w_v", "od_w_gate", "od_b_gate", "od_skip", "od_norm", "od_w_out",
        "ln1_g", "ln1_b", "ln2_g", "ln2_b", "mlp_w1", "mlp_w2"]


def kernel(**inputs):
    import numpy as _np
    import concourse.bacc as _bacc
    from concourse import mybir as _mybir
    from concourse.bass_utils import run_bass_kernel_spmd as _run

    nc = _bacc.Bacc("TRN2", target_bir_lowering=False, num_devices=1)
    arrays, args = {}, []
    for name in _INS:
        a = _np.ascontiguousarray(inputs[name])
        arrays[f"in_{name}"] = a
        args.append(nc.dram_tensor(f"in_{name}", a.shape, _mybir.dt.from_np(a.dtype), kind="ExternalInput").ap())
    shape = tuple(inputs["x"].shape)
    args.append(nc.dram_tensor("out_0", shape, _mybir.dt.float32, kind="ExternalOutput").ap())
    hybrid_trunk(nc, *args)
    r = _run(nc, [arrays], core_ids=[0])
    return r.results[0]["out_0"]
```

```python
from contextlib import ExitStack

import concourse.bass as bass
from concourse import mybir

F32 = mybir.dt.float32
F32R = mybir.dt.float32r
U32 = mybir.dt.uint32
ALU = mybir.AluOpType
ACT = mybir.ActivationFunctionType
AX = mybir.AxisListType

P = 128
SLOTS = 8
WIDE = 512
NEG = -3.0e38
MASKED = -1.0e30
LN_EPS = 1e-5

A_HEADS, A_DIM, TOPK = 8, 64, 128
G_HEADS, G_DIM, G_RANK, G_TAU = 4, 128, 16, 16.0
M_HEADS, M_CONV, M_BLK = 4, 4, 4


def hybrid_trunk(nc, x, ev_w_in, ev_g_w2, ev_g_b2, ev_g_norm, ev_w_out, od_w_in, od_conv_w, od_conv_b,
                 od_w_q, od_w_k, od_w_v, od_w_gate, od_b_gate, od_skip, od_norm, od_w_out,
                 ln1_g, ln1_b, ln2_g, ln2_b, mlp_w1, mlp_w2, out):
    _, S, D = x.shape
    T = S // P
    KD = D // P
    DEPTH = ln1_g.shape[0]
    ALPHA = (2 * DEPTH) ** 0.25
    FF = mlp_w1.shape[2]
    CH = FF // WIDE
    INNER = od_w_out.shape[1]
    DH = INNER // M_HEADS
    CT = DH // P
    assert (S, D, KD, T, DH) == (512, 1024, SLOTS, 4, WIDE)

    AQ, AK, AV = 0, 512, 576
    IQ, IK, IW = 640, 1152, 1216
    GQ, GK, GV, GR, GLR = 1224, 1736, 2248, 2760, 3272
    w_in = ev_w_in[0]

    def column_lap(w, c0, width, row0=0):
        return lambda k: [(0, w[row0 + k * P:row0 + (k + 1) * P, c0:c0 + width])]

    def small_lap(k):
        rows = slice(k * P, (k + 1) * P)
        return [(0, w_in[rows, AK:AK + 128]), (P, w_in[rows, IK:IK + 72]), (P + 96, w_in[rows, GLR:GLR + G_RANK])]

    def row_lap(w, r0):
        return lambda k: [(0, w[bass.ds(r0 + (k % 4) * P, P), (k // 4) * WIDE:(k // 4 + 1) * WIDE])]

    def up_lap(layer, c):
        return lambda k: [(0, mlp_w1[layer, k * P:(k + 1) * P, bass.ds(c * WIDE, WIDE)])]

    LAPS = [column_lap(w_in, IQ, 512), small_lap, column_lap(w_in, AQ, 512), column_lap(w_in, GQ, 512),
            column_lap(w_in, GK, 512), column_lap(w_in, GV, 512), column_lap(w_in, GR, 512),
            column_lap(ev_w_out[0], 0, WIDE), column_lap(ev_w_out[0], WIDE, WIDE)]
    L_IQ, L_SMALL, L_AQ, L_GQ, L_GK, L_GV, L_GR, L_WO = range(8)
    WIDTHS = {L_SMALL: P + 96 + G_RANK}

    def add_mlp(layer):
        base = len(LAPS)
        LAPS.append(up_lap(layer, 0))
        for c in range(CH):
            if c + 1 < CH:
                LAPS.append(up_lap(layer, c + 1))
            LAPS.append(row_lap(mlp_w2[layer], c * WIDE))
        return base

    L_MLP0 = add_mlp(0)
    L_XM = len(LAPS)
    for h in range(M_HEADS):
        LAPS.append(column_lap(od_w_in[0], h * WIDE, WIDE))
    L_GATE, L_PROJ = {}, {}
    for h in range(M_HEADS + 1):
        if h < M_HEADS:
            L_GATE[h] = len(LAPS)
            LAPS.append(column_lap(od_w_in[0], INNER + h * WIDE, WIDE))
        if h >= 1:
            L_PROJ[h - 1] = len(LAPS)
            LAPS.append(row_lap(od_w_out[0], (h - 1) * WIDE))
    L_MLP1 = add_mlp(1)
    N_LAPS = len(LAPS)

    top = ExitStack()

    def sem(name):
        return top.enter_context(nc.semaphore(name))

    def sbuf(scope, name, shape, dt=F32):
        return scope.enter_context(nc.sbuf_tensor(name, shape, dt))

    with top:
        resid = sbuf(top, "resid", [P, T, D])
        with ExitStack() as aliased:
            xT_hi = sbuf(aliased, "xT_hi", [P, KD, S], F32R)
            xT_lo = sbuf(aliased, "xT_lo", [P, KD, S], F32R)
        x_space = sbuf(top, "x_space", [P, 2 * KD, S])
        w_raw = sbuf(top, "w_raw", [P, SLOTS, WIDE])
        w_hi = sbuf(top, "w_hi", [P, SLOTS, WIDE], F32R)
        w_lo = sbuf(top, "w_lo", [P, SLOTS, WIDE], F32R)
        ident = sbuf(top, "ident", [P, P])
        eps = sbuf(top, "eps", [P, 1])
        ones = sbuf(top, "ones", [P, P])
        ps = top.enter_context(nc.psum_tensor("ps", [P, 8, WIDE], F32))

        w_landed = [sem(f"w_landed{k}") for k in range(SLOTS)]
        w_rounded = sem("w_rounded")
        w_split = sem("w_split")
        w_used = sem("w_used")
        xp_done = sem("xp_done")
        xp_hi = sem("xp_hi")
        xp_lo = sem("xp_lo")
        added = sem("added")
        consts = sem("consts")
        dve_step = sem("dve_step")
        act_step = sem("act_step")
        pool_step = sem("pool_step")
        n_step = {"dve": 0, "act": 0, "pool": 0}
        n_added = [0]
        n_xp = [0]

        def stepper(eng, name, semaphore):
            def step(ins):
                n_step[name] += 1
                ins.then_inc(semaphore, 1)
                eng.wait_ge(semaphore, n_step[name])
            return step

        def load_tile(sp, lap, k, parts):
            if not (isinstance(lap, int) and lap == 0):
                sp.wait_ge(w_split, lap * SLOTS + k - SLOTS + 1)
            for col, src in parts:
                sp.dma_start(w_raw[:, k, col:col + src.shape[1]], src).then_inc(w_landed[k], 16)

        def load_lap(sp, lap, ks=range(SLOTS)):
            if lap < N_LAPS:
                for k in ks:
                    load_tile(sp, lap, k, LAPS[lap](k))

        def landed(lap):
            before = not isinstance(lap, int) or lap >= L_SMALL
            return (lap + 1 + (len(small_lap(0)) - 1 if before else 0)) * 16

        def round_tile(act, lap, k, width=WIDE):
            act.wait_ge(w_landed[k], landed(lap))
            if not (isinstance(lap, int) and lap == 0):
                act.wait_ge(w_used, lap * SLOTS + k - SLOTS + 1)
            act.activation(w_hi[:, k, 0:width], w_raw[:, k, 0:width], ACT.Copy).then_inc(w_rounded, 1)

        def split_tile(dve, lap, k, width=WIDE):
            dve.wait_ge(w_rounded, lap * SLOTS + k + 1)
            dve.tensor_tensor(w_lo[:, k, 0:width], w_raw[:, k, 0:width], w_hi[:, k, 0:width].bitcast(F32),
                              ALU.subtract).then_inc(w_split, 1)

        def round_lap(act, lap, ks=range(SLOTS)):
            if not isinstance(lap, int) or lap < N_LAPS:
                for k in ks:
                    round_tile(act, lap, k, WIDTHS.get(lap, WIDE) if isinstance(lap, int) else WIDE)

        def split_lap(dve, lap, ks=range(SLOTS)):
            if not isinstance(lap, int) or lap < N_LAPS:
                for k in ks:
                    split_tile(dve, lap, k, WIDTHS.get(lap, WIDE) if isinstance(lap, int) else WIDE)

        def tile_T(pe, k, a_hi, a_lo, outs, first, last):
            for dst, c0, cn in outs:
                pe.matmul(dst, w_hi[:, k, c0:c0 + cn], a_hi, start=first, stop=False)
                pe.matmul(dst, w_hi[:, k, c0:c0 + cn], a_lo, start=False, stop=False)
                mm = pe.matmul(dst, w_lo[:, k, c0:c0 + cn], a_hi, start=False, stop=last)
            mm.then_inc(w_used, 1)

        def tile_N(pe, k, a_hi, a_lo, bank0, first, last):
            for t in range(T):
                ts = slice(t * P, (t + 1) * P)
                pe.matmul(ps[:, bank0 + t, :], a_hi[:, ts], w_hi[:, k, :], start=first, stop=False)
                pe.matmul(ps[:, bank0 + t, :], a_hi[:, ts], w_lo[:, k, :], start=False, stop=False)
                mm = pe.matmul(ps[:, bank0 + t, :], a_lo[:, ts], w_hi[:, k, :], start=False, stop=last)
            mm.then_inc(w_used, 1)

        def lap_T(pe, lap, outs):
            for k in range(SLOTS):
                pe.wait_ge(w_split, lap * SLOTS + k + 1)
                tile_T(pe, k, xT_hi[:, k, :], xT_lo[:, k, :], outs, k == 0, k == SLOTS - 1)

        def lap_N(pe, lap, bank0):
            for k in range(SLOTS):
                pe.wait_ge(w_split, lap * SLOTS + k + 1)
                tile_N(pe, k, xT_hi[:, k, :], xT_lo[:, k, :], bank0, k == 0, k == SLOTS - 1)

        def lap_rows(pe, lap, a_hi, a_lo, bank_left, bank_right, before_left, before_right):
            for half, bank0, before in ((0, bank_left, before_left), (1, bank_right, before_right)):
                before()
                for kk in range(4):
                    pe.wait_ge(w_split, lap * SLOTS + half * 4 + kk + 1)
                    tile_N(pe, half * 4 + kk, a_hi(kk), a_lo(kk), bank0, kk == 0, kk == 3)

        def by_tokens(pe, lap, parts, space, final=False):
            for t in range(T):
                ts = slice(t * P, (t + 1) * P)
                for slots, a_hi, a_lo, bank0 in parts:
                    for kk, k in enumerate(slots):
                        if t == 0:
                            pe.wait_ge(w_split, lap * SLOTS + k + 1)
                        first, end = kk == 0, k == slots[-1]
                        pe.matmul(ps[:, bank0 + t, :], a_hi(kk)[:, ts], w_hi[:, k, :], start=first, stop=False)
                        pe.matmul(ps[:, bank0 + t, :], a_hi(kk)[:, ts], w_lo[:, k, :], start=False, stop=False)
                        mm = pe.matmul(ps[:, bank0 + t, :], a_lo(kk)[:, ts], w_hi[:, k, :], start=False, stop=end)
                        if t == T - 1:
                            mm.then_inc(w_used, 1)
                        elif k == SLOTS - 1:
                            mm.then_inc(token_done, 1)
                if t >= 2 and not final:
                    norm_pe(pe, space, t - 2)
            if not final:
                for t in range(T - 2, T):
                    norm_pe(pe, space, t)

        def full_banks(bank0):
            return [(ps[:, bank0 + j, :], j * P, P) for j in range(4)]

        def lap_done(lap):
            return (lap + 1) * SLOTS

        def add_half(dve, half, bank0):
            for t in range(T):
                r = resid[:, t, half * WIDE:(half + 1) * WIDE]
                dve.tensor_tensor(r, ps[:, bank0 + t, :], r, ALU.add).then_inc(added, 1)

        def transpose_pe(pe, src, t):
            for half in range(2):
                for j in range(4):
                    c = (4 * half + j) * P
                    mm = pe.transpose(ps[:, 4 * half + t, j * P:(j + 1) * P], src[:, t, c:c + P], ident[:])
                mm.then_inc(xp_done, 1)

        def bank_as_tiles(b):
            return ps[:, b, :].rearrange("p (k q) -> p k q", k=4)

        def transpose_act(act, base, t):
            for half in range(2):
                act.wait_ge(xp_done, base + 2 * t + half + 1)
                act.activation(xT_hi[:, 4 * half:4 * half + 4, t * P:(t + 1) * P], bank_as_tiles(4 * half + t),
                               ACT.Copy).then_inc(xp_hi, 1)

        def transpose_dve(dve, base, t):
            for half in range(2):
                ap = (slice(None), slice(4 * half, 4 * half + 4), slice(t * P, (t + 1) * P))
                dve.wait_ge(xp_hi, base + 2 * t + half + 1)
                dve.tensor_tensor(xT_lo[ap], bank_as_tiles(4 * half + t), xT_hi[ap].bitcast(F32),
                                  ALU.subtract).then_inc(xp_lo, 1)

        gb_landed, norm_var, norm_std, norm_scaled, norm_y = (sem("gb_landed"), sem("norm_var"), sem("norm_std"),
                                                              sem("norm_scaled"), sem("norm_y"))
        norm_last = sem("norm_last")
        token_done = sem("token_done")
        out_stored = sem("out_stored")
        n_norm = [0]
        HEAD_KS, TAIL_KS = range(0, 1), range(1, SLOTS)

        def norm_space(scope, g_row, b_row, g_all=None, b_all=None):
            i = n_norm[0]
            n_norm[0] += 1
            g_all = sbuf(scope, f"ln_g{i}", [P, D]) if g_all is None else g_all
            b_all = sbuf(scope, f"ln_b{i}", [P, D]) if b_all is None else b_all
            return (i, g_row, b_row, g_all, b_all, sbuf(scope, f"ln_stat{i}", [P, T, 2, 6]),
                    sbuf(scope, f"ln_mv{i}", [P, T, 2]), sbuf(scope, f"ln_rstd{i}", [P, T]))

        def norm_load(sp, space):
            i, g_row, b_row, g_all, b_all = space[:5]
            sp.dma_start(g_all[:], g_row.broadcast_to([P, D])).then_inc(gb_landed, 16)
            sp.dma_start(b_all[:], b_row.broadcast_to([P, D])).then_inc(gb_landed, 16)

        def wait_norm(eng, space, t):
            if t < T - 1:
                eng.wait_ge(norm_y, space[0] * (T - 1) + t + 1)
            else:
                eng.wait_ge(norm_last, space[0] + 1)

        def norm_store(sp, space):
            for t in range(T):
                wait_norm(sp, space, t)
                sp.dma_start(out[0, t * P:(t + 1) * P, :], resid[:, t, :]).then_inc(out_stored, 16)
            sp.wait_ge(out_stored, 16 * T)

        def norm_dve(dve, space, lap, adds, final=False):
            i, _, _, g_all, b_all, stat, mv, rstd = space
            step = stepper(dve, "dve", dve_step)
            done, base = i * T, n_xp[0]

            def statistics(t):
                if t < T - 1:
                    dve.wait_ge(token_done, i * (T - 1) + t + 1)
                else:
                    dve.wait_ge(w_used, lap_done(lap))
                for half, bank0 in adds:
                    r = resid[:, t, half * WIDE:(half + 1) * WIDE]
                    dve.tensor_tensor(r, ps[:, bank0 + t, :], r, ALU.add).then_inc(added, 1)
                    n_added[0] += 1
                dve.wait_ge(added, n_added[0])
                dve.bn_stats(stat[:, t, 0, :], resid[:, t, 0:WIDE])
                step(dve.bn_stats(stat[:, t, 1, :], resid[:, t, WIDE:]))
                dve.bn_aggr(mv[:, t, :], stat[:, t, :, :].rearrange("p a b -> p (a b)")).then_inc(norm_var, 1)

            def scale(t):
                dve.wait_ge(norm_var, done + t + 1)
                dve.wait_ge(norm_std, done + t + 1)
                step(dve.reciprocal(rstd[:, t:t + 1], rstd[:, t:t + 1]))
                ins = dve.tensor_scalar(resid[:, t, :], resid[:, t, :], mv[:, t, 0:1], rstd[:, t:t + 1],
                                        ALU.subtract, ALU.mult)
                if t < T - 1:
                    ins.then_inc(norm_scaled, 1)
                else:
                    step(ins)
                    dve.wait_ge(gb_landed, 32 * (i + 1))
                    step(dve.tensor_tensor(resid[:, t, :], resid[:, t, :], g_all[:], ALU.mult))
                    dve.tensor_tensor(resid[:, t, :], resid[:, t, :], b_all[:], ALU.add).then_inc(norm_last, 1)

            for t in range(T):
                if t == T - 1 and not final:
                    transpose_dve(dve, base, 0)
                statistics(t)
                scale(t)
            if not final:
                transpose_dve(dve, base, 1)
                transpose_dve(dve, base, 2)
                split_lap(dve, lap + 1, HEAD_KS)
                transpose_dve(dve, base, 3)

        def norm_pool(pool, space):
            i, _, _, g_all, b_all = space[:5]
            step = stepper(pool, "pool", pool_step)
            pool.wait_ge(gb_landed, 32 * (i + 1))
            for t in range(T - 1):
                pool.wait_ge(norm_scaled, i * (T - 1) + t + 1)
                step(pool.tensor_tensor(resid[:, t, :], resid[:, t, :], g_all[:], ALU.mult))
                pool.tensor_tensor(resid[:, t, :], resid[:, t, :], b_all[:], ALU.add).then_inc(norm_y, 1)

        def norm_act(act, space, lap, final=False):
            i, mv, rstd = space[0], space[6], space[7]

            def root(t):
                act.wait_ge(norm_var, i * T + t + 1)
                act.activation(rstd[:, t:t + 1], mv[:, t, 1:2], ACT.Sqrt, bias=eps[:, 0:1]).then_inc(norm_std, 1)

            def turned(t):
                if not final:
                    transpose_act(act, n_xp[0], t)
                    act.mul(resid[:, t, :], resid[:, t, :], ALPHA)

            for t in range(T):
                root(t)
                if t >= 2:
                    turned(t - 2)
            turned(T - 2)
            if not final:
                round_lap(act, lap + 1, HEAD_KS)
            turned(T - 1)

        def norm_pe(pe, space, t):
            wait_norm(pe, space, t)
            transpose_pe(pe, resid, t)

        even = ExitStack()
        level_mask = sbuf(even, "level_mask", [P, 8, P])
        tri_tau = sbuf(even, "tri_tau", [P, P])
        g_w2_all = sbuf(even, "g_w2", [96 + G_RANK, WIDE])
        g_w2 = g_w2_all[96:96 + G_RANK, :]
        g_b2 = sbuf(even, "g_b2", [97, WIDE])[96:97, :]
        x_landed, params = sem("x_landed"), sem("params")
        with nc.Block() as block:
            @block.sync
            def _(sp):
                for t in range(T):
                    sp.dma_start(resid[:, t, :], x[0, t * P:(t + 1) * P, :]).then_inc(x_landed, 16)
                load_lap(sp, 0)

            @block.gpsimd
            def _(pool):
                step = stepper(pool, "pool", pool_step)
                step(pool.memset(ident[:], 0.0))
                pool.affine_select(out=ident[:], in_=ident[:], compare_op=ALU.not_equal, fill=1.0, base=0,
                                   pattern=[[-1, P]], channel_multiplier=1).then_inc(consts, 1)
                pool.memset(eps[:], LN_EPS)
                pool.memset(ones[:], 1.0)
                step(pool.memset(tri_tau[:], 1.0 / G_TAU))
                step(pool.affine_select(out=tri_tau[:], in_=tri_tau[:], compare_op=ALU.is_ge, fill=0.0, base=0,
                                        pattern=[[1, P]], channel_multiplier=-1))
                step(pool.memset(level_mask[:], 0.0))
                for lev in range(7):
                    half = 64 >> lev
                    nb = P // (2 * half)
                    v = level_mask[:, lev, :].rearrange("p (b j) -> p b j", b=nb)[:, :, half:2 * half]
                    step(pool.memset(v, 1.0))
                    step(pool.affine_select(out=v, in_=v, compare_op=ALU.is_ge, fill=0.0, base=0,
                                            pattern=[[-2 * half, nb], [0, half]], channel_multiplier=1))
                    step(pool.affine_select(out=v, in_=v, compare_op=ALU.is_ge, fill=0.0, base=half - 1,
                                            pattern=[[2 * half, nb], [0, half]], channel_multiplier=-1))
                step(pool.affine_select(out=level_mask[:, 7, :], in_=level_mask[:, 7, :], compare_op=ALU.not_equal,
                                        fill=1.0, base=0, pattern=[[-1, P]], channel_multiplier=1))

            @block.tensor
            def _(pe):
                pe.wait_ge(consts, 1)
                pe.wait_ge(x_landed, 16 * T)
                for t in range(T):
                    transpose_pe(pe, resid, t)

            @block.scalar
            def _(act):
                act.dma_start(g_w2, ev_g_w2[0]).then_inc(params, 16)
                act.dma_start(g_b2, ev_g_b2[0:1, :]).then_inc(params, 16)
                for t in range(T):
                    transpose_act(act, 0, t)
                    act.mul(resid[:, t, :], resid[:, t, :], ALPHA)
                round_lap(act, 0)

            @block.vector
            def _(dve):
                for t in range(T):
                    transpose_dve(dve, 0, t)
                split_lap(dve, 0)
        n_xp[0] = 8

        gla_in = ExitStack()
        gqT = sbuf(gla_in, "gqT", [P, G_HEADS, S])
        gkT = sbuf(gla_in, "gkT", [P, G_HEADS, S])
        gv = sbuf(gla_in, "gv", [P, T, WIDE])
        gr = sbuf(gla_in, "gr", [P, T, WIDE])
        misc = sbuf(gla_in, "misc", [96 + G_RANK, S])
        iwT, lrT = misc[64:72, :], misc[96:96 + G_RANK, :]
        cat = sbuf(gla_in, "cat", [P, T, D])
        dsa_in = ExitStack()
        aqT = sbuf(dsa_in, "aqT", [P, 4, S])
        akT = sbuf(dsa_in, "akT", [P, S])
        av = sbuf(dsa_in, "av", [P, T, A_DIM])
        key_mask = sbuf(dsa_in, "key_mask", [P, T, S])
        idx = ExitStack()
        iqT = sbuf(idx, "iqT", [P, 4, S])
        ikT = sbuf(idx, "ikT", [P, S])
        iw = sbuf(idx, "iw", [P, T, 8])
        avT_all = sbuf(idx, "avT", [P, S])
        avT = avT_all[64:P, :]
        relu_buf = sbuf(idx, "relu_buf", [P, 4, S])
        score = sbuf(idx, "score", [P, 3, S])
        left = sbuf(idx, "left", [P, S])
        best8 = sbuf(idx, "best8", [P, 8])

        proj_out = sem("proj_out")
        small_turned = sem("small_turned")
        keys_doubled = sem("keys_doubled")
        logits_done, relu_done, score_added = sem("logits_done"), sem("relu_done"), sem("score_added")
        causal_done, chosen, mask_ready = sem("causal_done"), sem("chosen"), sem("mask_ready")
        ITEMS = [(b, h) for b in range(1, T) for h in range(A_HEADS)]
        O_IQ, O_SMALL, O_TURNED, O_AQ, O_GQ, O_GK, O_GV, O_GR = 4, 8, 10, 14, 18, 22, 26, 30

        with nc.Block() as block:
            @block.sync
            def _(sp):
                for lap in range(L_IQ + 1, L_GR + 3):
                    load_lap(sp, lap)

            @block.tensor
            def _(pe):
                pe.wait_ge(xp_lo, n_xp[0])
                lap_T(pe, L_IQ, full_banks(0))
                lap_T(pe, L_SMALL, [(ps[:, 4, :], 0, P), (ps[0:96 + G_RANK, 5, :], P, 96 + G_RANK)])
                pe.wait_ge(proj_out, O_IQ)
                lap_T(pe, L_AQ, full_banks(0))
                pe.wait_ge(proj_out, O_SMALL)
                for t in range(T):
                    pe.transpose(ps[:, 6, 8 * t:8 * t + 8], iwT[:, t * P:(t + 1) * P], ident[64:72, 64:72])
                for t in range(T):
                    mm = pe.transpose(ps[:, 6, 64 + 64 * t:128 + 64 * t], avT[:, t * P:(t + 1) * P],
                                      ident[64:P, 64:P])
                mm.then_inc(small_turned, 1)
                pe.wait_ge(keys_doubled, 32)
                pe.wait_ge(proj_out, O_TURNED)
                for u, (b, h) in enumerate(ITEMS):
                    if u >= 4:
                        pe.wait_ge(relu_done, u - 3)
                    r = slice(64 * (h % 2), 64 * (h % 2) + 64)
                    pe.matmul(ps[:, 4 + u % 4, 0:(b + 1) * P], iqT[r, h // 2, b * P:(b + 1) * P],
                              ikT[r, 0:(b + 1) * P], start=True, stop=True).then_inc(logits_done, 1)
                pe.wait_ge(proj_out, O_AQ)
                lap_T(pe, L_GQ, full_banks(0))
                pe.wait_ge(relu_done, len(ITEMS))
                lap_T(pe, L_GK, full_banks(4))
                pe.wait_ge(proj_out, O_GQ)
                lap_N(pe, L_GV, 0)
                pe.wait_ge(proj_out, O_GK)
                lap_N(pe, L_GR, 4)

            @block.scalar
            def _(act):
                def copy_out(dst, src, scale=1.0):
                    act.activation(dst, src, ACT.Copy, scale=scale).then_inc(proj_out, 1)

                def copy_banks(dst, bank0, scale=1.0):
                    for j in range(4):
                        copy_out(dst[:, j, :], ps[:, bank0 + j, :], scale)

                round_lap(act, L_SMALL)
                act.wait_ge(w_used, lap_done(L_IQ))
                copy_banks(iqT, 0)
                round_lap(act, L_AQ)
                act.wait_ge(w_used, lap_done(L_SMALL))
                copy_out(akT[0:64, :], ps[0:64, 4, :])
                copy_out(avT, ps[64:P, 4, :])
                copy_out(ikT[0:64, :], ps[0:64, 5, :])
                copy_out(misc[64:, :], ps[64:96 + G_RANK, 5, :])
                act.wait_ge(proj_out, O_SMALL)
                act.dma_start(ikT[64:128, :], ikT[0:64, :]).then_inc(keys_doubled, 16)
                act.dma_start(akT[64:128, :], akT[0:64, :]).then_inc(keys_doubled, 16)
                round_lap(act, L_GQ)
                act.wait_ge(small_turned, 1)
                copy_out(iw[:].rearrange("p t h -> p (t h)"), ps[:, 6, 0:8 * T], A_HEADS ** -0.5)
                copy_out(av[:].rearrange("p t d -> p (t d)"), ps[:, 6, 64:64 + 64 * T])
                act.wait_ge(w_used, lap_done(L_AQ))
                copy_banks(aqT, 0)
                for u, (b, h) in enumerate(ITEMS):
                    act.wait_ge(logits_done, u + 1)
                    if u >= 4:
                        act.wait_ge(score_added, u - 3)
                    act.activation(relu_buf[:, u % 4, 0:(b + 1) * P], ps[:, 4 + u % 4, 0:(b + 1) * P], ACT.Relu,
                                   scale=A_DIM ** -0.5).then_inc(relu_done, 1)
                round_lap(act, L_GK)
                act.wait_ge(w_used, lap_done(L_GQ))
                copy_banks(gqT, 0, G_DIM ** -0.5)
                round_lap(act, L_GV)
                act.wait_ge(w_used, lap_done(L_GK))
                copy_banks(gkT, 4)
                round_lap(act, L_GR)
                act.wait_ge(w_used, lap_done(L_GV))
                copy_banks(gv, 0)
                round_lap(act, L_WO)
                act.wait_ge(w_used, lap_done(L_GR))
                for t in range(T):
                    act.activation(gr[:, t, :], ps[:, 4 + t, :], ACT.Silu).then_inc(proj_out, 1)

            @block.vector
            def _(dve):
                step = stepper(dve, "dve", dve_step)
                split_lap(dve, L_SMALL)
                split_lap(dve, L_AQ)
                split_lap(dve, L_GQ)
                dve.wait_ge(proj_out, O_TURNED)
                for u, (b, h) in enumerate(ITEMS):
                    n = (b + 1) * P
                    dve.wait_ge(relu_done, u + 1)
                    if h == 0:
                        ins = dve.tensor_scalar(score[:, b - 1, 0:n], relu_buf[:, u % 4, 0:n], iw[:, b, 0:1], None,
                                                ALU.mult)
                    else:
                        dve.wait_ge(score_added, u)
                        ins = dve.scalar_tensor_tensor(out=score[:, b - 1, 0:n], in0=relu_buf[:, u % 4, 0:n],
                                                       scalar=iw[:, b, h:h + 1], in1=score[:, b - 1, 0:n],
                                                       op0=ALU.mult, op1=ALU.add)
                    ins.then_inc(score_added, 1)
                tiles = [(lap, k) for lap in range(L_GK, L_WO + 1) for k in range(SLOTS)]
                for b in range(1, T):
                    n = (b + 1) * P
                    dve.wait_ge(causal_done, b)
                    for r in range(TOPK // 8):
                        src = score[:, b - 1, 0:n] if r == 0 else left[:, 0:n]
                        step(dve.max(best8[:], src))
                        step(dve.match_replace(out=left[:, 0:n], in_to_replace=best8[:], in_values=src, imm_value=NEG))
                        if tiles and r % 5 != 0:
                            split_tile(dve, *tiles.pop(0))
                    dve.tensor_scalar(key_mask[:, b, 0:n], left[:, 0:n], NEG / 3, MASKED, ALU.is_gt,
                                      ALU.mult).then_inc(chosen, 1)
                for lap, k in tiles:
                    split_tile(dve, lap, k)

            @block.gpsimd
            def _(pool):
                step = stepper(pool, "pool", pool_step)

                def causal(ap, fill):
                    return pool.affine_select(out=ap, in_=ap, compare_op=ALU.is_ge, fill=fill, base=0,
                                              pattern=[[-1, P]], channel_multiplier=1)

                step(pool.memset(key_mask[:, 0, 0:P], 0.0))
                causal(key_mask[:, 0, 0:P], MASKED).then_inc(mask_ready, 1)
                for b in range(1, T):
                    pool.wait_ge(score_added, b * A_HEADS)
                    causal(score[:, b - 1, b * P:(b + 1) * P], NEG).then_inc(causal_done, 1)
                for b in range(1, T):
                    pool.wait_ge(chosen, b)
                    causal(key_mask[:, b, b * P:(b + 1) * P], MASKED).then_inc(mask_ready, 1)
        idx.close()

        mix = ExitStack()
        s_neg = sbuf(mix, "s_neg", [P, 2, S])
        prob = sbuf(mix, "prob", [P, 2, S])
        probT = sbuf(mix, "probT", [P, 2, S])
        min_neg = sbuf(mix, "min_neg", [P, T * A_HEADS])
        row_sum = sbuf(mix, "row_sum", [P, T * A_HEADS])
        row_inv = sbuf(mix, "row_inv", [P, T * A_HEADS])
        loga = x_space[:, 0:4, :]
        bcum = x_space[:, 4:8, :]
        ebcum = x_space[:, 8:12, :]
        diff = x_space[:, 12:14, :]
        expd = diff
        q_lev = x_space[:, 14:16, :]
        k_lev = sbuf(mix, "k_lev", [P, 2, S])
        k_end = k_lev[:, (8 - 1) % 2, :]
        k_endT = sbuf(mix, "k_endT", [P, 3 * P])
        attT = sbuf(mix, "attT", [P, 2, S])
        state = sbuf(mix, "state", [P, 2, 3, G_DIM])
        g_norm = sbuf(mix, "g_norm", [P, WIDE])
        g_stat = sbuf(mix, "g_stat", [P, T, 6])
        g_mv = sbuf(mix, "g_mv", [P, T, G_HEADS, 2])
        g_std = sbuf(mix, "g_std", [P, T, G_HEADS])
        s_done, s_masked, exp_done = sem("s_done"), sem("s_masked"), sem("exp_done")
        pt_done, pt_out, pv_done, o_out = sem("pt_done"), sem("pt_out"), sem("pv_done"), sem("o_out")
        gate_mm, ln_done, loga_done = sem("gate_mm"), sem("ln_done"), sem("loga_done")
        cum_done, b_ready, eb_ready, qe_ready = sem("cum_done"), sem("b_ready"), sem("eb_ready"), sem("qe_ready")
        diff_ready, expd_ready, lev_ready = sem("diff_ready"), sem("expd_ready"), sem("lev_ready")
        lev_mm, lev_kept = sem("lev_mm"), sem("lev_kept")
        kend_turned, kend_out = sem("kend_turned"), sem("kend_out")
        su_mm, s_ready, o_mm = sem("su_mm"), sem("s_ready"), sem("o_mm")
        zeroed, sg_ready, o_gated, var_ready, std_ready = (sem("zeroed"), sem("sg_ready"), sem("o_gated"),
                                                           sem("var_ready"), sem("std_ready"))
        g_norm_landed = sem("g_norm_landed")
        QH = [(b, h) for b in range(T) for h in range(A_HEADS)]
        LEV = 8
        N_LEV = G_HEADS * LEV
        FIRST = 5
        CUM, EXP_B, Q_EXP = 2, 3, 4
        STEPS = range(N_LEV + FIRST + 5)

        def level_at(step, ahead=0):
            n = step - FIRST + ahead
            return n if 0 <= n < N_LEV else None

        def head_after(step, steps):
            h, lev = divmod(step - FIRST - steps, LEV)
            return h if lev == LEV - 1 and 0 <= h < G_HEADS else None

        def blocks_of(ap, half):
            return ap.rearrange("p (b j) -> p b j", j=2 * half)

        with nc.Block() as block:
            @block.sync
            def _(sp):
                sp.dma_start(g_norm[:], ev_g_norm[0:1].rearrange("o h d -> o (h d)").broadcast_to([P, WIDE])
                             ).then_inc(g_norm_landed, 16)

            @block.tensor
            def _(pe):
                def scores(i):
                    b, h = QH[i]
                    r = slice(64 * (h % 2), 64 * (h % 2) + 64)
                    if i >= 2:
                        pe.wait_ge(s_masked, i - 1)
                    pe.matmul(ps[:, i % 2, 0:(b + 1) * P], aqT[r, h // 2, b * P:(b + 1) * P], akT[r, 0:(b + 1) * P],
                              start=True, stop=True).then_inc(s_done, 1)

                def turn(i):
                    b, h = QH[i]
                    pe.wait_ge(exp_done, i + 1)
                    if i >= 1:
                        pe.wait_ge(pt_out, i)
                    for kt in range(b + 1):
                        mm = pe.transpose(ps[:, 2, kt * P:(kt + 1) * P], prob[:, i % 2, kt * P:(kt + 1) * P], ident[:])
                    mm.then_inc(pt_done, 1)

                def values(i):
                    b, h = QH[i]
                    pe.wait_ge(pt_out, i + 1)
                    if b >= 1 and h == 0:
                        pe.wait_ge(o_out, b)
                    for kt in range(b + 1):
                        mm = pe.matmul(ps[:, 3, h * A_DIM:(h + 1) * A_DIM], probT[:, i % 2, kt * P:(kt + 1) * P],
                                       av[:, kt, :], start=(kt == 0), stop=(kt == b))
                    mm.then_inc(pv_done, 1)

                def level(n):
                    h, lev = divmod(n, LEV)
                    pe.wait_ge(lev_ready, n + 1)
                    if n == 0:
                        pe.wait_ge(b_ready, G_HEADS)
                    if n >= 2:
                        pe.wait_ge(lev_kept, n - 1)
                    for c in range(T):
                        cs = slice(c * P, (c + 1) * P)
                        kk, qq = (k_lev[:, n % 2, cs], q_lev[:, n % 2, cs]) if lev < 7 else (gkT[:, h, cs], gqT[:, h, cs])
                        mm = pe.matmul(ps[:, 4 + n % 2, cs], kk, qq, start=True, stop=True)
                    mm.then_inc(lev_mm, 1)

                def turn_keys(h):
                    if h >= 1:
                        pe.wait_ge(s_ready, 3 * h)
                    for c in range(T - 1):
                        mm = pe.transpose(ps[:, 6, c * P:(c + 1) * P], k_end[:, c * P:(c + 1) * P], ident[:])
                    mm.then_inc(kend_turned, 1)

                def contributions(h):
                    pe.wait_ge(kend_out, h + 1)
                    for c in range(T - 1):
                        cs, hs = slice(c * P, (c + 1) * P), slice(h * P, (h + 1) * P)
                        mm = pe.matmul(ps[:, 6, cs], k_endT[:, cs], gv[:, c, hs], start=True, stop=True)
                    mm.then_inc(su_mm, 1)

                def outputs(h):
                    pe.wait_ge(lev_kept, (h + 1) * LEV)
                    pe.wait_ge(s_ready, 3 * (h + 1))
                    pe.wait_ge(qe_ready, G_HEADS)
                    if h >= 1:
                        pe.wait_ge(o_gated, T * h)
                    for c in range(T):
                        cs, hs = slice(c * P, (c + 1) * P), slice(h * P, (h + 1) * P)
                        mm = pe.matmul(ps[:, 7, cs], attT[:, h % 2, cs], gv[:, c, hs], start=True, stop=(c == 0))
                        if c >= 1:
                            mm = pe.matmul(ps[:, 7, cs], loga[:, h, cs], state[:, h % 2, c - 1, :], start=False,
                                           stop=True)
                    mm.then_inc(o_mm, 1)

                pe.wait_ge(params, 32)
                for c in range(T):
                    pe.matmul(ps[:, 4 + c, :], lrT[:, c * P:(c + 1) * P], g_w2, start=True, stop=False)
                    pe.matmul(ps[:, 4 + c, :], ones[96:97, :], g_b2, start=False, stop=True).then_inc(gate_mm, 1)
                for i in STEPS:
                    if i < len(QH):
                        scores(i)
                    if 1 <= i <= len(QH):
                        turn(i - 1)
                    if 2 <= i <= len(QH) + 1:
                        values(i - 2)
                    if i == CUM:
                        pe.wait_ge(loga_done, T)
                        for h in range(G_HEADS):
                            for c in range(T):
                                mm = pe.matmul(ps[:, 4 + h, c * P:(c + 1) * P], loga[:, c, h * P:(h + 1) * P],
                                               tri_tau[:], start=True, stop=True)
                            mm.then_inc(cum_done, 1)
                    if head_after(i, 1) is not None:
                        turn_keys(head_after(i, 1))
                    if head_after(i, 2) is not None:
                        contributions(head_after(i, 2))
                    if head_after(i, 3) is not None:
                        outputs(head_after(i, 3))
                    if level_at(i) is not None:
                        level(level_at(i))

            @block.scalar
            def _(act):
                step = stepper(act, "act", act_step)

                def exponential(i):
                    b, h = QH[i]
                    n = (b + 1) * P
                    act.wait_ge(s_masked, i + 1)
                    if i >= 2:
                        act.wait_ge(pt_done, i - 1)
                    act.activation(prob[:, i % 2, 0:n], s_neg[:, i % 2, 0:n], ACT.Exp, scale=-1.0,
                                   bias=min_neg[:, i:i + 1], accum_out=row_sum[:, i:i + 1]).then_inc(exp_done, 1)

                def copy_pt(i):
                    n = (QH[i][0] + 1) * P
                    act.wait_ge(pt_done, i + 1)
                    if i >= 2:
                        act.wait_ge(pv_done, i - 1)
                    act.activation(probT[:, i % 2, 0:n], ps[:, 2, 0:n], ACT.Copy).then_inc(pt_out, 1)

                def exp_level(n):
                    lev = n % LEV
                    act.wait_ge(diff_ready, n + 1)
                    if lev < 7:
                        half = 64 >> lev
                        d, e = blocks_of(diff[:, n % 2, :], half), blocks_of(expd[:, n % 2, :], half)
                        act.activation(e[:, :, half:], d[:, :, half:], ACT.Exp)
                        act.activation(e[:, :, :half], d[:, :, :half], ACT.Exp, scale=-1.0).then_inc(expd_ready, 1)
                    else:
                        act.activation(expd[:, n % 2, :], diff[:, n % 2, :], ACT.Exp, scale=-1.0).then_inc(expd_ready, 1)

                def copy_keys(h):
                    act.wait_ge(kend_turned, h + 1)
                    if h >= 1:
                        act.wait_ge(su_mm, h)
                    act.activation(k_endT[:], ps[:, 6, 0:3 * P], ACT.Copy).then_inc(kend_out, 1)

                for c in range(T):
                    act.wait_ge(gate_mm, c + 1)
                    ins = act.activation(loga[:, c, :], ps[:, 4 + c, :], ACT.Abs)
                step(ins)
                step(act.activation(loga, loga, ACT.Exp, scale=-1.0))
                act.activation(loga, loga, ACT.Ln, bias=1.0).then_inc(ln_done, 1)
                for i in STEPS:
                    if i < len(QH):
                        exponential(i)
                    if 1 <= i <= len(QH):
                        copy_pt(i - 1)
                    if i == CUM:
                        for h in range(G_HEADS):
                            act.wait_ge(cum_done, h + 1)
                            act.activation(bcum[:, h, :], ps[:, 4 + h, :], ACT.Copy).then_inc(b_ready, 1)
                    if i == EXP_B:
                        act.wait_ge(b_ready, G_HEADS)
                        act.activation(ebcum, bcum, ACT.Exp).then_inc(eb_ready, 1)
                    if level_at(i, 1) is not None:
                        exp_level(level_at(i, 1))
                    if head_after(i, 1) is not None:
                        copy_keys(head_after(i, 1))
                act.wait_ge(var_ready, G_HEADS)
                act.activation(g_std[:], g_mv[:, :, :, 1], ACT.Sqrt, bias=eps[:, 0:1]).then_inc(std_ready, 1)

            @block.gpsimd
            def _(pool):
                pool.memset(q_lev, 0.0).then_inc(zeroed, 1)
                pool.memset(k_lev[:], 0.0).then_inc(zeroed, 1)
                pool.wait_ge(g_norm_landed, 16)
                for c in range(T):
                    pool.tensor_tensor(gr[:, c, :], gr[:, c, :], g_norm[:], ALU.mult).then_inc(sg_ready, 1)
                pool.wait_ge(zeroed, 2)
                for n in range(N_LEV):
                    h, lev = divmod(n, LEV)
                    pool.wait_ge(expd_ready, n + 1)
                    if n >= 2:
                        pool.wait_ge(lev_mm, n - 1)
                    if lev == 1 and h >= 1:
                        pool.wait_ge(kend_turned, h)
                    if lev < 7:
                        half = 64 >> lev
                        e = blocks_of(expd[:, n % 2, :], half)
                        pool.tensor_tensor(blocks_of(q_lev[:, n % 2, :], half)[:, :, half:],
                                           blocks_of(gqT[:, h, :], half)[:, :, half:], e[:, :, half:], ALU.mult)
                        pool.tensor_tensor(blocks_of(k_lev[:, n % 2, :], half)[:, :, :half],
                                           blocks_of(gkT[:, h, :], half)[:, :, :half], e[:, :, :half],
                                           ALU.mult).then_inc(lev_ready, 1)
                    else:
                        pool.tensor_tensor(k_end, gkT[:, h, :], expd[:, n % 2, :], ALU.mult).then_inc(lev_ready, 1)

            @block.vector
            def _(dve):
                step = stepper(dve, "dve", dve_step)

                def mask(i):
                    b, h = QH[i]
                    n = (b + 1) * P
                    dve.wait_ge(s_done, i + 1)
                    if i >= 2:
                        dve.wait_ge(exp_done, i - 1)
                    dve.tensor_tensor_reduce(out=s_neg[:, i % 2, 0:n], in0=ps[:, i % 2, 0:n], in1=key_mask[:, b, 0:n],
                                             scale=-A_DIM ** -0.5, scalar=3.0e38, op0=ALU.add, op1=ALU.min,
                                             accum_out=min_neg[:, i:i + 1]).then_inc(s_masked, 1)

                def normalise(b):
                    dve.wait_ge(pv_done, (b + 1) * A_HEADS)
                    hs = slice(b * A_HEADS, (b + 1) * A_HEADS)
                    step(dve.reciprocal(row_inv[:, hs], row_sum[:, hs]))
                    dve.tensor_tensor(cat[:, b, 0:A_HEADS * A_DIM].rearrange("p (h d) -> p h d", h=A_HEADS),
                                      ps[:, 3, :].rearrange("p (h d) -> p h d", h=A_HEADS),
                                      row_inv[:, hs].unsqueeze(2).broadcast_to([P, A_HEADS, A_DIM]),
                                      ALU.mult).then_inc(o_out, 1)

                def make_diff(n):
                    h, lev = divmod(n, LEV)
                    dve.wait_ge(b_ready, h + 1)
                    if n >= 2:
                        dve.wait_ge(lev_ready, n - 1)
                    half, ref = (64 >> lev, (64 >> lev) - 1) if lev < 7 else (64, 127)
                    b = blocks_of(bcum[:, h, :], half)
                    dve.tensor_tensor(blocks_of(diff[:, n % 2, :], half), b,
                                      b[:, :, ref:ref + 1].broadcast_to([P, S // (2 * half), 2 * half]),
                                      ALU.subtract).then_inc(diff_ready, 1)

                def keep(n):
                    h, lev = divmod(n, LEV)
                    dve.wait_ge(lev_mm, n + 1)
                    if lev == 0 and h >= 2:
                        dve.wait_ge(o_mm, h - 1)
                    if n >= 1:
                        dve.wait_ge(lev_kept, n)
                    dve.copy_predicated(attT[:, h % 2, :].rearrange("p (c t) -> p c t", c=T),
                                        level_mask[:, lev, :].bitcast(U32).unsqueeze(1).broadcast_to([P, T, P]),
                                        ps[:, 4 + n % 2, :].rearrange("p (c t) -> p c t", c=T)).then_inc(lev_kept, 1)

                def states(h):
                    dve.wait_ge(su_mm, h + 1)
                    dve.wait_ge(eb_ready, 1)
                    if h >= 2:
                        dve.wait_ge(o_mm, h - 1)
                    for c in range(T - 1):
                        if c == 0:
                            ins = dve.tensor_copy(state[:, h % 2, 0, :], ps[:, 6, 0:P])
                        else:
                            dve.wait_ge(s_ready, h * 3 + c)
                            ins = dve.scalar_tensor_tensor(out=state[:, h % 2, c, :], in0=state[:, h % 2, c - 1, :],
                                                           scalar=ebcum[:, h, (c + 1) * P - 1:(c + 1) * P],
                                                           in1=ps[:, 6, c * P:(c + 1) * P], op0=ALU.mult, op1=ALU.add)
                        ins.then_inc(s_ready, 1)

                def norm_head(h):
                    dve.wait_ge(o_mm, h + 1)
                    for c in range(T):
                        ins = dve.bn_stats(g_stat[:, c, :], ps[:, 7, c * P:(c + 1) * P])
                    step(ins)
                    for c in range(T):
                        ins = dve.bn_aggr(g_mv[:, c, h, :], g_stat[:, c, :])
                    ins.then_inc(var_ready, 1)
                    dve.wait_ge(var_ready, h + 1)
                    dve.wait_ge(sg_ready, T)
                    for c in range(T):
                        hs = slice(h * P, (h + 1) * P)
                        dve.scalar_tensor_tensor(out=cat[:, c, WIDE + h * P:WIDE + (h + 1) * P],
                                                 in0=ps[:, 7, c * P:(c + 1) * P], scalar=g_mv[:, c, h, 0:1],
                                                 in1=gr[:, c, hs], op0=ALU.subtract, op1=ALU.mult).then_inc(o_gated, 1)

                step(dve.memset(attT[:], 0.0))
                dve.wait_ge(ln_done, 1)
                for c in range(T):
                    dve.scalar_tensor_tensor(out=loga[:, c, :], in0=ps[:, 4 + c, :], scalar=0.0, in1=loga[:, c, :],
                                             op0=ALU.min, op1=ALU.subtract).then_inc(loga_done, 1)
                for i in STEPS:
                    if i < len(QH):
                        mask(i)
                    if level_at(i, 2) is not None:
                        make_diff(level_at(i, 2))
                    if i == Q_EXP:
                        dve.wait_ge(cum_done, G_HEADS)
                        dve.wait_ge(eb_ready, 1)
                        dve.tensor_tensor(loga, gqT[:], ebcum, ALU.mult).then_inc(qe_ready, G_HEADS)
                    if level_at(i) is not None:
                        keep(level_at(i))
                    if i % A_HEADS == 1 and 1 <= i // A_HEADS <= T:
                        normalise(i // A_HEADS - 1)
                    if head_after(i, 2) is not None:
                        states(head_after(i, 2))
                    if head_after(i, 4) is not None:
                        norm_head(head_after(i, 4))
                dve.wait_ge(o_gated, T * G_HEADS)
                dve.wait_ge(std_ready, 1)
                step(dve.reciprocal(g_std[:], g_std[:]))
                for c in range(T):
                    o = cat[:, c, WIDE:].rearrange("p (h d) -> p h d", h=G_HEADS)
                    ins = dve.tensor_tensor(o, o, g_std[:, c, :].unsqueeze(2).broadcast_to([P, G_HEADS, G_DIM]), ALU.mult)
                step(ins)
        mix.close()
        dsa_in.close()

        base = n_xp[0]
        n_xp[0] += 8
        space = norm_space(gla_in, ln1_g[0:1], ln1_b[0:1])
        with nc.Block() as block:
            @block.sync
            def _(sp):
                norm_load(sp, space)
                load_lap(sp, L_MLP0)
                load_lap(sp, L_MLP0 + 1, HEAD_KS)

            @block.tensor
            def _(pe):
                for t in range(T):
                    transpose_pe(pe, cat, t)
                pe.wait_ge(xp_lo, base + 8)
                lap_N(pe, L_WO, 0)
                pe.wait_ge(xp_lo, base + 8)
                by_tokens(pe, L_WO + 1, [(range(SLOTS), lambda k: xT_hi[:, k, :], lambda k: xT_lo[:, k, :], 4)],
                          space)

            @block.scalar
            def _(act):
                for t in range(T):
                    transpose_act(act, base, t)
                round_lap(act, L_WO + 1)
                norm_act(act, space, L_WO + 1)

            @block.vector
            def _(dve):
                for t in range(T):
                    transpose_dve(dve, base, t)
                split_lap(dve, L_WO + 1)
                dve.wait_ge(w_used, lap_done(L_WO))
                add_half(dve, 0, 0)
                n_added[0] += T
                norm_dve(dve, space, L_WO + 1, [(1, 4)])

            @block.gpsimd
            def _(pool):
                norm_pool(pool, space)
        n_xp[0] += 8
        gla_in.close()
        even.close()

        h_relu, h_rounded, h_sq, h_ready = sem("h_relu"), sem("h_rounded"), sem("h_sq"), sem("h_ready")
        n_mlp = [0]

        def mlp_stage(layer, L0, final=False, with_pool=None):
            own = ExitStack()
            space = norm_space(own, ln2_g[layer:layer + 1], ln2_b[layer:layer + 1])
            m = n_mlp[0]
            r_buf = sbuf(own, f"r_buf{m}", [P, 4, S])
            h_hi = sbuf(own, f"h_hi{m}", [P, 2, 4, S], F32R)
            h_lo = sbuf(own, f"h_lo{m}", [P, 2, 4, S], F32R)
            HB = m * CH * 4
            AB = n_added[0]
            up = lambda c: L0 + 2 * c - 1
            down = lambda c: L0 + 2 * c + 2
            last = CH - 1
            DOWN_LAST = L0 + 2 * CH - 1
            assert CH % 2 == 0

            with nc.Block() as block:
                @block.sync
                def _(sp):
                    load_lap(sp, L0 + 1, TAIL_KS)
                    norm_load(sp, space)
                    with sp.Fori(0, CH - 2) as c:
                        for k in range(SLOTS):
                            load_tile(sp, down(c), k, row_lap(mlp_w2[layer], c * WIDE)(k))
                        for k in range(SLOTS):
                            load_tile(sp, up(c + 2), k, up_lap(layer, c + 2)(k))
                    for lap in (down(CH - 2), DOWN_LAST, DOWN_LAST + 1):
                        load_lap(sp, lap)
                    load_lap(sp, DOWN_LAST + 2, HEAD_KS)
                    if final:
                        norm_store(sp, space)

                @block.tensor
                def _(pe):
                    def up_chunk(c, lap, bank0):
                        for k in range(SLOTS):
                            pe.wait_ge(w_split, lap * SLOTS + k + 1)
                            tile_T(pe, k, xT_hi[:, k, :], xT_lo[:, k, :], full_banks(bank0), k == 0, k == SLOTS - 1)

                    def down_chunk(c, lap, par, bank_left, left_free, right_free):
                        pe.wait_ge(h_ready, HB + c * 4 + 4)
                        lap_rows(pe, lap, lambda kk: h_hi[:, par, kk, :], lambda kk: h_lo[:, par, kk, :],
                                 bank_left, 4 - bank_left, left_free, right_free)

                    def both(c, par, first=False):
                        if not first:
                            pe.wait_ge(added, AB + (c - 1) * 8 + 4)
                        up_chunk(c + 1, up(c + 1), 4 - 4 * par)
                        down_chunk(c, down(c), par, 4 * par,
                                   (lambda: None) if first else (lambda: pe.wait_ge(added, AB + c * 8)),
                                   lambda: pe.wait_ge(h_relu, HB + c * 4 + 8))

                    pe.wait_ge(xp_lo, n_xp[0])
                    up_chunk(0, L0, 0)
                    both(0, 0, first=True)
                    with pe.Fori(0, CH // 2 - 1) as i:
                        both(i * 2 + 1, 1)
                        both(i * 2 + 2, 0)
                    pe.wait_ge(h_ready, HB + last * 4 + 4)
                    pe.wait_ge(added, AB + last * 8)
                    h_parts = (lambda kk: h_hi[:, 1, kk, :], lambda kk: h_lo[:, 1, kk, :])
                    by_tokens(pe, DOWN_LAST, [(range(4), *h_parts, 0), (range(4, 8), *h_parts, 4)], space, final)

                @block.scalar
                def _(act):
                    def squares(c, lap, par, bank0, deep=True):
                        act.wait_ge(w_used, lap * SLOTS + SLOTS)
                        act.wait_ge(h_ready, HB + c * 4) if not isinstance(c, int) or HB + c else None
                        for j in range(4):
                            act.activation(r_buf[:, j, :], ps[:, bank0 + j, :], ACT.Relu).then_inc(h_relu, 1)
                        if deep:
                            act.wait_ge(w_used, (lap - 1) * SLOTS)
                        for j in range(4):
                            act.wait_ge(h_relu, HB + c * 4 + j + 1)
                            act.activation(h_hi[:, par, j, :], r_buf[:, j, :], ACT.Square).then_inc(h_rounded, 1)

                    def both(c, par):
                        round_lap(act, down(c))
                        squares(c + 1, up(c + 1), 1 - par, 4 - 4 * par)
                        round_lap(act, up(c + 2))

                    round_lap(act, L0, TAIL_KS)
                    round_lap(act, L0 + 1)
                    squares(0, L0, 0, 0, deep=False)
                    both(0, 0)
                    with act.Fori(0, CH // 2 - 1) as i:
                        both(i * 2 + 1, 1)
                        both(i * 2 + 2, 0)
                    norm_act(act, space, DOWN_LAST, final)

                @block.vector
                def _(dve):
                    def rest(c, par):
                        for j in range(4):
                            dve.wait_ge(h_rounded, HB + c * 4 + j + 1)
                            dve.tensor_tensor(r_buf[:, j, :], r_buf[:, j, :], r_buf[:, j, :], ALU.mult).then_inc(h_sq, 1)
                        for j in range(4):
                            dve.wait_ge(h_sq, HB + c * 4 + j + 1)
                            dve.tensor_tensor(h_lo[:, par, j, :], r_buf[:, j, :], h_hi[:, par, j, :].bitcast(F32),
                                              ALU.subtract).then_inc(h_ready, 1)

                    def add_down(half, lap, bank0):
                        dve.wait_ge(w_used, lap * SLOTS + 4 + 4 * half)
                        add_half(dve, half, bank0)

                    def both(c, par):
                        split_lap(dve, down(c))
                        rest(c + 1, 1 - par)
                        split_lap(dve, up(c + 2), range(4))
                        add_down(0, down(c), 4 * par)
                        split_lap(dve, up(c + 2), range(4, 8))
                        add_down(1, down(c), 4 - 4 * par)

                    split_lap(dve, L0, TAIL_KS)
                    split_lap(dve, L0 + 1)
                    rest(0, 0)
                    both(0, 0)
                    with dve.Fori(0, CH // 2 - 1) as i:
                        both(i * 2 + 1, 1)
                        both(i * 2 + 2, 0)
                    n_added[0] += 8 * last
                    norm_dve(dve, space, DOWN_LAST, [(0, 0), (1, 4)], final)

                @block.gpsimd
                def _(pool):
                    if with_pool:
                        with_pool(pool)
                    norm_pool(pool, space)
            own.close()
            n_mlp[0] += 1
            if not final:
                n_xp[0] += 8

        odd = ExitStack()
        NC = INNER // P
        OFF = [sum((T - j) * P for j in range(i)) for i in range(T)]
        wts = sbuf(odd, "wts", [P, OFF[-1] + P])
        hg = sbuf(odd, "hg", [P, T, DH])
        conv_w = sbuf(odd, "conv_w", [P, M_CONV, NC])
        conv_b = sbuf(odd, "conv_b", [P, NC])
        skip_c = sbuf(odd, "skip_c", [P, NC])
        norm_c = sbuf(odd, "norm_c", [P, NC])
        gate_b = sbuf(odd, "gate_b", [36, 1])
        N_BLK = NC * M_BLK
        blk = wts[:, 0:3 * N_BLK].rearrange("p (i t e) -> p i t e", i=3, t=NC)
        k_rows = wts[:, 3 * N_BLK:3 * N_BLK + N_BLK * M_BLK].rearrange("p (t r) -> p t r", t=NC)
        g_rows = hg[:, 0:3, :].rearrange("p i (t r) -> p i t r", t=NC)
        g_prod = hg[:, 3, :].rearrange("p (t g e) -> p t g e", t=NC, e=M_BLK)
        assert (3 + M_BLK) * N_BLK <= OFF[-1] + P
        od_params = sem("od_params")
        N_PARAMS = 28

        def load_params(pool):
            n_params = [0]

            def param(dst, src):
                with nc.allow_non_contiguous_dma("small parameters, by channel"):
                    pool.dma_start(dst, src).then_inc(od_params, 16)
                n_params[0] += 1
            for i, w in enumerate((od_w_q, od_w_k, od_w_v)):
                param(blk[:, i, :, :], w[0].rearrange("(t j) d e -> (j d) t e", t=NC))
            for d in range(M_CONV):
                param(conv_w[:, d, :], od_conv_w[0, d].rearrange("(t p) -> p t", p=P))
            param(conv_b[:], od_conv_b[0].rearrange("(t p) -> p t", p=P))
            param(skip_c[:], od_skip[0].rearrange("(t p) -> p t", p=P))
            param(norm_c[:], od_norm[0].rearrange("h (t p) -> p (h t)", p=P))
            param(gate_b[0:4, :], od_b_gate[0, 0:4].rearrange("(g o) -> g o", o=1))
            param(gate_b[32:36, :], od_b_gate[0, 4:8].rearrange("(g o) -> g o", o=1))
            for d in range(M_BLK):
                for i in range(3):
                    param(g_rows[d:P:M_BLK, i, :, :], od_w_gate[0, i * INNER:(i + 1) * INNER].rearrange(
                        "(t j e) g -> j t (e g)", t=NC, e=M_BLK))
                param(k_rows[d:P:M_BLK, :, :], od_w_k[0].rearrange("(t j) d e -> j t (d e)", t=NC))
            assert n_params[0] == N_PARAMS

        mlp_stage(0, L_MLP0, with_pool=load_params)

        xcT = sbuf(odd, "xcT", [P, NC, S])
        val = sbuf(odd, "val", [P, T, INNER])
        qk_blk = sbuf(odd, "qk_blk", [P, NC, M_BLK])
        bd_mask = sbuf(odd, "bd_mask", [P, P // M_BLK, M_BLK])
        neg_all = sbuf(odd, "neg_all", [P, S])
        gate_x = neg_all[0:36, :]
        pre = ExitStack()
        xm = sbuf(pre, "xm", [P, 2, CT, M_CONV - 1 + S])
        conv = sbuf(pre, "conv", [P, 2, S])
        bd_v = sbuf(pre, "bd_v", [P, 2, P])
        g_fold = sbuf(pre, "g_fold", [P, 2, NC, 8])
        g_mat = sbuf(pre, "g_mat", [P, 2, NC, 36])
        od_zero, fold_done = sem("od_zero"), sem("fold_done")
        xm_out, conv0, conv_done, xc_ready = sem("xm_out"), sem("conv0"), sem("conv_done"), sem("xc_ready")
        bd_ready, v_mm, v_out, gates_mm, gate_out = (sem("bd_ready"), sem("v_mm"), sem("v_out"), sem("gates_mm"),
                                                     sem("gate_out"))
        PAD = M_CONV - 1
        with nc.Block() as block:
            @block.sync
            def _(sp):
                load_lap(sp, L_XM + 1, TAIL_KS)
                for lap in range(L_XM + 2, L_GATE[0] + 2):
                    load_lap(sp, lap)

            @block.gpsimd
            def _(pool):
                step = stepper(pool, "pool", pool_step)
                pool.memset(xm[:, :, :, 0:PAD], 0.0).then_inc(od_zero, 1)
                pool.memset(g_mat[:], 0.0).then_inc(od_zero, 1)
                step(pool.memset(bd_mask[:], 1.0))
                step(pool.affine_select(out=bd_mask[:], in_=bd_mask[:], compare_op=ALU.is_ge, fill=0.0, base=0,
                                        pattern=[[-M_BLK, P // M_BLK], [0, M_BLK]], channel_multiplier=1))
                step(pool.affine_select(out=bd_mask[:], in_=bd_mask[:], compare_op=ALU.is_ge, fill=0.0, base=M_BLK - 1,
                                        pattern=[[M_BLK, P // M_BLK], [0, M_BLK]], channel_multiplier=-1))
                pool.wait_ge(od_params, 16 * N_PARAMS)
                for ct in range(NC):
                    if ct >= 2:
                        pool.wait_ge(v_mm, ct - 1)
                    pool.tensor_tensor(bd_v[:, ct % 2, :].rearrange("p (j e) -> p j e", e=M_BLK), bd_mask[:],
                                       blk[:, 2, ct, :].unsqueeze(1).broadcast_to([P, P // M_BLK, M_BLK]),
                                       ALU.mult).then_inc(bd_ready, 1)

            @block.tensor
            def _(pe):
                def from_group(g):
                    for j in range(CT):
                        ct = g * CT + j
                        pe.wait_ge(bd_ready, ct + 1)
                        if ct >= 3:
                            pe.wait_ge(v_out, ct - 2)
                        for t in range(T):
                            mm = pe.matmul(ps[:, 4 + ct % 3, t * P:(t + 1) * P],
                                           xm[:, g % 2, j, PAD + t * P:PAD + (t + 1) * P], bd_v[:, ct % 2, :],
                                           start=True, stop=True)
                        mm.then_inc(v_mm, 1)
                        if ct == 0:
                            pe.wait_ge(fold_done, 2)
                        pe.matmul(ps[0:36, 7, :], g_mat[:, 1, ct, :], xm[:, g % 2, j, PAD:], start=(ct == 0), stop=False)
                    for j in range(CT):
                        ct = g * CT + j
                        pe.wait_ge(xc_ready, ct + 1)
                        mm = pe.matmul(ps[0:36, 7, :], g_mat[:, 0, ct, :], xcT[:, ct, :], start=False,
                                       stop=(ct == NC - 1))
                    mm.then_inc(gates_mm, 1)

                pe.wait_ge(xp_lo, n_xp[0])
                for g in range(M_HEADS):
                    if g >= 1:
                        pe.wait_ge(xm_out, CT * g)
                    lap_T(pe, L_XM + g, full_banks(0))
                    if g >= 1:
                        from_group(g - 1)
                pe.wait_ge(xm_out, CT * M_HEADS)
                from_group(M_HEADS - 1)

            @block.scalar
            def _(act):
                def silu(ct):
                    act.wait_ge(conv_done, ct + 1)
                    act.activation(xcT[:, ct, :], conv[:, ct % 2, :], ACT.Silu).then_inc(xc_ready, 1)

                round_lap(act, L_XM, TAIL_KS)
                for g in range(M_HEADS):
                    round_lap(act, L_XM + g + 1)
                    act.wait_ge(w_used, lap_done(L_XM + g))
                    if g == 0:
                        act.wait_ge(od_zero, 2)
                        act.wait_ge(od_params, 16 * N_PARAMS)
                    if g >= 2:
                        act.wait_ge(gates_mm, g - 1)
                        act.wait_ge(conv_done, CT * (g - 1))
                    for j in range(CT):
                        act.activation(xm[:, g % 2, j, PAD:], ps[:, j, :], ACT.Copy).then_inc(xm_out, 1)
                    for j in range(CT):
                        ct = g * CT + j
                        if ct >= 2:
                            act.wait_ge(xc_ready, ct - 1)
                        act.wait_ge(xm_out, ct + 1)
                        act.activation(conv[:, ct % 2, :], xm[:, g % 2, j, PAD:], ACT.Identity, bias=conv_b[:, ct:ct + 1],
                                       scale=conv_w[:, PAD, ct:ct + 1]).then_inc(conv0, 1)
                        if j >= 1:
                            silu(ct - 1)
                    silu(g * CT + CT - 1)
                act.wait_ge(gates_mm, M_HEADS)
                act.activation(gate_x[0:36, :], ps[0:36, 7, :], ACT.Copy).then_inc(gate_out, 1)

            @block.vector
            def _(dve):
                step = stepper(dve, "dve", dve_step)
                dve.wait_ge(od_params, 16 * N_PARAMS)
                dve.wait_ge(od_zero, 2)
                qk_prod = g_prod[:, :, 0:M_BLK, :]
                step(dve.tensor_tensor(qk_prod, blk[:, 0, :, :].unsqueeze(2).broadcast_to([P, NC, M_BLK, M_BLK]),
                                       k_rows.rearrange("p t (d e) -> p t d e", e=M_BLK), ALU.mult))
                step(dve.tensor_reduce(qk_blk[:], qk_prod, AX.X, ALU.add))
                for i in range(3):
                    step(dve.tensor_tensor(g_prod, blk[:, i, :, :].unsqueeze(2).broadcast_to([P, NC, 8, M_BLK]),
                                           g_rows[:, i, :, :].rearrange("p t (e g) -> p t g e", e=M_BLK), ALU.mult))
                    step(dve.tensor_reduce(g_fold[:, min(i, 1), :, :], g_prod, AX.X, ALU.add))
                    if i == 1:
                        step(dve.tensor_tensor(g_fold[:, 0, :, :], g_fold[:, 0, :, :], g_fold[:, 1, :, :], ALU.add))
                dve.tensor_copy(g_mat[:, :, :, 0:4], g_fold[:, :, :, 0:4]).then_inc(fold_done, 1)
                dve.tensor_copy(g_mat[:, :, :, 32:36], g_fold[:, :, :, 4:8]).then_inc(fold_done, 1)

                def values_out(g):
                    for ct in range(g * CT, (g + 1) * CT):
                        dve.wait_ge(v_mm, ct + 1)
                        dve.tensor_copy(val[:, :, ct * P:(ct + 1) * P], bank_as_tiles(4 + ct % 3)).then_inc(v_out, 1)

                split_lap(dve, L_XM, TAIL_KS)
                for g in range(M_HEADS):
                    split_lap(dve, L_XM + g + 1)
                    for j in range(CT):
                        ct = g * CT + j
                        dve.wait_ge(conv0, ct + 1)
                        for tap in range(PAD):
                            ins = dve.scalar_tensor_tensor(out=conv[:, ct % 2, :], in0=xm[:, g % 2, j, tap:tap + S],
                                                           scalar=conv_w[:, tap, ct:ct + 1], in1=conv[:, ct % 2, :],
                                                           op0=ALU.mult, op1=ALU.add)
                            if tap < PAD - 1:
                                step(ins)
                        ins.then_inc(conv_done, 1)
                    if g >= 1:
                        values_out(g - 1)
                values_out(M_HEADS - 1)
        pre.close()

        rows = ExitStack()
        a_col = sbuf(odd, "a_col", [P, 2, T, M_HEADS])
        neg_M = sbuf(odd, "neg_M", [4, S])
        above = sbuf(odd, "above", [P, P])
        i_row = sbuf(rows, "i_row", [4, S])
        f_rows = sbuf(rows, "f_rows", [36, 2, S])
        lf_row = sbuf(rows, "lf_row", [4, S])
        b_row = sbuf(rows, "b_row", [4, S])
        a_row = sbuf(rows, "a_row", [4, S])
        m_row = sbuf(rows, "m_row", [4, S])
        m_max = sbuf(rows, "m_max", [4, S])
        one_row = sbuf(rows, "one_row", [4, S])
        f_ready, row_const, a_ready, em_ready, m_done, cols_done = (sem("f_ready"), sem("row_const"), sem("a_ready"),
                                                                    sem("em_ready"), sem("m_done"), sem("cols_done"))
        sig_ready = sem("sig_ready")
        with nc.Block() as block:
            @block.sync
            def _(sp):
                load_lap(sp, L_GATE[0] + 2)

            @block.gpsimd
            def _(pool):
                step = stepper(pool, "pool", pool_step)
                pool.memset(one_row[:], 1.0).then_inc(row_const, 1)
                step(pool.memset(above[:], 0.0))
                step(pool.affine_select(out=above[:], in_=above[:], compare_op=ALU.is_ge, fill=MASKED, base=0,
                                        pattern=[[1, P]], channel_multiplier=-1))

            @block.scalar
            def _(act):
                step = stepper(act, "act", act_step)
                act.activation(i_row[:], gate_x[0:4, :], ACT.Identity, bias=gate_b[0:4, :])
                step(act.activation(f_rows[32:36, 0, :], gate_x[32:36, :], ACT.Identity, bias=gate_b[32:36, :]))
                step(act.activation(f_rows[32:36, 1, :], f_rows[32:36, 0, :], ACT.Abs))
                step(act.activation(f_rows[32:36, 1, :], f_rows[32:36, 1, :], ACT.Exp, scale=-1.0))
                act.activation(f_rows[32:36, 1, :], f_rows[32:36, 1, :], ACT.Ln, bias=1.0).then_inc(f_ready, 1)
                act.wait_ge(m_done, 1)
                act.activation(m_row[:], m_row[:], ACT.Exp, scale=-1.0).then_inc(em_ready, 1)
                round_lap(act, L_GATE[0] + 1)
                act.wait_ge(w_used, lap_done(L_GATE[0]))
                for t in range(T):
                    act.activation(hg[:, t, :], ps[:, 4 + t, :], ACT.Sigmoid).then_inc(sig_ready, 1)

            @block.vector
            def _(dve):
                step = stepper(dve, "dve", dve_step)
                dve.wait_ge(f_ready, 1)
                dve.wait_ge(row_const, 1)
                step(dve.scalar_tensor_tensor(out=lf_row[:], in0=f_rows[32:36, 0, :], scalar=0.0,
                                              in1=f_rows[32:36, 1, :], op0=ALU.min, op1=ALU.subtract))
                step(dve.tensor_tensor_scan(b_row[:], one_row[:], lf_row[:], 0.0, ALU.mult, ALU.add))
                dve.tensor_tensor(a_row[:], i_row[:], b_row[:], ALU.subtract).then_inc(a_ready, 1)
                dve.wait_ge(a_ready, 1)
                step(dve.tensor_tensor_scan(m_max[:], a_row[:], a_row[:], 0.0, ALU.max, ALU.max))
                step(dve.tensor_tensor(m_row[:], b_row[:], m_max[:], ALU.add))
                dve.tensor_scalar(neg_M[:], m_max[:], -1.0, None, ALU.mult).then_inc(m_done, 1)
                split_lap(dve, L_GATE[0] + 1)
                dve.wait_ge(cols_done, 1)
                step(dve.tensor_copy(a_col[:].rearrange("p a t h -> p (a t h)"), ps[:, 0, 0:2 * T * M_HEADS]))

            @block.tensor
            def _(pe):
                lap_N(pe, L_GATE[0], 4)
                pe.wait_ge(a_ready, 1)
                for t in range(T):
                    pe.transpose(ps[:, 0, t * 4:t * 4 + 4], a_row[:, t * P:(t + 1) * P], ident[0:4, 0:4])
                pe.wait_ge(em_ready, 1)
                for t in range(T):
                    mm = pe.transpose(ps[:, 0, (T + t) * 4:(T + t) * 4 + 4], m_row[:, t * P:(t + 1) * P],
                                      ident[0:4, 0:4])
                mm.then_inc(cols_done, 1)
        rows.close()

        heads = ExitStack()
        bd_qk = sbuf(heads, "bd_qk", [P, CT, P])
        zT = sbuf(heads, "zT", [P, CT, S])
        den = sbuf(heads, "den", [P, 2, T])
        h_stat = sbuf(heads, "h_stat", [P, T, 6])
        h_mv = sbuf(heads, "h_mv", [P, T, 2])
        h_std = sbuf(heads, "h_std", [P, T])
        y_hi = sbuf(heads, "y_hi", [P, CT, S], F32R)
        y_lo = sbuf(heads, "y_lo", [P, CT, S], F32R)
        bdqk_ready, z_mm, z_out, m_bc, m_bc_out = (sem("bdqk_ready"), sem("z_mm"), sem("z_out"), sem("m_bc"),
                                                   sem("m_bc_out"))
        diag_ready, wexp, dot_mm, w_ready = sem("diag_ready"), sem("wexp"), sem("dot_mm"), sem("w_ready")
        den_mm, den_ready, num_mm, h_gated, h_var, h_stdr, h_normed = (
            sem("den_mm"), sem("den_ready"), sem("num_mm"), sem("h_gated"), sem("h_var"), sem("h_stdr"),
            sem("h_normed"))
        hT_mm, xs_ready, y_f32, y_rounded, y_ready = (sem("hT_mm"), sem("xs_ready"), sem("y_f32"), sem("y_rounded"),
                                                      sem("y_ready"))
        AB = n_added[0]
        near = lambda h: 4 if h % 2 == 0 else 0
        far = lambda h: 4 - near(h)
        LAST = M_HEADS - 1
        space = norm_space(heads, ln1_g[1:2], ln1_b[1:2], val[:, 0, 0:D], val[:, 1, 0:D])
        assert 2 * DH >= D
        with nc.Block() as block:
            @block.sync
            def _(sp):
                for lap in range(L_GATE[0] + 3, L_MLP1 + 1):
                    if lap == L_PROJ[2]:
                        sp.wait_ge(num_mm, 2 * T)
                        norm_load(sp, space)
                    load_lap(sp, lap)
                load_lap(sp, L_MLP1 + 1, HEAD_KS)

            @block.gpsimd
            def _(pool):
                for h in range(M_HEADS):
                    for j in range(CT):
                        if h >= 1:
                            pool.wait_ge(z_mm, CT * (h - 1) + j + 1)
                        pool.tensor_tensor(
                            bd_qk[:, j, :].rearrange("p (j e) -> p j e", e=M_BLK), bd_mask[:],
                            qk_blk[:, h * CT + j, :].unsqueeze(1).broadcast_to([P, P // M_BLK, M_BLK]),
                            ALU.mult).then_inc(bdqk_ready, 1)
                norm_pool(pool, space)

            @block.tensor
            def _(pe):
                def start(h):
                    pe.matmul(ps[:, far(h) + 3, :], ident[0:M_HEADS, h:h + 1].broadcast_to([M_HEADS, P]), neg_M[:], start=True, stop=True).then_inc(m_bc, 1)
                    for j in range(CT):
                        pe.wait_ge(bdqk_ready, h * CT + j + 1)
                        if j == 3:
                            pe.wait_ge(m_bc_out, h + 1)
                        pe.matmul(ps[:, far(h) + j, :], bd_qk[:, j, :], xcT[:, h * CT + j, :],
                                  start=True, stop=True).then_inc(z_mm, 1)

                def dots(h):
                    pe.wait_ge(z_out, CT * (h + 1))
                    for i in range(T):
                        n = (T - i) * P
                        for j in range(CT):
                            mm = pe.matmul(ps[:, far(h) + i, 0:n], xcT[:, h * CT + j, i * P:(i + 1) * P],
                                           zT[:, j, i * P:], start=(j == 0), stop=(j == CT - 1))
                        mm.then_inc(dot_mm, 1)

                def lhs(i, t):
                    return wts[:, OFF[i] + (t - i) * P:OFF[i] + (t - i + 1) * P]

                def numerators(h):
                    pe.wait_ge(w_ready, T * (h + 1))
                    for t in range(T):
                        for i in range(t + 1):
                            mm = pe.matmul(ps[:, far(h), t:t + 1], lhs(i, t), ones[:, 0:1], start=(i == 0), stop=(i == t))
                    mm.then_inc(den_mm, 1)
                    for t in range(T):
                        for i in range(t + 1):
                            mm = pe.matmul(ps[:, near(h) + t, :], lhs(i, t), val[:, i, h * DH:(h + 1) * DH],
                                           start=(i == 0), stop=(i == t))
                        mm.then_inc(num_mm, 1)

                def turn(h):
                    pe.wait_ge(h_normed, T * (h + 1))
                    for j in range(CT):
                        if h < LAST:
                            pe.wait_ge(z_out, CT * (h + 1) + j + 1)
                        for t in range(T):
                            mm = pe.transpose(ps[:, near(h) + j, t * P:(t + 1) * P], hg[:, t, j * P:(j + 1) * P],
                                              ident[:])
                        mm.then_inc(hT_mm, 1)

                def project(h):
                    pe.wait_ge(y_f32, CT * (h + 1))

                    for half, bank0 in ((0, near(h)), (1, far(h))):
                        if half:
                            pe.wait_ge(sig_ready, T * (h + 2))
                        for kk in range(4):
                            if half == 0:
                                pe.wait_ge(y_ready, CT * h + kk + 1)
                            pe.wait_ge(w_split, L_PROJ[h] * SLOTS + half * 4 + kk + 1)
                            tile_N(pe, half * 4 + kk, y_hi[:, kk, :], y_lo[:, kk, :], bank0, kk == 0, kk == 3)

                start(0)
                dots(0)
                for h in range(M_HEADS):
                    numerators(h)
                    if h < LAST:
                        pe.wait_ge(den_ready, h + 1)
                        lap_N(pe, L_GATE[h + 1], far(h))
                        pe.wait_ge(h_gated, T * (h + 1))
                        start(h + 1)
                    turn(h)
                    if h < LAST:
                        project(h)
                        pe.wait_ge(added, AB + 8 * h + 4)
                        dots(h + 1)
                        pe.wait_ge(added, AB + 8 * (h + 1))
                pe.wait_ge(y_ready, CT * M_HEADS)
                y_parts = (lambda kk: y_hi[:, kk, :], lambda kk: y_lo[:, kk, :])
                by_tokens(pe, L_PROJ[LAST], [(range(4), *y_parts, near(LAST)), (range(4, 8), *y_parts, far(LAST))],
                          space)

            @block.scalar
            def _(act):
                def start(h):
                    act.wait_ge(m_bc, h + 1)
                    act.activation(neg_all[:], ps[:, far(h) + 3, :], ACT.Copy).then_inc(m_bc_out, 1)
                    for j in range(CT):
                        act.wait_ge(z_mm, CT * h + j + 1)
                        act.activation(zT[:, j, :], ps[:, far(h) + j, :], ACT.Copy).then_inc(z_out, 1)

                def exponentials(h):
                    for i in range(T):
                        act.wait_ge(diag_ready, T * h + i + 1)
                        bias = a_col[:, 0, i, h:h + 1]
                        if i < T - 1:
                            act.activation(wts[:, OFF[i] + P:OFF[i] + (T - i) * P], neg_all[:, (i + 1) * P:], ACT.Exp,
                                           bias=bias)
                        act.activation(wts[:, OFF[i]:OFF[i] + P], wts[:, OFF[i]:OFF[i] + P], ACT.Exp, bias=bias).then_inc(wexp, 1)

                start(0)
                exponentials(0)
                for h in range(M_HEADS):
                    act.wait_ge(dot_mm, T * (h + 1))
                    for j in range(CT):
                        ct = h * CT + j
                        act.activation(xcT[:, ct, :], xcT[:, ct, :], ACT.Copy, scale=skip_c[:, ct:ct + 1]).then_inc(xs_ready, 1)
                    act.wait_ge(h_var, h + 1)
                    act.activation(h_std[:], h_mv[:, :, 1], ACT.Sqrt, bias=eps[:, 0:1]).then_inc(h_stdr, 1)
                    if h < LAST:
                        round_lap(act, L_PROJ[h])
                        start(h + 1)
                    for j in range(CT):
                        act.wait_ge(y_f32, CT * h + j + 1)
                        act.activation(y_hi[:, j, :], hg[:, j, :], ACT.Copy).then_inc(y_rounded, 1)
                    if h < LAST:
                        act.wait_ge(y_ready, CT * (h + 1))
                        act.wait_ge(w_used, lap_done(L_GATE[h + 1]))
                        for t in range(T):
                            act.activation(hg[:, t, :], ps[:, far(h) + t, :], ACT.Sigmoid).then_inc(sig_ready, 1)
                        exponentials(h + 1)
                        round_lap(act, L_PROJ[h] + 1)
                norm_act(act, space, L_PROJ[LAST])

            @block.vector
            def _(dve):
                step = stepper(dve, "dve", dve_step)

                def diagonals(h):
                    dve.wait_ge(m_bc_out, h + 1)
                    for i in range(T):
                        dve.tensor_tensor(wts[:, OFF[i]:OFF[i] + P], neg_all[:, i * P:(i + 1) * P], above[:],
                                          ALU.add).then_inc(diag_ready, 1)

                def weights(h):
                    for i in range(T):
                        n = (T - i) * P
                        dve.wait_ge(wexp, T * h + i + 1)
                        dve.wait_ge(dot_mm, T * h + i + 1)
                        w = wts[:, OFF[i]:OFF[i] + n]
                        dve.scalar_tensor_tensor(out=w, in0=ps[:, far(h) + i, 0:n], scalar=DH ** -0.5, in1=w,
                                                 op0=ALU.mult, op1=ALU.mult).then_inc(w_ready, 1)

                diagonals(0)
                weights(0)
                for h in range(M_HEADS):
                    dve.wait_ge(den_mm, h + 1)
                    step(dve.tensor_scalar(den[:, 0, :], ps[:, far(h), 0:T], -1.0, None, ALU.mult))
                    ins = dve.tensor_tensor(den[:, 0, :], ps[:, far(h), 0:T], den[:, 0, :], ALU.max)
                    ins.then_inc(den_ready, 1)
                    dve.wait_ge(den_ready, h + 1)
                    step(dve.tensor_tensor(den[:, 0, :], den[:, 0, :], a_col[:, 1, :, h], ALU.max))
                    step(dve.reciprocal(den[:, 1, :], den[:, 0, :]))
                    dve.wait_ge(sig_ready, T * (h + 1))
                    for t in range(T):
                        dve.wait_ge(num_mm, T * h + t + 1)
                        dve.scalar_tensor_tensor(out=hg[:, t, :], in0=ps[:, near(h) + t, :], scalar=den[:, 1, t:t + 1],
                                                 in1=hg[:, t, :], op0=ALU.mult, op1=ALU.mult).then_inc(h_gated, 1)
                        dve.wait_ge(h_gated, T * h + t + 1)
                        ins = dve.bn_stats(h_stat[:, t, :], hg[:, t, :])
                    step(ins)
                    for t in range(T):
                        ins = dve.bn_aggr(h_mv[:, t, :], h_stat[:, t, :])
                    ins.then_inc(h_var, 1)
                    dve.wait_ge(h_stdr, h + 1)
                    step(dve.reciprocal(h_std[:], h_std[:]))
                    for t in range(T):
                        dve.tensor_scalar(hg[:, t, :], hg[:, t, :], h_mv[:, t, 0:1], h_std[:, t:t + 1],
                                          ALU.subtract, ALU.mult).then_inc(h_normed, 1)
                    if h < LAST:
                        split_lap(dve, L_PROJ[h])
                        diagonals(h + 1)
                    dve.wait_ge(xs_ready, CT * (h + 1))
                    dve.wait_ge(hT_mm, CT * (h + 1))
                    for j in range(CT):
                        ct = h * CT + j
                        dve.scalar_tensor_tensor(out=hg[:, j, :], in0=ps[:, near(h) + j, :], scalar=norm_c[:, ct:ct + 1],
                                                 in1=xcT[:, ct, :], op0=ALU.mult, op1=ALU.add).then_inc(y_f32, 1)
                    for j in range(CT):
                        dve.wait_ge(y_rounded, CT * h + j + 1)
                        dve.tensor_tensor(y_lo[:, j, :], hg[:, j, :], y_hi[:, j, :].bitcast(F32),
                                          ALU.subtract).then_inc(y_ready, 1)
                    if h < LAST:
                        lap = L_PROJ[h]
                        split_lap(dve, lap + 1, range(4))
                        dve.wait_ge(w_used, lap * SLOTS + 4)
                        add_half(dve, 0, near(h))
                        split_lap(dve, lap + 1, range(4, 8))
                        dve.wait_ge(w_used, lap * SLOTS + 8)
                        add_half(dve, 1, far(h))
                        weights(h + 1)
                n_added[0] += 8 * LAST
                norm_dve(dve, space, L_PROJ[LAST], [(0, near(LAST)), (1, far(LAST))])
        n_xp[0] += 8
        heads.close()
        odd.close()

        mlp_stage(1, L_MLP1, final=True)


_INS = ["x", "ev_w_in", "ev_g_w2", "ev_g_b2", "ev_g_norm", "ev_w_out", "od_w_in", "od_conv_w", "od_conv_b",
        "od_w_q", "od_w_k", "od_w_v", "od_w_gate", "od_b_gate", "od_skip", "od_norm", "od_w_out",
        "ln1_g", "ln1_b", "ln2_g", "ln2_b", "mlp_w1", "mlp_w2"]


def kernel(**inputs):
    import numpy as _np
    import concourse.bacc as _bacc
    from concourse import mybir as _mybir
    from concourse.bass_utils import run_bass_kernel_spmd as _run

    nc = _bacc.Bacc("TRN2", target_bir_lowering=False, num_devices=1)
    arrays, args = {}, []
    for name in _INS:
        a = _np.ascontiguousarray(inputs[name])
        arrays[f"in_{name}"] = a
        args.append(nc.dram_tensor(f"in_{name}", a.shape, _mybir.dt.from_np(a.dtype), kind="ExternalInput").ap())
    shape = tuple(inputs["x"].shape)
    args.append(nc.dram_tensor("out_0", shape, _mybir.dt.float32, kind="ExternalOutput").ap())
    hybrid_trunk(nc, *args)
    r = _run(nc, [arrays], core_ids=[0])
    return r.results[0]["out_0"]
```

```python
from contextlib import ExitStack

import concourse.bass as bass
from concourse import mybir

F32 = mybir.dt.float32
F32R = mybir.dt.float32r
U32 = mybir.dt.uint32
ALU = mybir.AluOpType
ACT = mybir.ActivationFunctionType
AX = mybir.AxisListType

P = 128
SLOTS = 8
WIDE = 512
NEG = -3.0e38
MASKED = -1.0e30
LN_EPS = 1e-5

A_HEADS, A_DIM, TOPK = 8, 64, 128
G_HEADS, G_DIM, G_RANK, G_TAU = 4, 128, 16, 16.0
M_HEADS, M_CONV, M_BLK = 4, 4, 4


def hybrid_trunk(nc, x, ev_w_in, ev_g_w2, ev_g_b2, ev_g_norm, ev_w_out, od_w_in, od_conv_w, od_conv_b,
                 od_w_q, od_w_k, od_w_v, od_w_gate, od_b_gate, od_skip, od_norm, od_w_out,
                 ln1_g, ln1_b, ln2_g, ln2_b, mlp_w1, mlp_w2, out):
    _, S, D = x.shape
    T = S // P
    KD = D // P
    DEPTH = ln1_g.shape[0]
    ALPHA = (2 * DEPTH) ** 0.25
    FF = mlp_w1.shape[2]
    CH = FF // WIDE
    INNER = od_w_out.shape[1]
    DH = INNER // M_HEADS
    CT = DH // P
    assert (S, D, KD, T, DH) == (512, 1024, SLOTS, 4, WIDE)

    AQ, AK, AV = 0, 512, 576
    IQ, IK, IW = 640, 1152, 1216
    GQ, GK, GV, GR, GLR = 1224, 1736, 2248, 2760, 3272
    w_in = ev_w_in[0]

    def column_lap(w, c0, width, row0=0):
        return lambda k: [(0, w[row0 + k * P:row0 + (k + 1) * P, c0:c0 + width])]

    def small_lap(k):
        rows = slice(k * P, (k + 1) * P)
        return [(0, w_in[rows, AK:AK + 128]), (P, w_in[rows, IK:IK + 72]), (P + 96, w_in[rows, GLR:GLR + G_RANK])]

    def row_lap(w, r0):
        return lambda k: [(0, w[bass.ds(r0 + (k % 4) * P, P), (k // 4) * WIDE:(k // 4 + 1) * WIDE])]

    def up_lap(layer, c):
        return lambda k: [(0, mlp_w1[layer, k * P:(k + 1) * P, bass.ds(c * WIDE, WIDE)])]

    LAPS = [column_lap(w_in, IQ, 512), small_lap, column_lap(w_in, AQ, 512), column_lap(w_in, GQ, 512),
            column_lap(w_in, GK, 512), column_lap(w_in, GR, 512), column_lap(w_in, GV, 512),
            column_lap(ev_w_out[0], 0, WIDE), column_lap(ev_w_out[0], WIDE, WIDE)]
    L_IQ, L_SMALL, L_AQ, L_GQ, L_GK, L_GR, L_GV, L_WO = range(8)
    WIDTHS = {L_SMALL: P + 96 + G_RANK}

    def add_mlp(layer):
        base = len(LAPS)
        LAPS.append(up_lap(layer, 0))
        for c in range(CH):
            if c + 1 < CH:
                LAPS.append(up_lap(layer, c + 1))
            LAPS.append(row_lap(mlp_w2[layer], c * WIDE))
        return base

    L_MLP0 = add_mlp(0)
    L_XM = len(LAPS)
    for h in range(M_HEADS):
        LAPS.append(column_lap(od_w_in[0], h * WIDE, WIDE))
    L_GATE, L_PROJ = {}, {}
    for h in range(M_HEADS + 1):
        if h < M_HEADS:
            L_GATE[h] = len(LAPS)
            LAPS.append(column_lap(od_w_in[0], INNER + h * WIDE, WIDE))
        if h >= 1:
            L_PROJ[h - 1] = len(LAPS)
            LAPS.append(row_lap(od_w_out[0], (h - 1) * WIDE))
    L_MLP1 = add_mlp(1)
    N_LAPS = len(LAPS)

    top = ExitStack()

    def sem(name):
        return top.enter_context(nc.semaphore(name))

    def sbuf(scope, name, shape, dt=F32):
        return scope.enter_context(nc.sbuf_tensor(name, shape, dt))

    with top:
        resid = sbuf(top, "resid", [P, T, D])
        with ExitStack() as aliased:
            xT_hi = sbuf(aliased, "xT_hi", [P, KD, S], F32R)
            xT_lo = sbuf(aliased, "xT_lo", [P, KD, S], F32R)
        x_space = sbuf(top, "x_space", [P, 2 * KD, S])
        w_raw = sbuf(top, "w_raw", [P, SLOTS, WIDE])
        w_hi = sbuf(top, "w_hi", [P, SLOTS, WIDE], F32R)
        w_lo = sbuf(top, "w_lo", [P, SLOTS, WIDE], F32R)
        ident = sbuf(top, "ident", [P, P])
        eps = sbuf(top, "eps", [P, 1])
        ones = sbuf(top, "ones", [P, P])
        ps = top.enter_context(nc.psum_tensor("ps", [P, 8, WIDE], F32))

        w_landed = [sem(f"w_landed{k}") for k in range(SLOTS)]
        w_rounded = sem("w_rounded")
        w_split = sem("w_split")
        w_used = sem("w_used")
        xp_done = sem("xp_done")
        xp_hi = sem("xp_hi")
        xp_lo = sem("xp_lo")
        added = sem("added")
        consts = sem("consts")
        dve_step = sem("dve_step")
        act_step = sem("act_step")
        pool_step = sem("pool_step")
        n_step = {"dve": 0, "act": 0, "pool": 0}
        n_added = [0]
        n_xp = [0]

        def stepper(eng, name, semaphore):
            def step(ins):
                n_step[name] += 1
                ins.then_inc(semaphore, 1)
                eng.wait_ge(semaphore, n_step[name])
            return step

        def load_tile(sp, lap, k, parts):
            if not (isinstance(lap, int) and lap == 0):
                sp.wait_ge(w_split, lap * SLOTS + k - SLOTS + 1)
            for col, src in parts:
                sp.dma_start(w_raw[:, k, col:col + src.shape[1]], src).then_inc(w_landed[k], 16)

        def load_lap(sp, lap, ks=range(SLOTS)):
            if lap < N_LAPS:
                for k in ks:
                    load_tile(sp, lap, k, LAPS[lap](k))

        def landed(lap):
            before = not isinstance(lap, int) or lap >= L_SMALL
            return (lap + 1 + (len(small_lap(0)) - 1 if before else 0)) * 16

        def round_tile(act, lap, k, width=WIDE):
            act.wait_ge(w_landed[k], landed(lap))
            if not (isinstance(lap, int) and lap == 0):
                act.wait_ge(w_used, lap * SLOTS + k - SLOTS + 1)
            act.activation(w_hi[:, k, 0:width], w_raw[:, k, 0:width], ACT.Copy).then_inc(w_rounded, 1)

        def split_tile(dve, lap, k, width=WIDE):
            dve.wait_ge(w_rounded, lap * SLOTS + k + 1)
            dve.tensor_tensor(w_lo[:, k, 0:width], w_raw[:, k, 0:width], w_hi[:, k, 0:width].bitcast(F32),
                              ALU.subtract).then_inc(w_split, 1)

        def round_lap(act, lap, ks=range(SLOTS)):
            if not isinstance(lap, int) or lap < N_LAPS:
                for k in ks:
                    round_tile(act, lap, k, WIDTHS.get(lap, WIDE) if isinstance(lap, int) else WIDE)

        def split_lap(dve, lap, ks=range(SLOTS)):
            if not isinstance(lap, int) or lap < N_LAPS:
                for k in ks:
                    split_tile(dve, lap, k, WIDTHS.get(lap, WIDE) if isinstance(lap, int) else WIDE)

        def tile_T(pe, k, a_hi, a_lo, outs, first, last):
            for dst, c0, cn in outs:
                pe.matmul(dst, w_hi[:, k, c0:c0 + cn], a_hi, start=first, stop=False)
                pe.matmul(dst, w_hi[:, k, c0:c0 + cn], a_lo, start=False, stop=False)
                mm = pe.matmul(dst, w_lo[:, k, c0:c0 + cn], a_hi, start=False, stop=last)
            mm.then_inc(w_used, 1)

        def tile_N(pe, k, a_hi, a_lo, bank0, first, last):
            for t in range(T):
                ts = slice(t * P, (t + 1) * P)
                pe.matmul(ps[:, bank0 + t, :], a_hi[:, ts], w_hi[:, k, :], start=first, stop=False)
                pe.matmul(ps[:, bank0 + t, :], a_hi[:, ts], w_lo[:, k, :], start=False, stop=False)
                mm = pe.matmul(ps[:, bank0 + t, :], a_lo[:, ts], w_hi[:, k, :], start=False, stop=last)
            mm.then_inc(w_used, 1)

        def lap_T(pe, lap, outs):
            for k in range(SLOTS):
                pe.wait_ge(w_split, lap * SLOTS + k + 1)
                tile_T(pe, k, xT_hi[:, k, :], xT_lo[:, k, :], outs, k == 0, k == SLOTS - 1)

        def lap_N(pe, lap, bank0, ks=range(SLOTS)):
            for k in ks:
                pe.wait_ge(w_split, lap * SLOTS + k + 1)
                tile_N(pe, k, xT_hi[:, k, :], xT_lo[:, k, :], bank0, k == 0, k == SLOTS - 1)

        def lap_rows(pe, lap, a_hi, a_lo, bank_left, bank_right, before_left, before_right):
            for half, bank0, before in ((0, bank_left, before_left), (1, bank_right, before_right)):
                before()
                for kk in range(4):
                    pe.wait_ge(w_split, lap * SLOTS + half * 4 + kk + 1)
                    tile_N(pe, half * 4 + kk, a_hi(kk), a_lo(kk), bank0, kk == 0, kk == 3)

        def by_tokens(pe, lap, parts, space, final=False, operand_ready=lambda kk: None):
            for t in range(T):
                ts = slice(t * P, (t + 1) * P)
                for slots, a_hi, a_lo, bank0, bank_free in parts:
                    bank_free(t)
                    for kk, k in enumerate(slots):
                        if t == 0:
                            operand_ready(kk)
                            pe.wait_ge(w_split, lap * SLOTS + k + 1)
                        first, end = kk == 0, k == slots[-1]
                        pe.matmul(ps[:, bank0 + t, :], a_hi(kk)[:, ts], w_hi[:, k, :], start=first, stop=False)
                        pe.matmul(ps[:, bank0 + t, :], a_hi(kk)[:, ts], w_lo[:, k, :], start=False, stop=False)
                        mm = pe.matmul(ps[:, bank0 + t, :], a_lo(kk)[:, ts], w_hi[:, k, :], start=False, stop=end)
                        if t == T - 1:
                            mm.then_inc(w_used, 1)
                        elif k == SLOTS - 1:
                            mm.then_inc(token_done, 1)
                if t >= 2 and not final:
                    norm_pe(pe, space, t - 2)
            if not final:
                for t in range(T - 2, T):
                    norm_pe(pe, space, t)

        def full_banks(bank0):
            return [(ps[:, bank0 + j, :], j * P, P) for j in range(4)]

        def lap_done(lap):
            return (lap + 1) * SLOTS

        def add_half(dve, half, bank0):
            for t in range(T):
                r = resid[:, t, half * WIDE:(half + 1) * WIDE]
                dve.tensor_tensor(r, ps[:, bank0 + t, :], r, ALU.add).then_inc(added, 1)

        def bank_as_tiles(b):
            return ps[:, b, :].rearrange("p (k q) -> p k q", k=4)

        def turn_half(pe, src, t, half):
            for j in range(4):
                c = (4 * half + j) * P
                mm = pe.transpose(ps[:, 4 * half + t, j * P:(j + 1) * P], src[:, t, c:c + P], ident[:])
            mm.then_inc(xp_done, 1)

        def hi_half(act, turned, t, half):
            act.wait_ge(xp_done, turned + 1)
            act.activation(xT_hi[:, 4 * half:4 * half + 4, t * P:(t + 1) * P], bank_as_tiles(4 * half + t),
                           ACT.Copy).then_inc(xp_hi, 1)

        def lo_half(dve, turned, t, half):
            ap = (slice(None), slice(4 * half, 4 * half + 4), slice(t * P, (t + 1) * P))
            dve.wait_ge(xp_hi, turned + 1)
            dve.tensor_tensor(xT_lo[ap], bank_as_tiles(4 * half + t), xT_hi[ap].bitcast(F32),
                              ALU.subtract).then_inc(xp_lo, 1)

        def transpose_pe(pe, src, t):
            for half in range(2):
                turn_half(pe, src, t, half)

        def transpose_act(act, base, t):
            for half in range(2):
                hi_half(act, base + 2 * t + half, t, half)

        def transpose_dve(dve, base, t):
            for half in range(2):
                lo_half(dve, base + 2 * t + half, t, half)

        gb_landed, norm_var, norm_std, norm_scaled, norm_y = (sem("gb_landed"), sem("norm_var"), sem("norm_std"),
                                                              sem("norm_scaled"), sem("norm_y"))
        norm_last = sem("norm_last")
        token_done = sem("token_done")
        out_stored = sem("out_stored")
        n_norm = [0]
        HEAD_KS, TAIL_KS = range(0, 1), range(1, SLOTS)

        def norm_space(scope, g_row, b_row, g_all=None, b_all=None):
            i = n_norm[0]
            n_norm[0] += 1
            g_all = sbuf(scope, f"ln_g{i}", [P, D]) if g_all is None else g_all
            b_all = sbuf(scope, f"ln_b{i}", [P, D]) if b_all is None else b_all
            return (i, g_row, b_row, g_all, b_all, sbuf(scope, f"ln_stat{i}", [P, T, 2, 6]),
                    sbuf(scope, f"ln_mv{i}", [P, T, 2]), sbuf(scope, f"ln_rstd{i}", [P, T]))

        def norm_load(sp, space):
            i, g_row, b_row, g_all, b_all = space[:5]
            sp.dma_start(g_all[:], g_row.broadcast_to([P, D])).then_inc(gb_landed, 16)
            sp.dma_start(b_all[:], b_row.broadcast_to([P, D])).then_inc(gb_landed, 16)

        def wait_norm(eng, space, t):
            if t < T - 1:
                eng.wait_ge(norm_y, space[0] * (T - 1) + t + 1)
            else:
                eng.wait_ge(norm_last, space[0] + 1)

        def norm_store(sp, space):
            for t in range(T):
                wait_norm(sp, space, t)
                sp.dma_start(out[0, t * P:(t + 1) * P, :], resid[:, t, :]).then_inc(out_stored, 16)
            sp.wait_ge(out_stored, 16 * T)

        def norm_dve(dve, space, lap, adds, final=False):
            i, _, _, g_all, b_all, stat, mv, rstd = space
            step = stepper(dve, "dve", dve_step)
            done, base = i * T, n_xp[0]

            def statistics(t):
                if t < T - 1:
                    dve.wait_ge(token_done, i * (T - 1) + t + 1)
                else:
                    dve.wait_ge(w_used, lap_done(lap))
                for half, bank0 in adds:
                    r = resid[:, t, half * WIDE:(half + 1) * WIDE]
                    dve.tensor_tensor(r, ps[:, bank0 + t, :], r, ALU.add).then_inc(added, 1)
                    n_added[0] += 1
                dve.wait_ge(added, n_added[0])
                dve.bn_stats(stat[:, t, 0, :], resid[:, t, 0:WIDE])
                step(dve.bn_stats(stat[:, t, 1, :], resid[:, t, WIDE:]))
                dve.bn_aggr(mv[:, t, :], stat[:, t, :, :].rearrange("p a b -> p (a b)")).then_inc(norm_var, 1)

            def scale(t):
                dve.wait_ge(norm_var, done + t + 1)
                r, mean = resid[:, t, :], mv[:, t, 0:1]
                if t < T - 1:
                    dve.wait_ge(norm_std, done + t + 1)
                    step(dve.reciprocal(rstd[:, t:t + 1], rstd[:, t:t + 1]))
                    dve.tensor_scalar(r, r, mean, rstd[:, t:t + 1], ALU.subtract, ALU.mult).then_inc(norm_scaled, 1)
                else:
                    dve.wait_ge(gb_landed, 32 * (i + 1))
                    dve.scalar_tensor_tensor(out=r, in0=r, scalar=mean, in1=g_all[:], op0=ALU.subtract, op1=ALU.mult)
                    dve.wait_ge(norm_std, done + t + 1)
                    step(dve.reciprocal(rstd[:, t:t + 1], rstd[:, t:t + 1]))
                    dve.scalar_tensor_tensor(out=r, in0=r, scalar=rstd[:, t:t + 1], in1=b_all[:], op0=ALU.mult,
                                             op1=ALU.add).then_inc(norm_last, 1)

            for t in range(T):
                if t == T - 1 and not final:
                    transpose_dve(dve, base, 0)
                statistics(t)
                scale(t)
            if not final:
                transpose_dve(dve, base, 1)
                transpose_dve(dve, base, 2)
                split_lap(dve, lap + 1, HEAD_KS)
                transpose_dve(dve, base, 3)

        def norm_pool(pool, space):
            i, _, _, g_all, b_all = space[:5]
            step = stepper(pool, "pool", pool_step)
            pool.wait_ge(gb_landed, 32 * (i + 1))
            for t in range(T - 1):
                pool.wait_ge(norm_scaled, i * (T - 1) + t + 1)
                step(pool.tensor_tensor(resid[:, t, :], resid[:, t, :], g_all[:], ALU.mult))
                pool.tensor_tensor(resid[:, t, :], resid[:, t, :], b_all[:], ALU.add).then_inc(norm_y, 1)

        def norm_act(act, space, lap, final=False):
            i, mv, rstd = space[0], space[6], space[7]

            def root(t):
                act.wait_ge(norm_var, i * T + t + 1)
                act.activation(rstd[:, t:t + 1], mv[:, t, 1:2], ACT.Sqrt, bias=eps[:, 0:1]).then_inc(norm_std, 1)

            def turned(t):
                if not final:
                    transpose_act(act, n_xp[0], t)
                    act.mul(resid[:, t, :], resid[:, t, :], ALPHA)

            for t in range(T):
                root(t)
                if t >= 2:
                    turned(t - 2)
            turned(T - 2)
            if not final:
                round_lap(act, lap + 1, HEAD_KS)
            turned(T - 1)

        def norm_pe(pe, space, t):
            wait_norm(pe, space, t)
            transpose_pe(pe, resid, t)

        even = ExitStack()
        level_mask = sbuf(even, "level_mask", [P, 8, P])
        tri_tau = sbuf(even, "tri_tau", [P, P])
        g_w2 = sbuf(even, "g_w2", [P, WIDE])[96:P, :]
        x_landed = [sem(f"x_landed{t}") for t in range(T)]
        params, g_w2_zero = sem("params"), sem("g_w2_zero")
        with nc.Block() as block:
            @block.sync
            def _(sp):
                for t in range(T):
                    sp.dma_start(resid[:, t, :], x[0, t * P:(t + 1) * P, :]).then_inc(x_landed[t], 16)
                load_lap(sp, 0)

            @block.gpsimd
            def _(pool):
                step = stepper(pool, "pool", pool_step)
                step(pool.memset(ident[:], 0.0))
                pool.affine_select(out=ident[:], in_=ident[:], compare_op=ALU.not_equal, fill=1.0, base=0,
                                   pattern=[[-1, P]], channel_multiplier=1).then_inc(consts, 1)
                pool.memset(eps[:], LN_EPS)
                pool.memset(ones[:], 1.0)
                step(pool.memset(tri_tau[:], 1.0 / G_TAU))
                step(pool.affine_select(out=tri_tau[:], in_=tri_tau[:], compare_op=ALU.is_ge, fill=0.0, base=0,
                                        pattern=[[1, P]], channel_multiplier=-1))
                step(pool.memset(level_mask[:], 0.0))
                for lev in range(7):
                    half = 64 >> lev
                    nb = P // (2 * half)
                    v = level_mask[:, lev, :].rearrange("p (b j) -> p b j", b=nb)[:, :, half:2 * half]
                    step(pool.memset(v, 1.0))
                    step(pool.affine_select(out=v, in_=v, compare_op=ALU.is_ge, fill=0.0, base=0,
                                            pattern=[[-2 * half, nb], [0, half]], channel_multiplier=1))
                    step(pool.affine_select(out=v, in_=v, compare_op=ALU.is_ge, fill=0.0, base=half - 1,
                                            pattern=[[2 * half, nb], [0, half]], channel_multiplier=-1))
                step(pool.affine_select(out=level_mask[:, 7, :], in_=level_mask[:, 7, :], compare_op=ALU.not_equal,
                                        fill=1.0, base=0, pattern=[[-1, P]], channel_multiplier=1))

            @block.tensor
            def _(pe):
                pe.wait_ge(consts, 1)
                for t in range(T):
                    pe.wait_ge(x_landed[t], 16)
                    transpose_pe(pe, resid, t)

            @block.scalar
            def _(act):
                act.wait_ge(g_w2_zero, 1)
                act.dma_start(g_w2[0:G_RANK, :], ev_g_w2[0]).then_inc(params, 16)
                act.dma_start(g_w2[G_RANK:G_RANK + 1, :], ev_g_b2[0:1, :]).then_inc(params, 16)
                for t in range(T):
                    transpose_act(act, 0, t)
                round_lap(act, L_IQ, HEAD_KS)

            @block.vector
            def _(dve):
                dve.memset(g_w2, 0.0).then_inc(g_w2_zero, 1)
                for t in range(T):
                    transpose_dve(dve, 0, t)
                split_lap(dve, L_IQ, HEAD_KS)
        n_xp[0] = 8

        gla_in = ExitStack()
        gqT = sbuf(gla_in, "gqT", [P, G_HEADS, S])
        gkT = sbuf(gla_in, "gkT", [P, G_HEADS, S])
        gv = sbuf(gla_in, "gv", [P, T, WIDE])
        gr = sbuf(gla_in, "gr", [P, T, WIDE])
        misc = sbuf(gla_in, "misc", [P, S])
        iwT, lrT = misc[64:72, :], misc[96:P, :]
        g_std = sbuf(gla_in, "g_std", [P, T, G_HEADS])
        cat = sbuf(gla_in, "cat", [P, T, D])
        dsa_in = ExitStack()
        aqT = sbuf(dsa_in, "aqT", [P, 4, S])
        akT = sbuf(dsa_in, "akT", [P, S])
        av = sbuf(dsa_in, "av", [P, T, A_DIM])
        left = sbuf(dsa_in, "left", [P, S])
        best8 = sbuf(dsa_in, "best8", [P, 8])
        bcum = sbuf(dsa_in, "bcum", [P, G_HEADS, S])
        key_mask = sbuf(dsa_in, "key_mask", [P, T, S])
        idx = ExitStack()
        iqT = sbuf(idx, "iqT", [P, 4, S])
        ikT = sbuf(idx, "ikT", [P, S])
        iw = sbuf(idx, "iw", [P, T, 8])
        relu_buf = sbuf(idx, "relu_buf", [P, 4, S])
        avT = relu_buf[64:P, 3, :]
        score = sbuf(idx, "score", [P, 3, S])

        proj_out = sem("proj_out")
        small_turned = sem("small_turned")
        keys_doubled = sem("keys_doubled")
        logits_done, relu_done, score_added = sem("logits_done"), sem("relu_done"), sem("score_added")
        lr_ones, gate_mm, ln_done, loga_done = sem("lr_ones"), sem("gate_mm"), sem("ln_done"), sem("loga_done")
        cum_done, b_ready = sem("cum_done"), sem("b_ready")
        causal_done, chosen, mask_ready = sem("causal_done"), sem("chosen"), sem("mask_ready")
        ITEMS = [(b, h) for b in range(1, T) for h in range(A_HEADS)]
        ROUNDS = TOPK // 8
        EARLY_ROUNDS = ROUNDS // 2

        def topk_round(dve, step, b, r):
            n = (b + 1) * P
            src = score[:, b - 1, 0:n] if r == 0 else left[:, 0:n]
            step(dve.max(best8[:], src))
            step(dve.match_replace(out=left[:, 0:n], in_to_replace=best8[:], in_values=src, imm_value=NEG))

        def topk_mask(dve, b):
            n = (b + 1) * P
            dve.tensor_scalar(key_mask[:, b, 0:n], left[:, 0:n], NEG / 3, MASKED, ALU.is_gt,
                              ALU.mult).then_inc(chosen, 1)

        def causal_select(pool, ap, fill):
            return pool.affine_select(out=ap, in_=ap, compare_op=ALU.is_ge, fill=fill, base=0,
                                      pattern=[[-1, P]], channel_multiplier=1)

        O_IQ, O_SMALL, O_TURNED, O_AQ, O_GQ, O_GK, O_GR, O_GV = 4, 8, 10, 14, 18, 22, 26, 30

        loga = relu_buf[:]

        with nc.Block() as block:
            @block.sync
            def _(sp):
                for lap in range(L_IQ + 1, L_WO + 2):
                    load_lap(sp, lap)

            @block.tensor
            def _(pe):
                pe.wait_ge(xp_lo, n_xp[0])
                lap_T(pe, L_IQ, full_banks(0))
                lap_T(pe, L_SMALL, [(ps[:, 4, :], 0, P), (ps[0:96 + G_RANK, 5, :], P, 96 + G_RANK)])
                pe.wait_ge(proj_out, O_IQ)
                lap_T(pe, L_AQ, full_banks(0))
                pe.wait_ge(proj_out, O_SMALL)
                for t in range(T):
                    pe.transpose(ps[:, 6, 8 * t:8 * t + 8], iwT[:, t * P:(t + 1) * P], ident[64:72, 64:72])
                for t in range(T):
                    mm = pe.transpose(ps[:, 6, 64 + 64 * t:128 + 64 * t], avT[:, t * P:(t + 1) * P],
                                      ident[64:P, 64:P])
                mm.then_inc(small_turned, 1)
                pe.wait_ge(keys_doubled, 32)
                pe.wait_ge(proj_out, O_TURNED)
                for u, (b, h) in enumerate(ITEMS):
                    if u >= 4:
                        pe.wait_ge(relu_done, u - 3)
                    r = slice(64 * (h % 2), 64 * (h % 2) + 64)
                    pe.matmul(ps[:, 4 + u % 4, 0:(b + 1) * P], iqT[r, h // 2, b * P:(b + 1) * P],
                              ikT[r, 0:(b + 1) * P], start=True, stop=True).then_inc(logits_done, 1)
                pe.wait_ge(params, 32)
                pe.wait_ge(relu_done, len(ITEMS))
                for c in range(T):
                    pe.matmul(ps[:, 4 + c, :], lrT[:, c * P:(c + 1) * P], g_w2, start=True, stop=True).then_inc(gate_mm, 1)
                pe.wait_ge(proj_out, O_AQ)
                lap_T(pe, L_GQ, full_banks(0))
                pe.wait_ge(loga_done, T)
                for h in range(G_HEADS):
                    for c in range(T):
                        mm = pe.matmul(ps[:, 4 + h, c * P:(c + 1) * P], loga[:, c, h * P:(h + 1) * P],
                                       tri_tau[:], start=True, stop=True)
                    mm.then_inc(cum_done, 1)
                pe.wait_ge(b_ready, G_HEADS)
                lap_T(pe, L_GK, full_banks(4))
                pe.wait_ge(proj_out, O_GQ)
                lap_N(pe, L_GR, 0)
                pe.wait_ge(proj_out, O_GK)
                lap_N(pe, L_GV, 4)

            @block.scalar
            def _(act):
                def copy_out(dst, src, scale=1.0):
                    act.activation(dst, src, ACT.Copy, scale=scale).then_inc(proj_out, 1)

                def copy_banks(dst, bank0, scale=1.0):
                    for j in range(4):
                        copy_out(dst[:, j, :], ps[:, bank0 + j, :], scale)

                round_lap(act, L_IQ, TAIL_KS)
                for t in range(T):
                    act.mul(resid[:, t, :], resid[:, t, :], ALPHA)
                round_lap(act, L_SMALL)
                act.wait_ge(w_used, lap_done(L_IQ))
                copy_banks(iqT, 0)
                round_lap(act, L_AQ)
                act.wait_ge(w_used, lap_done(L_SMALL))
                copy_out(akT[0:64, :], ps[0:64, 4, :])
                copy_out(avT, ps[64:P, 4, :])
                copy_out(ikT[0:64, :], ps[0:64, 5, :])
                act.wait_ge(lr_ones, 1)
                copy_out(misc[64:96 + G_RANK, :], ps[64:96 + G_RANK, 5, :])
                act.wait_ge(proj_out, O_SMALL)
                act.dma_start(ikT[64:128, :], ikT[0:64, :]).then_inc(keys_doubled, 16)
                act.dma_start(akT[64:128, :], akT[0:64, :]).then_inc(keys_doubled, 16)
                round_lap(act, L_GQ)
                act.wait_ge(small_turned, 1)
                copy_out(iw[:].rearrange("p t h -> p (t h)"), ps[:, 6, 0:8 * T], A_HEADS ** -0.5)
                copy_out(av[:].rearrange("p t d -> p (t d)"), ps[:, 6, 64:64 + 64 * T])
                act.wait_ge(w_used, lap_done(L_AQ))
                copy_banks(aqT, 0)
                for u, (b, h) in enumerate(ITEMS):
                    act.wait_ge(logits_done, u + 1)
                    if u >= 4:
                        act.wait_ge(score_added, u - 3)
                    act.activation(relu_buf[:, u % 4, 0:(b + 1) * P], ps[:, 4 + u % 4, 0:(b + 1) * P], ACT.Relu,
                                   scale=A_DIM ** -0.5).then_inc(relu_done, 1)
                step = stepper(act, "act", act_step)
                act.wait_ge(score_added, len(ITEMS))
                for c in range(T):
                    act.wait_ge(gate_mm, c + 1)
                    ins = act.activation(loga[:, c, :], ps[:, 4 + c, :], ACT.Abs)
                step(ins)
                step(act.activation(loga, loga, ACT.Exp, scale=-1.0))
                act.activation(loga, loga, ACT.Ln, bias=1.0).then_inc(ln_done, 1)
                round_lap(act, L_GK)
                for h in range(G_HEADS):
                    act.wait_ge(cum_done, h + 1)
                    act.activation(bcum[:, h, :], ps[:, 4 + h, :], ACT.Copy).then_inc(b_ready, 1)
                act.wait_ge(w_used, lap_done(L_GQ))
                copy_banks(gqT, 0, G_DIM ** -0.5)
                round_lap(act, L_GR)
                act.wait_ge(w_used, lap_done(L_GK))
                copy_banks(gkT, 4)
                round_lap(act, L_GV)
                act.wait_ge(w_used, lap_done(L_GR))
                for t in range(T):
                    act.activation(gr[:, t, :], ps[:, t, :], ACT.Silu).then_inc(proj_out, 1)
                round_lap(act, L_WO)

            @block.vector
            def _(dve):
                step = stepper(dve, "dve", dve_step)
                dve.memset(lrT, 1.0).then_inc(lr_ones, 1)
                split_lap(dve, L_IQ, TAIL_KS)
                split_lap(dve, L_SMALL)
                split_lap(dve, L_AQ)
                split_lap(dve, L_GQ)
                dve.wait_ge(proj_out, O_TURNED)
                for u, (b, h) in enumerate(ITEMS):
                    n = (b + 1) * P
                    dve.wait_ge(relu_done, u + 1)
                    if h == 0:
                        ins = dve.tensor_scalar(score[:, b - 1, 0:n], relu_buf[:, u % 4, 0:n], iw[:, b, 0:1], None,
                                                ALU.mult)
                    else:
                        dve.wait_ge(score_added, u)
                        ins = dve.scalar_tensor_tensor(out=score[:, b - 1, 0:n], in0=relu_buf[:, u % 4, 0:n],
                                                       scalar=iw[:, b, h:h + 1], in1=score[:, b - 1, 0:n],
                                                       op0=ALU.mult, op1=ALU.add)
                    ins.then_inc(score_added, 1)
                dve.wait_ge(ln_done, 1)
                for c in range(T):
                    dve.scalar_tensor_tensor(out=loga[:, c, :], in0=ps[:, 4 + c, :], scalar=0.0, in1=loga[:, c, :],
                                             op0=ALU.min, op1=ALU.subtract).then_inc(loga_done, 1)
                tiles = [(lap, k) for lap in range(L_GK, L_WO + 1) for k in range(SLOTS)]
                for b in range(1, T):
                    dve.wait_ge(causal_done, b)
                    for r in range(ROUNDS if b < T - 1 else EARLY_ROUNDS):
                        topk_round(dve, step, b, r)
                        if tiles and r % 5 != 0:
                            split_tile(dve, *tiles.pop(0))
                    if b < T - 1:
                        topk_mask(dve, b)
                for lap, k in tiles:
                    split_tile(dve, lap, k)

            @block.gpsimd
            def _(pool):
                step = stepper(pool, "pool", pool_step)

                def causal(ap, fill):
                    return causal_select(pool, ap, fill)

                step(pool.memset(key_mask[:, 0, 0:P], 0.0))
                causal(key_mask[:, 0, 0:P], MASKED).then_inc(mask_ready, 1)
                for b in range(1, T):
                    pool.wait_ge(score_added, b * A_HEADS)
                    causal(score[:, b - 1, b * P:(b + 1) * P], NEG).then_inc(causal_done, 1)
                for b in range(1, T - 1):
                    pool.wait_ge(chosen, b)
                    causal(key_mask[:, b, b * P:(b + 1) * P], MASKED).then_inc(mask_ready, 1)
        idx.close()

        mix = ExitStack()
        s_neg = sbuf(mix, "s_neg", [P, 2, S])
        prob = sbuf(mix, "prob", [P, 2, S])
        probT = sbuf(mix, "probT", [P, 2, S])
        min_neg = sbuf(mix, "min_neg", [P, T * A_HEADS])
        row_sum = sbuf(mix, "row_sum", [P, T * A_HEADS])
        row_inv = sbuf(mix, "row_inv", [P, T * A_HEADS])
        q_exp = x_space[:, 0:4, :]
        ebcum = x_space[:, 4:8, :]
        diff = x_space[:, 8:12, :]
        expd = diff
        k_lev = x_space[:, 12:14, :]
        q_lev = x_space[:, 14:15, :].rearrange("p o (n q) -> p (o n) q", n=2)
        k_end = k_lev[:, (8 - 1) % 2, :]
        k_endT = sbuf(mix, "k_endT", [P, 3 * P])
        attT = sbuf(mix, "attT", [P, 2, S])
        state = sbuf(mix, "state", [P, 2, 3, G_DIM])
        g_norm = sbuf(mix, "g_norm", [P, WIDE])
        g_stat = sbuf(mix, "g_stat", [P, T, 6])
        g_mv = sbuf(mix, "g_mv", [P, T, G_HEADS, 2])
        s_done, s_masked, exp_done = sem("s_done"), sem("s_masked"), sem("exp_done")
        pt_done, pt_out, pv_done, o_out = sem("pt_done"), sem("pt_out"), sem("pv_done"), sem("o_out")
        eb_ready, qe_ready = sem("eb_ready"), sem("qe_ready")
        diff_ready, expd_ready, lev_ready = sem("diff_ready"), sem("expd_ready"), sem("lev_ready")
        lev_mm, lev_kept = sem("lev_mm"), sem("lev_kept")
        kend_turned, kend_out = sem("kend_turned"), sem("kend_out")
        su_mm, s_ready, o_mm = sem("su_mm"), sem("s_ready"), sem("o_mm")
        sg_ready, o_gated, var_ready, std_ready = sem("sg_ready"), sem("o_gated"), sem("var_ready"), sem("std_ready")
        g_norm_landed, attT_zero = sem("g_norm_landed"), sem("attT_zero")
        QH = [(b, h) for b in range(T) for h in range(A_HEADS)]
        LEV = 8
        N_LEV = G_HEADS * LEV
        EXP_B, Q_EXP = 4, 6
        FIRST = 3
        FIRST_ITEM = 5
        AHEAD = 3
        STEPS = range(max(FIRST + N_LEV + 6, FIRST_ITEM + len(QH) + 2))

        ROUND_STEPS = (0, 1, 2, 4, 6, 8, 10, 11)
        MASK_LEVEL = 12
        assert len(ROUND_STEPS) == ROUNDS - EARLY_ROUNDS

        def item_at(step, ahead=0):
            i = step - FIRST_ITEM + ahead
            return i if 0 <= i < len(QH) else None

        def level_at(step, ahead=0):
            n = step - FIRST + ahead
            return n if 0 <= n < N_LEV else None

        def head_after(step, steps):
            h, lev = divmod(step - FIRST - steps, LEV)
            return h if lev == LEV - 1 and 0 <= h < G_HEADS else None

        def blocks_of(ap, half):
            return ap.rearrange("p (b j) -> p b j", j=2 * half)

        with nc.Block() as block:
            @block.sync
            def _(sp):
                sp.dma_start(g_norm[:], ev_g_norm[0:1].rearrange("o h d -> o (h d)").broadcast_to([P, WIDE])
                             ).then_inc(g_norm_landed, 16)

            @block.tensor
            def _(pe):
                def scores(i):
                    b, h = QH[i]
                    r = slice(64 * (h % 2), 64 * (h % 2) + 64)
                    if i == 0:
                        pe.wait_ge(proj_out, O_GV)
                    if i >= 2:
                        pe.wait_ge(s_masked, i - 1)
                    pe.matmul(ps[:, 4 + i % 2, 0:(b + 1) * P], aqT[r, h // 2, b * P:(b + 1) * P], akT[r, 0:(b + 1) * P],
                              start=True, stop=True).then_inc(s_done, 1)

                def turn(i):
                    b, h = QH[i]
                    pe.wait_ge(exp_done, i + 1)
                    if i >= 1:
                        pe.wait_ge(pt_out, i)
                    for kt in range(b + 1):
                        mm = pe.transpose(ps[:, 6, kt * P:(kt + 1) * P], prob[:, i % 2, kt * P:(kt + 1) * P], ident[:])
                    mm.then_inc(pt_done, 1)

                def values(i):
                    b, h = QH[i]
                    pe.wait_ge(pt_out, i + 1)
                    if b >= 1 and h == 0:
                        pe.wait_ge(o_out, b)
                    for kt in range(b + 1):
                        mm = pe.matmul(ps[:, 7, h * A_DIM:(h + 1) * A_DIM], probT[:, i % 2, kt * P:(kt + 1) * P],
                                       av[:, kt, :], start=(kt == 0), stop=(kt == b))
                    mm.then_inc(pv_done, 1)

                def level(n):
                    h, lev = divmod(n, LEV)
                    pe.wait_ge(lev_ready, n + 1)
                    if n >= 2:
                        pe.wait_ge(lev_kept, n - 1)
                    for c in range(T):
                        cs, us = slice(c * P, (c + 1) * P), slice(c * P // 2, (c + 1) * P // 2)
                        if lev < 7:
                            mm = pe.matmul(ps[:, n % 2, us], k_lev[:, n % 2, cs], q_lev[:, n % 2, us],
                                           start=True, stop=True)
                        else:
                            mm = pe.matmul(ps[:, n % 2, cs], gkT[:, h, cs], gqT[:, h, cs], start=True, stop=True)
                    mm.then_inc(lev_mm, 1)

                def turn_keys(h):
                    if h >= 1:
                        pe.wait_ge(s_ready, 3 * h)
                    for c in range(T - 1):
                        mm = pe.transpose(ps[:, 2, c * P:(c + 1) * P], k_end[:, c * P:(c + 1) * P], ident[:])
                    mm.then_inc(kend_turned, 1)

                def contributions(h):
                    pe.wait_ge(kend_out, h + 1)
                    if h == 0:
                        pe.wait_ge(proj_out, O_GV)
                    for c in range(T - 1):
                        cs, hs = slice(c * P, (c + 1) * P), slice(h * P, (h + 1) * P)
                        mm = pe.matmul(ps[:, 2, cs], k_endT[:, cs], gv[:, c, hs], start=True, stop=True)
                    mm.then_inc(su_mm, 1)

                def outputs(h):
                    pe.wait_ge(lev_kept, (h + 1) * LEV)
                    pe.wait_ge(s_ready, 3 * (h + 1))
                    pe.wait_ge(qe_ready, 1)
                    if h >= 1:
                        pe.wait_ge(o_gated, T * h)
                    for c in range(T):
                        cs, hs = slice(c * P, (c + 1) * P), slice(h * P, (h + 1) * P)
                        mm = pe.matmul(ps[:, 3, cs], attT[:, h % 2, cs], gv[:, c, hs], start=True, stop=(c == 0))
                        if c >= 1:
                            mm = pe.matmul(ps[:, 3, cs], q_exp[:, h, cs], state[:, h % 2, c - 1, :], start=False,
                                           stop=True)
                    mm.then_inc(o_mm, 1)

                for i in STEPS:
                    if item_at(i) is not None:
                        scores(item_at(i))
                    if item_at(i, -1) is not None:
                        turn(item_at(i, -1))
                    if item_at(i, -2) is not None:
                        values(item_at(i, -2))
                    if head_after(i, 1) is not None:
                        turn_keys(head_after(i, 1))
                    if head_after(i, 2) is not None:
                        contributions(head_after(i, 2))
                    if head_after(i, 3) is not None:
                        outputs(head_after(i, 3))
                    if level_at(i) is not None:
                        level(level_at(i))

            @block.scalar
            def _(act):
                step = stepper(act, "act", act_step)

                def exponential(i):
                    b, h = QH[i]
                    n = (b + 1) * P
                    act.wait_ge(s_masked, i + 1)
                    if i >= 2:
                        act.wait_ge(pt_done, i - 1)
                    act.activation(prob[:, i % 2, 0:n], s_neg[:, i % 2, 0:n], ACT.Exp, scale=-1.0,
                                   bias=min_neg[:, i:i + 1], accum_out=row_sum[:, i:i + 1]).then_inc(exp_done, 1)

                def copy_pt(i):
                    n = (QH[i][0] + 1) * P
                    act.wait_ge(pt_done, i + 1)
                    if i >= 2:
                        act.wait_ge(pv_done, i - 1)
                    act.activation(probT[:, i % 2, 0:n], ps[:, 6, 0:n], ACT.Copy).then_inc(pt_out, 1)

                def exp_level(n):
                    lev = n % LEV
                    act.wait_ge(diff_ready, n + 1)
                    if lev < 7:
                        half = 64 >> lev
                        d, e = blocks_of(diff[:, n % 4, :], half), blocks_of(expd[:, n % 4, :], half)
                        act.activation(e[:, :, half:], d[:, :, half:], ACT.Exp)
                        act.activation(e[:, :, :half], d[:, :, :half], ACT.Exp, scale=-1.0).then_inc(expd_ready, 1)
                    else:
                        act.activation(expd[:, n % 4, :], diff[:, n % 4, :], ACT.Exp, scale=-1.0).then_inc(expd_ready, 1)

                def copy_keys(h):
                    act.wait_ge(kend_turned, h + 1)
                    if h >= 1:
                        act.wait_ge(su_mm, h)
                    act.activation(k_endT[:], ps[:, 2, 0:3 * P], ACT.Copy).then_inc(kend_out, 1)

                for i in STEPS:
                    if item_at(i, -1) is not None:
                        copy_pt(item_at(i, -1))
                    if item_at(i) is not None:
                        exponential(item_at(i))
                    if i == EXP_B:
                        act.activation(ebcum, bcum[:], ACT.Exp).then_inc(eb_ready, 1)
                    if level_at(i, AHEAD - 1) is not None:
                        exp_level(level_at(i, AHEAD - 1))
                    if 1 <= i <= T:
                        act.activation(gv[:, i - 1, :], ps[:, 3 + i, :], ACT.Copy).then_inc(proj_out, 1)
                    if head_after(i, 1) is not None:
                        copy_keys(head_after(i, 1))
                act.wait_ge(var_ready, G_HEADS)
                act.activation(g_std[:], g_mv[:, :, :, 1], ACT.Sqrt, bias=eps[:, 0:1]).then_inc(std_ready, 1)

            @block.gpsimd
            def _(pool):
                step = stepper(pool, "pool", pool_step)
                step(pool.memset(k_lev, 0.0))
                for n in range(N_LEV):
                    h, lev = divmod(n, LEV)
                    pool.wait_ge(expd_ready, n + 1)
                    if n >= 2:
                        pool.wait_ge(lev_mm, n - 1)
                    if lev == 1 and h >= 1:
                        pool.wait_ge(kend_turned, h)
                    if lev < 7:
                        half = 64 >> lev
                        e = blocks_of(expd[:, n % 4, :], half)
                        pool.tensor_tensor(q_lev[:, n % 2, :].rearrange("p (b j) -> p b j", j=half),
                                           blocks_of(gqT[:, h, :], half)[:, :, half:], e[:, :, half:], ALU.mult)
                        pool.tensor_tensor(blocks_of(k_lev[:, n % 2, :], half)[:, :, :half],
                                           blocks_of(gkT[:, h, :], half)[:, :, :half], e[:, :, :half],
                                           ALU.mult).then_inc(lev_ready, 1)
                    else:
                        pool.tensor_tensor(k_end, gkT[:, h, :], expd[:, n % 4, :], ALU.mult).then_inc(lev_ready, 1)
                    if n == MASK_LEVEL:
                        pool.wait_ge(chosen, T - 1)
                        causal_select(pool, key_mask[:, T - 1, (T - 1) * P:], MASKED).then_inc(mask_ready, 1)
                    if 2 <= n < 2 + T:
                        c = n - 2
                        pool.wait_ge(g_norm_landed, 16)
                        pool.tensor_tensor(gr[:, c, :], gr[:, c, :], g_norm[:], ALU.mult).then_inc(sg_ready, 1)

            @block.vector
            def _(dve):
                step = stepper(dve, "dve", dve_step)

                def mask(i):
                    b, h = QH[i]
                    n = (b + 1) * P
                    if h == 0:
                        dve.wait_ge(mask_ready, b + 1)
                    dve.wait_ge(s_done, i + 1)
                    if i >= 2:
                        dve.wait_ge(exp_done, i - 1)
                    dve.tensor_tensor_reduce(out=s_neg[:, i % 2, 0:n], in0=ps[:, 4 + i % 2, 0:n], in1=key_mask[:, b, 0:n],
                                             scale=-A_DIM ** -0.5, scalar=3.0e38, op0=ALU.add, op1=ALU.min,
                                             accum_out=min_neg[:, i:i + 1]).then_inc(s_masked, 1)

                def normalise(b):
                    dve.wait_ge(pv_done, (b + 1) * A_HEADS)
                    hs = slice(b * A_HEADS, (b + 1) * A_HEADS)
                    step(dve.reciprocal(row_inv[:, hs], row_sum[:, hs]))
                    dve.tensor_tensor(cat[:, b, 0:A_HEADS * A_DIM].rearrange("p (h d) -> p h d", h=A_HEADS),
                                      ps[:, 7, :].rearrange("p (h d) -> p h d", h=A_HEADS),
                                      row_inv[:, hs].unsqueeze(2).broadcast_to([P, A_HEADS, A_DIM]),
                                      ALU.mult).then_inc(o_out, 1)

                def make_diff(n):
                    h, lev = divmod(n, LEV)
                    if n >= 4:
                        dve.wait_ge(lev_ready, n - 3)
                    half, ref = (64 >> lev, (64 >> lev) - 1) if lev < 7 else (64, 127)
                    b = blocks_of(bcum[:, h, :], half)
                    dve.tensor_tensor(blocks_of(diff[:, n % 4, :], half), b,
                                      b[:, :, ref:ref + 1].broadcast_to([P, S // (2 * half), 2 * half]),
                                      ALU.subtract).then_inc(diff_ready, 1)

                def keep(n):
                    h, lev = divmod(n, LEV)
                    dve.wait_ge(lev_mm, n + 1)
                    if lev == 0 and h >= 2:
                        dve.wait_ge(o_mm, h - 1)
                    if n == 0:
                        dve.wait_ge(attT_zero, 1)
                    else:
                        dve.wait_ge(lev_kept, n)
                    if lev < 7:
                        half = 64 >> lev
                        mask = blocks_of(level_mask[:, lev, :], half)[:, :, half:]
                        kept = attT[:, h % 2, :].rearrange("p (c b j) -> p c b j", c=T, j=2 * half)[:, :, :, half:]
                        made = ps[:, n % 2, 0:S // 2].rearrange("p (c b j) -> p c b j", c=T, j=half)
                    else:
                        mask = level_mask[:, lev, :]
                        kept = attT[:, h % 2, :].rearrange("p (c t) -> p c t", c=T)
                        made = ps[:, n % 2, :].rearrange("p (c t) -> p c t", c=T)
                    dve.copy_predicated(kept, mask.bitcast(U32).unsqueeze(1).broadcast_to(kept.shape),
                                        made).then_inc(lev_kept, 1)

                def states(h):
                    dve.wait_ge(su_mm, h + 1)
                    dve.wait_ge(eb_ready, 1)
                    if h >= 2:
                        dve.wait_ge(o_mm, h - 1)
                    for c in range(T - 1):
                        if c == 0:
                            ins = dve.tensor_copy(state[:, h % 2, 0, :], ps[:, 2, 0:P])
                        else:
                            dve.wait_ge(s_ready, h * 3 + c)
                            ins = dve.scalar_tensor_tensor(out=state[:, h % 2, c, :], in0=state[:, h % 2, c - 1, :],
                                                           scalar=ebcum[:, h, (c + 1) * P - 1:(c + 1) * P],
                                                           in1=ps[:, 2, c * P:(c + 1) * P], op0=ALU.mult, op1=ALU.add)
                        ins.then_inc(s_ready, 1)

                def moments(h):
                    dve.wait_ge(o_mm, h + 1)
                    for c in range(T):
                        ins = dve.bn_stats(g_stat[:, c, :], ps[:, 3, c * P:(c + 1) * P])
                    step(ins)
                    for c in range(T):
                        ins = dve.bn_aggr(g_mv[:, c, h, :], g_stat[:, c, :])
                    ins.then_inc(var_ready, 1)

                def gate_head(h):
                    dve.wait_ge(var_ready, h + 1)
                    dve.wait_ge(sg_ready, T)
                    for c in range(T):
                        hs = slice(h * P, (h + 1) * P)
                        dve.scalar_tensor_tensor(out=cat[:, c, WIDE + h * P:WIDE + (h + 1) * P],
                                                 in0=ps[:, 3, c * P:(c + 1) * P], scalar=g_mv[:, c, h, 0:1],
                                                 in1=gr[:, c, hs], op0=ALU.subtract, op1=ALU.mult).then_inc(o_gated, 1)

                for i in STEPS:
                    if item_at(i) is not None:
                        mask(item_at(i))
                    if i == 0:
                        for n in range(AHEAD):
                            make_diff(n)
                        dve.memset(attT[:], 0.0).then_inc(attT_zero, 1)
                    if level_at(i, AHEAD) is not None and i >= FIRST:
                        make_diff(level_at(i, AHEAD))
                    if i == Q_EXP:
                        dve.wait_ge(eb_ready, 1)
                        dve.tensor_tensor(q_exp, gqT[:], ebcum, ALU.mult).then_inc(qe_ready, 1)
                    if level_at(i) is not None:
                        keep(level_at(i))
                    if i in ROUND_STEPS:
                        topk_round(dve, step, T - 1, EARLY_ROUNDS + ROUND_STEPS.index(i))
                    if i == ROUND_STEPS[-1]:
                        topk_mask(dve, T - 1)
                    if item_at(i, -2) is not None and item_at(i, -2) % A_HEADS == A_HEADS - 1:
                        normalise(item_at(i, -2) // A_HEADS)
                    if head_after(i, 2) is not None:
                        states(head_after(i, 2))
                    if head_after(i, 4) is not None:
                        moments(head_after(i, 4))
                    if head_after(i, 5) is not None:
                        gate_head(head_after(i, 5))
        mix.close()
        dsa_in.close()

        base = n_xp[0]
        n_xp[0] += 8
        space = norm_space(gla_in, ln1_g[0:1], ln1_b[0:1])
        o_scaled = sem("o_scaled")
        with nc.Block() as block:
            @block.sync
            def _(sp):
                norm_load(sp, space)
                load_lap(sp, L_MLP0)
                load_lap(sp, L_MLP0 + 1, HEAD_KS)

            @block.tensor
            def _(pe):
                for half in range(2):
                    for t in range(T):
                        if half == 1:
                            pe.wait_ge(o_scaled, t + 1)
                        turn_half(pe, cat, t, half)
                pe.wait_ge(xp_lo, base + 8)
                lap_N(pe, L_WO, 0)
                pe.wait_ge(xp_lo, base + 8)
                by_tokens(pe, L_WO + 1, [(range(SLOTS), lambda k: xT_hi[:, k, :], lambda k: xT_lo[:, k, :], 4,
                                            lambda t: None)], space)

            @block.scalar
            def _(act):
                for half in range(2):
                    for t in range(T):
                        hi_half(act, base + 4 * half + t, t, half)
                round_lap(act, L_WO + 1)
                norm_act(act, space, L_WO + 1)

            @block.vector
            def _(dve):
                step = stepper(dve, "dve", dve_step)
                step(dve.reciprocal(g_std[:], g_std[:]))
                for c in range(T):
                    o = cat[:, c, WIDE:].rearrange("p (h d) -> p h d", h=G_HEADS)
                    dve.tensor_tensor(o, o, g_std[:, c, :].unsqueeze(2).broadcast_to([P, G_HEADS, G_DIM]),
                                      ALU.mult).then_inc(o_scaled, 1)
                for half in range(2):
                    for t in range(T):
                        lo_half(dve, base + 4 * half + t, t, half)
                split_lap(dve, L_WO + 1)
                dve.wait_ge(w_used, lap_done(L_WO))
                add_half(dve, 0, 0)
                n_added[0] += T
                norm_dve(dve, space, L_WO + 1, [(1, 4)])

            @block.gpsimd
            def _(pool):
                norm_pool(pool, space)
        n_xp[0] += 8
        gla_in.close()
        even.close()

        h_relu, h_rounded, h_sq, h_ready = sem("h_relu"), sem("h_rounded"), sem("h_sq"), sem("h_ready")
        n_mlp = [0]

        def mlp_stage(layer, L0, final=False, with_pool=None):
            own = ExitStack()
            space = norm_space(own, ln2_g[layer:layer + 1], ln2_b[layer:layer + 1])
            m = n_mlp[0]
            r_buf = sbuf(own, f"r_buf{m}", [P, 4, S])
            h_hi = sbuf(own, f"h_hi{m}", [P, 2, 4, S], F32R)
            h_lo = sbuf(own, f"h_lo{m}", [P, 2, 4, S], F32R)
            HB = m * CH * 4
            AB = n_added[0]
            up = lambda c: L0 + 2 * c - 1
            down = lambda c: L0 + 2 * c + 2
            last = CH - 1
            DOWN_LAST = L0 + 2 * CH - 1
            assert CH % 2 == 0

            with nc.Block() as block:
                @block.sync
                def _(sp):
                    load_lap(sp, L0 + 1, TAIL_KS)
                    norm_load(sp, space)
                    with sp.Fori(0, CH - 2) as c:
                        for k in range(SLOTS):
                            load_tile(sp, down(c), k, row_lap(mlp_w2[layer], c * WIDE)(k))
                        for k in range(SLOTS):
                            load_tile(sp, up(c + 2), k, up_lap(layer, c + 2)(k))
                    for lap in (down(CH - 2), DOWN_LAST, DOWN_LAST + 1):
                        load_lap(sp, lap)
                    load_lap(sp, DOWN_LAST + 2, HEAD_KS)
                    if final:
                        norm_store(sp, space)

                @block.tensor
                def _(pe):
                    def up_chunk(c, lap, bank0):
                        for k in range(SLOTS):
                            pe.wait_ge(w_split, lap * SLOTS + k + 1)
                            tile_T(pe, k, xT_hi[:, k, :], xT_lo[:, k, :], full_banks(bank0), k == 0, k == SLOTS - 1)

                    def down_chunk(c, lap, par, bank_left, left_free, right_free):
                        pe.wait_ge(h_ready, HB + c * 4 + 4)
                        lap_rows(pe, lap, lambda kk: h_hi[:, par, kk, :], lambda kk: h_lo[:, par, kk, :],
                                 bank_left, 4 - bank_left, left_free, right_free)

                    def both(c, par, first=False):
                        if not first:
                            pe.wait_ge(added, AB + (c - 1) * 8 + 4)
                        up_chunk(c + 1, up(c + 1), 4 - 4 * par)
                        down_chunk(c, down(c), par, 4 * par,
                                   (lambda: None) if first else (lambda: pe.wait_ge(added, AB + c * 8)),
                                   lambda: pe.wait_ge(h_relu, HB + c * 4 + 8))

                    pe.wait_ge(xp_lo, n_xp[0])
                    up_chunk(0, L0, 0)
                    both(0, 0, first=True)
                    with pe.Fori(0, CH // 2 - 1) as i:
                        both(i * 2 + 1, 1)
                        both(i * 2 + 2, 0)
                    pe.wait_ge(h_ready, HB + last * 4 + 4)
                    pe.wait_ge(added, AB + last * 8 - 4)
                    h_parts = (lambda kk: h_hi[:, 1, kk, :], lambda kk: h_lo[:, 1, kk, :])
                    by_tokens(pe, DOWN_LAST, [(range(4), *h_parts, 0, lambda t: None),
                                              (range(4, 8), *h_parts, 4,
                                               lambda t: pe.wait_ge(added, AB + last * 8 - 3 + t))], space, final)

                @block.scalar
                def _(act):
                    def squares(c, lap, par, bank0, deep=True):
                        act.wait_ge(w_used, lap * SLOTS + SLOTS)
                        act.wait_ge(h_ready, HB + c * 4) if not isinstance(c, int) or HB + c else None
                        for j in range(4):
                            act.activation(r_buf[:, j, :], ps[:, bank0 + j, :], ACT.Relu).then_inc(h_relu, 1)
                        if deep:
                            act.wait_ge(w_used, (lap - 1) * SLOTS)
                        for j in range(4):
                            act.wait_ge(h_relu, HB + c * 4 + j + 1)
                            act.activation(h_hi[:, par, j, :], r_buf[:, j, :], ACT.Square).then_inc(h_rounded, 1)

                    def both(c, par):
                        round_lap(act, down(c))
                        squares(c + 1, up(c + 1), 1 - par, 4 - 4 * par)
                        round_lap(act, up(c + 2))

                    round_lap(act, L0, TAIL_KS)
                    round_lap(act, L0 + 1)
                    squares(0, L0, 0, 0, deep=False)
                    both(0, 0)
                    with act.Fori(0, CH // 2 - 1) as i:
                        both(i * 2 + 1, 1)
                        both(i * 2 + 2, 0)
                    norm_act(act, space, DOWN_LAST, final)

                @block.vector
                def _(dve):
                    def rest(c, par):
                        for j in range(4):
                            dve.wait_ge(h_rounded, HB + c * 4 + j + 1)
                            dve.tensor_tensor(r_buf[:, j, :], r_buf[:, j, :], r_buf[:, j, :], ALU.mult).then_inc(h_sq, 1)
                        for j in range(4):
                            dve.wait_ge(h_sq, HB + c * 4 + j + 1)
                            dve.tensor_tensor(h_lo[:, par, j, :], r_buf[:, j, :], h_hi[:, par, j, :].bitcast(F32),
                                              ALU.subtract).then_inc(h_ready, 1)

                    def add_down(half, lap, bank0):
                        dve.wait_ge(w_used, lap * SLOTS + 4 + 4 * half)
                        add_half(dve, half, bank0)

                    def both(c, par):
                        split_lap(dve, down(c))
                        rest(c + 1, 1 - par)
                        split_lap(dve, up(c + 2), range(4))
                        add_down(0, down(c), 4 * par)
                        split_lap(dve, up(c + 2), range(4, 8))
                        add_down(1, down(c), 4 - 4 * par)

                    split_lap(dve, L0, TAIL_KS)
                    split_lap(dve, L0 + 1)
                    rest(0, 0)
                    both(0, 0)
                    with dve.Fori(0, CH // 2 - 1) as i:
                        both(i * 2 + 1, 1)
                        both(i * 2 + 2, 0)
                    n_added[0] += 8 * last
                    norm_dve(dve, space, DOWN_LAST, [(0, 0), (1, 4)], final)

                @block.gpsimd
                def _(pool):
                    if with_pool:
                        with_pool(pool)
                    norm_pool(pool, space)
            own.close()
            n_mlp[0] += 1
            if not final:
                n_xp[0] += 8

        odd = ExitStack()
        NC = INNER // P
        OFF = [sum((T - j) * P for j in range(i)) for i in range(T)]
        wts = sbuf(odd, "wts", [P, OFF[-1] + P])
        hg = sbuf(odd, "hg", [P, T, DH])
        conv_w = sbuf(odd, "conv_w", [P, M_CONV, NC])
        conv_b = sbuf(odd, "conv_b", [P, NC])
        skip_c = sbuf(odd, "skip_c", [P, NC])
        norm_c = sbuf(odd, "norm_c", [P, NC])
        gate_b = sbuf(odd, "gate_b", [36, 1])
        N_BLK = NC * M_BLK
        blk = wts[:, 0:3 * N_BLK].rearrange("p (i t e) -> p i t e", i=3, t=NC)
        k_rows = wts[:, 3 * N_BLK:3 * N_BLK + N_BLK * M_BLK].rearrange("p (t r) -> p t r", t=NC)
        g_rows = hg[:, 0:3, :].rearrange("p i (t r) -> p i t r", t=NC)
        g_prod = hg[:, 3, :].rearrange("p (t g e) -> p t g e", t=NC, e=M_BLK)
        assert (3 + M_BLK) * N_BLK <= OFF[-1] + P
        od_params = sem("od_params")
        N_PARAMS = 28

        def load_params(pool):
            n_params = [0]

            def param(dst, src):
                with nc.allow_non_contiguous_dma("small parameters, by channel"):
                    pool.dma_start(dst, src).then_inc(od_params, 16)
                n_params[0] += 1
            for i, w in enumerate((od_w_q, od_w_k, od_w_v)):
                param(blk[:, i, :, :], w[0].rearrange("(t j) d e -> (j d) t e", t=NC))
            for d in range(M_CONV):
                param(conv_w[:, d, :], od_conv_w[0, d].rearrange("(t p) -> p t", p=P))
            param(conv_b[:], od_conv_b[0].rearrange("(t p) -> p t", p=P))
            param(skip_c[:], od_skip[0].rearrange("(t p) -> p t", p=P))
            param(norm_c[:], od_norm[0].rearrange("h (t p) -> p (h t)", p=P))
            param(gate_b[0:4, :], od_b_gate[0, 0:4].rearrange("(g o) -> g o", o=1))
            param(gate_b[32:36, :], od_b_gate[0, 4:8].rearrange("(g o) -> g o", o=1))
            for d in range(M_BLK):
                for i in range(3):
                    param(g_rows[d:P:M_BLK, i, :, :], od_w_gate[0, i * INNER:(i + 1) * INNER].rearrange(
                        "(t j e) g -> j t (e g)", t=NC, e=M_BLK))
                param(k_rows[d:P:M_BLK, :, :], od_w_k[0].rearrange("(t j) d e -> j t (d e)", t=NC))
            assert n_params[0] == N_PARAMS

        mlp_stage(0, L_MLP0, with_pool=load_params)

        xcT = sbuf(odd, "xcT", [P, NC, S])
        val = sbuf(odd, "val", [P, T, INNER])
        qk_blk = sbuf(odd, "qk_blk", [P, NC, M_BLK])
        bd_mask = sbuf(odd, "bd_mask", [P, P // M_BLK, M_BLK])
        neg_all = sbuf(odd, "neg_all", [P, S])
        gate_x = neg_all[0:36, :]
        pre = ExitStack()
        xm = sbuf(pre, "xm", [P, 2, CT, M_CONV - 1 + S])
        conv = sbuf(pre, "conv", [P, 2, S])
        bd_v = sbuf(pre, "bd_v", [P, 2, P])
        g_fold = sbuf(pre, "g_fold", [P, 2, NC, 8])
        g_mat = sbuf(pre, "g_mat", [P, 2, NC, 36])
        od_zero, fold_done = sem("od_zero"), sem("fold_done")
        xm_out, conv0, conv_done, xc_ready = sem("xm_out"), sem("conv0"), sem("conv_done"), sem("xc_ready")
        bd_ready, v_mm, v_out, gates_mm, gate_out = (sem("bd_ready"), sem("v_mm"), sem("v_out"), sem("gates_mm"),
                                                     sem("gate_out"))
        PAD = M_CONV - 1
        with nc.Block() as block:
            @block.sync
            def _(sp):
                load_lap(sp, L_XM + 1, TAIL_KS)
                for lap in range(L_XM + 2, L_GATE[0] + 2):
                    load_lap(sp, lap)

            @block.gpsimd
            def _(pool):
                step = stepper(pool, "pool", pool_step)
                pool.memset(xm[:, :, :, 0:PAD], 0.0).then_inc(od_zero, 1)
                pool.memset(g_mat[:], 0.0).then_inc(od_zero, 1)
                step(pool.memset(bd_mask[:], 1.0))
                step(pool.affine_select(out=bd_mask[:], in_=bd_mask[:], compare_op=ALU.is_ge, fill=0.0, base=0,
                                        pattern=[[-M_BLK, P // M_BLK], [0, M_BLK]], channel_multiplier=1))
                step(pool.affine_select(out=bd_mask[:], in_=bd_mask[:], compare_op=ALU.is_ge, fill=0.0, base=M_BLK - 1,
                                        pattern=[[M_BLK, P // M_BLK], [0, M_BLK]], channel_multiplier=-1))
                pool.wait_ge(od_params, 16 * N_PARAMS)
                for ct in range(NC):
                    if ct >= 2:
                        pool.wait_ge(v_mm, ct - 1)
                    pool.tensor_tensor(bd_v[:, ct % 2, :].rearrange("p (j e) -> p j e", e=M_BLK), bd_mask[:],
                                       blk[:, 2, ct, :].unsqueeze(1).broadcast_to([P, P // M_BLK, M_BLK]),
                                       ALU.mult).then_inc(bd_ready, 1)

            @block.tensor
            def _(pe):
                def from_group(g):
                    for j in range(CT):
                        ct = g * CT + j
                        pe.wait_ge(bd_ready, ct + 1)
                        if ct >= 3:
                            pe.wait_ge(v_out, ct - 2)
                        for t in range(T):
                            mm = pe.matmul(ps[:, 4 + ct % 3, t * P:(t + 1) * P],
                                           xm[:, g % 2, j, PAD + t * P:PAD + (t + 1) * P], bd_v[:, ct % 2, :],
                                           start=True, stop=True)
                        mm.then_inc(v_mm, 1)
                        if ct == 0:
                            pe.wait_ge(fold_done, 2)
                        pe.matmul(ps[0:36, 7, :], g_mat[:, 1, ct, :], xm[:, g % 2, j, PAD:], start=(ct == 0), stop=False)
                    for j in range(CT):
                        ct = g * CT + j
                        pe.wait_ge(xc_ready, ct + 1)
                        mm = pe.matmul(ps[0:36, 7, :], g_mat[:, 0, ct, :], xcT[:, ct, :], start=False,
                                       stop=(ct == NC - 1))
                    mm.then_inc(gates_mm, 1)

                pe.wait_ge(xp_lo, n_xp[0])
                for g in range(M_HEADS):
                    if g >= 1:
                        pe.wait_ge(xm_out, CT * g)
                    lap_T(pe, L_XM + g, full_banks(0))
                    if g >= 1:
                        from_group(g - 1)
                pe.wait_ge(xm_out, CT * M_HEADS)
                from_group(M_HEADS - 1)

            @block.scalar
            def _(act):
                def silu(ct):
                    act.wait_ge(conv_done, ct + 1)
                    act.activation(xcT[:, ct, :], conv[:, ct % 2, :], ACT.Silu).then_inc(xc_ready, 1)

                round_lap(act, L_XM, TAIL_KS)
                for g in range(M_HEADS):
                    round_lap(act, L_XM + g + 1)
                    act.wait_ge(w_used, lap_done(L_XM + g))
                    if g == 0:
                        act.wait_ge(od_zero, 2)
                        act.wait_ge(od_params, 16 * N_PARAMS)
                    if g >= 2:
                        act.wait_ge(gates_mm, g - 1)
                        act.wait_ge(conv_done, CT * (g - 1))
                    for j in range(CT):
                        act.activation(xm[:, g % 2, j, PAD:], ps[:, j, :], ACT.Copy).then_inc(xm_out, 1)
                    for j in range(CT):
                        ct = g * CT + j
                        if ct >= 2:
                            act.wait_ge(xc_ready, ct - 1)
                        act.wait_ge(xm_out, ct + 1)
                        act.activation(conv[:, ct % 2, :], xm[:, g % 2, j, PAD:], ACT.Identity, bias=conv_b[:, ct:ct + 1],
                                       scale=conv_w[:, PAD, ct:ct + 1]).then_inc(conv0, 1)
                        if j >= 1:
                            silu(ct - 1)
                    silu(g * CT + CT - 1)
                act.wait_ge(gates_mm, M_HEADS)
                act.activation(gate_x[0:36, :], ps[0:36, 7, :], ACT.Copy).then_inc(gate_out, 1)

            @block.vector
            def _(dve):
                step = stepper(dve, "dve", dve_step)
                def values_out(ct):
                    dve.wait_ge(v_mm, ct + 1)
                    dve.tensor_copy(val[:, :, ct * P:(ct + 1) * P], bank_as_tiles(4 + ct % 3)).then_inc(v_out, 1)

                split_lap(dve, L_XM, TAIL_KS)
                dve.wait_ge(od_params, 16 * N_PARAMS)
                dve.wait_ge(od_zero, 2)
                qk_prod = g_prod[:, :, 0:M_BLK, :]
                step(dve.tensor_tensor(qk_prod, blk[:, 0, :, :].unsqueeze(2).broadcast_to([P, NC, M_BLK, M_BLK]),
                                       k_rows.rearrange("p t (d e) -> p t d e", e=M_BLK), ALU.mult))
                step(dve.tensor_reduce(qk_blk[:], qk_prod, AX.X, ALU.add))
                for i in range(3):
                    step(dve.tensor_tensor(g_prod, blk[:, i, :, :].unsqueeze(2).broadcast_to([P, NC, 8, M_BLK]),
                                           g_rows[:, i, :, :].rearrange("p t (e g) -> p t g e", e=M_BLK), ALU.mult))
                    step(dve.tensor_reduce(g_fold[:, min(i, 1), :, :], g_prod, AX.X, ALU.add))
                    if i == 1:
                        step(dve.tensor_tensor(g_fold[:, 0, :, :], g_fold[:, 0, :, :], g_fold[:, 1, :, :], ALU.add))
                dve.tensor_copy(g_mat[:, :, :, 0:4], g_fold[:, :, :, 0:4]).then_inc(fold_done, 1)
                dve.tensor_copy(g_mat[:, :, :, 32:36], g_fold[:, :, :, 4:8]).then_inc(fold_done, 1)
                for g in range(M_HEADS):
                    split_lap(dve, L_XM + g + 1)
                    for j in range(CT):
                        ct = g * CT + j
                        if g >= 1:
                            values_out(ct - CT)
                        dve.wait_ge(conv0, ct + 1)
                        for tap in range(PAD):
                            ins = dve.scalar_tensor_tensor(out=conv[:, ct % 2, :], in0=xm[:, g % 2, j, tap:tap + S],
                                                           scalar=conv_w[:, tap, ct:ct + 1], in1=conv[:, ct % 2, :],
                                                           op0=ALU.mult, op1=ALU.add)
                            if tap < PAD - 1:
                                step(ins)
                        ins.then_inc(conv_done, 1)
                for ct in range(NC - CT, NC):
                    values_out(ct)
        pre.close()

        rows = ExitStack()
        a_col = sbuf(odd, "a_col", [P, 2, T, M_HEADS])
        neg_M = sbuf(odd, "neg_M", [4, S])
        above = sbuf(odd, "above", [P, P])
        i_row = sbuf(rows, "i_row", [4, S])
        f_rows = sbuf(rows, "f_rows", [36, 2, S])
        lf_row = sbuf(rows, "lf_row", [4, S])
        b_row = sbuf(rows, "b_row", [4, S])
        a_row = sbuf(rows, "a_row", [4, S])
        m_row = sbuf(rows, "m_row", [4, S])
        m_max = sbuf(rows, "m_max", [4, S])
        one_row = sbuf(rows, "one_row", [4, S])
        f_ready, row_const, a_ready, em_ready, m_done, cols_done = (sem("f_ready"), sem("row_const"), sem("a_ready"),
                                                                    sem("em_ready"), sem("m_done"), sem("cols_done"))
        sig_ready = sem("sig_ready")
        with nc.Block() as block:
            @block.sync
            def _(sp):
                load_lap(sp, L_GATE[0] + 2)

            @block.gpsimd
            def _(pool):
                step = stepper(pool, "pool", pool_step)
                pool.memset(one_row[:], 1.0).then_inc(row_const, 1)
                step(pool.memset(above[:], 0.0))
                step(pool.affine_select(out=above[:], in_=above[:], compare_op=ALU.is_ge, fill=MASKED, base=0,
                                        pattern=[[1, P]], channel_multiplier=-1))

            @block.scalar
            def _(act):
                step = stepper(act, "act", act_step)
                act.activation(i_row[:], gate_x[0:4, :], ACT.Identity, bias=gate_b[0:4, :])
                step(act.activation(f_rows[32:36, 0, :], gate_x[32:36, :], ACT.Identity, bias=gate_b[32:36, :]))
                step(act.activation(f_rows[32:36, 1, :], f_rows[32:36, 0, :], ACT.Abs))
                step(act.activation(f_rows[32:36, 1, :], f_rows[32:36, 1, :], ACT.Exp, scale=-1.0))
                act.activation(f_rows[32:36, 1, :], f_rows[32:36, 1, :], ACT.Ln, bias=1.0).then_inc(f_ready, 1)
                act.wait_ge(m_done, 1)
                act.activation(m_row[:], m_row[:], ACT.Exp, scale=-1.0).then_inc(em_ready, 1)
                round_lap(act, L_GATE[0] + 1)

            @block.vector
            def _(dve):
                step = stepper(dve, "dve", dve_step)
                dve.wait_ge(f_ready, 1)
                dve.wait_ge(row_const, 1)
                step(dve.scalar_tensor_tensor(out=lf_row[:], in0=f_rows[32:36, 0, :], scalar=0.0,
                                              in1=f_rows[32:36, 1, :], op0=ALU.min, op1=ALU.subtract))
                step(dve.tensor_tensor_scan(b_row[:], one_row[:], lf_row[:], 0.0, ALU.mult, ALU.add))
                dve.tensor_tensor(a_row[:], i_row[:], b_row[:], ALU.subtract).then_inc(a_ready, 1)
                dve.wait_ge(a_ready, 1)
                step(dve.tensor_tensor_scan(m_max[:], a_row[:], a_row[:], 0.0, ALU.max, ALU.max))
                step(dve.tensor_tensor(m_row[:], b_row[:], m_max[:], ALU.add))
                dve.tensor_scalar(neg_M[:], m_max[:], -1.0, None, ALU.mult).then_inc(m_done, 1)
                split_lap(dve, L_GATE[0] + 1)
                dve.wait_ge(cols_done, 1)
                step(dve.tensor_copy(a_col[:].rearrange("p a t h -> p (a t h)"), ps[:, 0, 0:2 * T * M_HEADS]))

            @block.tensor
            def _(pe):
                lap_N(pe, L_GATE[0], 4)
                pe.wait_ge(a_ready, 1)
                for t in range(T):
                    pe.transpose(ps[:, 0, t * 4:t * 4 + 4], a_row[:, t * P:(t + 1) * P], ident[0:4, 0:4])
                pe.wait_ge(em_ready, 1)
                for t in range(T):
                    mm = pe.transpose(ps[:, 0, (T + t) * 4:(T + t) * 4 + 4], m_row[:, t * P:(t + 1) * P],
                                      ident[0:4, 0:4])
                mm.then_inc(cols_done, 1)
        rows.close()

        heads = ExitStack()
        bd_qk = sbuf(heads, "bd_qk", [P, CT, P])
        zT = sbuf(heads, "zT", [P, CT, S])
        den = sbuf(heads, "den", [P, 2, T])
        h_stat = sbuf(heads, "h_stat", [P, T, 6])
        h_mv = sbuf(heads, "h_mv", [P, T, 2])
        h_std = sbuf(heads, "h_std", [P, T])
        y_hi = sbuf(heads, "y_hi", [P, CT, S], F32R)
        y_lo = sbuf(heads, "y_lo", [P, CT, S], F32R)
        bdqk_ready, z_mm, z_out, m_bc, m_bc_out = (sem("bdqk_ready"), sem("z_mm"), sem("z_out"), sem("m_bc"),
                                                   sem("m_bc_out"))
        diag_ready, wexp, dot_mm, w_ready = sem("diag_ready"), sem("wexp"), sem("dot_mm"), sem("w_ready")
        den_mm, den_ready, num_mm, h_gated, h_var, h_stdr, h_normed = (
            sem("den_mm"), sem("den_ready"), sem("num_mm"), sem("h_gated"), sem("h_var"), sem("h_stdr"),
            sem("h_normed"))
        hT_mm, xs_ready, y_f32, y_rounded, y_ready = (sem("hT_mm"), sem("xs_ready"), sem("y_f32"), sem("y_rounded"),
                                                      sem("y_ready"))
        AB = n_added[0]
        near = lambda h: 4 if h % 2 == 0 else 0
        far = lambda h: 4 - near(h)
        LAST = M_HEADS - 1
        SOONER, LATER = range(SLOTS - 2), range(SLOTS - 2, SLOTS)
        space = norm_space(heads, ln1_g[1:2], ln1_b[1:2], val[:, 0, 0:D], val[:, 1, 0:D])
        assert 2 * DH >= D
        with nc.Block() as block:
            @block.sync
            def _(sp):
                for lap in range(L_GATE[0] + 3, L_MLP1 + 1):
                    if lap == L_PROJ[2]:
                        sp.wait_ge(num_mm, 2 * T)
                        norm_load(sp, space)
                    load_lap(sp, lap)
                load_lap(sp, L_MLP1 + 1, HEAD_KS)

            @block.gpsimd
            def _(pool):
                for h in range(M_HEADS):
                    for j in range(CT):
                        if h >= 1:
                            pool.wait_ge(z_mm, CT * (h - 1) + j + 1)
                        pool.tensor_tensor(
                            bd_qk[:, j, :].rearrange("p (j e) -> p j e", e=M_BLK), bd_mask[:],
                            qk_blk[:, h * CT + j, :].unsqueeze(1).broadcast_to([P, P // M_BLK, M_BLK]),
                            ALU.mult).then_inc(bdqk_ready, 1)
                norm_pool(pool, space)

            @block.tensor
            def _(pe):
                def start(h):
                    this_head = ident[0:M_HEADS, h:h + 1].broadcast_to([M_HEADS, P])
                    pe.matmul(ps[:, far(h) + 3, :], this_head, neg_M[:], start=True, stop=True).then_inc(m_bc, 1)
                    for j in range(CT):
                        pe.wait_ge(bdqk_ready, h * CT + j + 1)
                        if j == 3:
                            pe.wait_ge(m_bc_out, h + 1)
                        pe.matmul(ps[:, far(h) + j, :], bd_qk[:, j, :], xcT[:, h * CT + j, :],
                                  start=True, stop=True).then_inc(z_mm, 1)

                def dots(h):
                    pe.wait_ge(z_out, CT * (h + 1))
                    for i in range(T):
                        n = (T - i) * P
                        for j in range(CT):
                            mm = pe.matmul(ps[:, far(h) + i, 0:n], xcT[:, h * CT + j, i * P:(i + 1) * P],
                                           zT[:, j, i * P:], start=(j == 0), stop=(j == CT - 1))
                        mm.then_inc(dot_mm, 1)

                def lhs(i, t):
                    return wts[:, OFF[i] + (t - i) * P:OFF[i] + (t - i + 1) * P]

                def numerators(h):
                    pe.wait_ge(w_ready, T * (h + 1))
                    for t in range(T):
                        for i in range(t + 1):
                            mm = pe.matmul(ps[:, far(h), t:t + 1], lhs(i, t), ones[:, 0:1], start=(i == 0), stop=(i == t))
                    mm.then_inc(den_mm, 1)
                    if h == 0:
                        pe.wait_ge(sig_ready, T)
                    for t in range(T):
                        for i in range(t + 1):
                            mm = pe.matmul(ps[:, near(h) + t, :], lhs(i, t), val[:, i, h * DH:(h + 1) * DH],
                                           start=(i == 0), stop=(i == t))
                        mm.then_inc(num_mm, 1)

                def turn(h):
                    pe.wait_ge(h_gated, T * (h + 1))
                    pairs = ([(j, t) for j in range(CT) for t in range(T)] if h < LAST
                             else [(j, t) for t in range(T) for j in range(CT)])
                    for j, t in pairs:
                        pe.wait_ge(h_normed, T * h + (t + 1 if h == LAST else T))
                        if h < LAST:
                            pe.wait_ge(z_out, CT * (h + 1) + j + 1)
                        mm = pe.transpose(ps[:, near(h) + j, t * P:(t + 1) * P], hg[:, t, j * P:(j + 1) * P], ident[:])
                        if t == T - 1:
                            mm.then_inc(hT_mm, 1)

                def project(h):
                    pe.wait_ge(y_f32, CT * (h + 1))

                    for half, bank0 in ((0, near(h)), (1, far(h))):
                        if half:
                            pe.wait_ge(sig_ready, T * (h + 2))
                        for kk in range(4):
                            if half == 0:
                                pe.wait_ge(y_ready, CT * h + kk + 1)
                            pe.wait_ge(w_split, L_PROJ[h] * SLOTS + half * 4 + kk + 1)
                            tile_N(pe, half * 4 + kk, y_hi[:, kk, :], y_lo[:, kk, :], bank0, kk == 0, kk == 3)

                start(0)
                dots(0)
                for h in range(M_HEADS):
                    numerators(h)
                    if h < LAST:
                        pe.wait_ge(den_ready, h + 1)
                        lap_N(pe, L_GATE[h + 1], far(h), SOONER)
                        pe.wait_ge(h_gated, T * (h + 1))
                        start(h + 1)
                    turn(h)
                    if h < LAST:
                        lap_N(pe, L_GATE[h + 1], far(h), LATER)
                        project(h)
                        pe.wait_ge(added, AB + 8 * h + 4)
                        dots(h + 1)
                        pe.wait_ge(added, AB + 8 * (h + 1))
                y_parts = (lambda kk: y_hi[:, kk, :], lambda kk: y_lo[:, kk, :])
                by_tokens(pe, L_PROJ[LAST], [(range(4), *y_parts, near(LAST),
                                              lambda t: pe.wait_ge(y_f32, CT * LAST + t + 1)),
                                             (range(4, 8), *y_parts, far(LAST), lambda t: None)], space,
                          operand_ready=lambda kk: pe.wait_ge(y_ready, CT * LAST + kk + 1))

            @block.scalar
            def _(act):
                def start(h):
                    act.wait_ge(m_bc, h + 1)
                    act.activation(neg_all[:], ps[:, far(h) + 3, :], ACT.Copy).then_inc(m_bc_out, 1)
                    for j in range(CT):
                        act.wait_ge(z_mm, CT * h + j + 1)
                        act.activation(zT[:, j, :], ps[:, far(h) + j, :], ACT.Copy).then_inc(z_out, 1)

                def exponentials(h):
                    for i in range(T):
                        act.wait_ge(diag_ready, T * h + i + 1)
                        bias = a_col[:, 0, i, h:h + 1]
                        if i < T - 1:
                            act.activation(wts[:, OFF[i] + P:OFF[i] + (T - i) * P], neg_all[:, (i + 1) * P:], ACT.Exp,
                                           bias=bias)
                        act.activation(wts[:, OFF[i]:OFF[i] + P], wts[:, OFF[i]:OFF[i] + P], ACT.Exp, bias=bias).then_inc(wexp, 1)

                start(0)
                exponentials(0)
                act.wait_ge(w_used, lap_done(L_GATE[0]))
                for t in range(T):
                    act.activation(hg[:, t, :], ps[:, near(0) + t, :], ACT.Sigmoid).then_inc(sig_ready, 1)
                for h in range(M_HEADS):
                    act.wait_ge(dot_mm, T * (h + 1))
                    for j in range(CT):
                        ct = h * CT + j
                        act.activation(xcT[:, ct, :], xcT[:, ct, :], ACT.Copy, scale=skip_c[:, ct:ct + 1]).then_inc(xs_ready, 1)
                    for t in range(T):
                        act.wait_ge(h_var, T * h + t + 1)
                        act.activation(h_std[:, t:t + 1], h_mv[:, t, 1:2], ACT.Sqrt, bias=eps[:, 0:1]).then_inc(h_stdr, 1)
                    if h < LAST:
                        round_lap(act, L_PROJ[h], SOONER)
                        start(h + 1)
                    for j in range(CT):
                        act.wait_ge(y_f32, CT * h + j + 1)
                        act.activation(y_hi[:, j, :], hg[:, j, :], ACT.Copy).then_inc(y_rounded, 1)
                    if h < LAST:
                        round_lap(act, L_PROJ[h], LATER)
                        act.wait_ge(y_ready, CT * (h + 1))
                        act.wait_ge(w_used, lap_done(L_GATE[h + 1]))
                        for t in range(T):
                            act.activation(hg[:, t, :], ps[:, far(h) + t, :], ACT.Sigmoid).then_inc(sig_ready, 1)
                        exponentials(h + 1)
                        round_lap(act, L_PROJ[h] + 1)
                norm_act(act, space, L_PROJ[LAST])

            @block.vector
            def _(dve):
                step = stepper(dve, "dve", dve_step)

                def diagonals(h):
                    dve.wait_ge(m_bc_out, h + 1)
                    for i in range(T):
                        dve.tensor_tensor(wts[:, OFF[i]:OFF[i] + P], neg_all[:, i * P:(i + 1) * P], above[:],
                                          ALU.add).then_inc(diag_ready, 1)

                def weights(h):
                    for i in range(T):
                        n = (T - i) * P
                        dve.wait_ge(wexp, T * h + i + 1)
                        dve.wait_ge(dot_mm, T * h + i + 1)
                        w = wts[:, OFF[i]:OFF[i] + n]
                        dve.scalar_tensor_tensor(out=w, in0=ps[:, far(h) + i, 0:n], scalar=DH ** -0.5, in1=w,
                                                 op0=ALU.mult, op1=ALU.mult).then_inc(w_ready, 1)

                def standardise(h, t):
                    dve.wait_ge(h_var, T * h + t + 1)
                    dve.wait_ge(h_stdr, T * h + t + 1)
                    step(dve.reciprocal(h_std[:, t:t + 1], h_std[:, t:t + 1]))
                    dve.tensor_scalar(hg[:, t, :], hg[:, t, :], h_mv[:, t, 0:1], h_std[:, t:t + 1],
                                      ALU.subtract, ALU.mult).then_inc(h_normed, 1)

                def make_y(h, j):
                    ct = h * CT + j
                    dve.scalar_tensor_tensor(out=hg[:, j, :], in0=ps[:, near(h) + j, :], scalar=norm_c[:, ct:ct + 1],
                                             in1=xcT[:, ct, :], op0=ALU.mult, op1=ALU.add).then_inc(y_f32, 1)

                def split_y(h, j):
                    dve.wait_ge(y_rounded, CT * h + j + 1)
                    dve.tensor_tensor(y_lo[:, j, :], hg[:, j, :], y_hi[:, j, :].bitcast(F32),
                                      ALU.subtract).then_inc(y_ready, 1)

                diagonals(0)
                weights(0)
                for h in range(M_HEADS):
                    dve.wait_ge(den_mm, h + 1)
                    step(dve.tensor_scalar(den[:, 0, :], ps[:, far(h), 0:T], -1.0, None, ALU.mult))
                    ins = dve.tensor_tensor(den[:, 0, :], ps[:, far(h), 0:T], den[:, 0, :], ALU.max)
                    ins.then_inc(den_ready, 1)
                    dve.wait_ge(den_ready, h + 1)
                    step(dve.tensor_tensor(den[:, 0, :], den[:, 0, :], a_col[:, 1, :, h], ALU.max))
                    step(dve.reciprocal(den[:, 1, :], den[:, 0, :]))
                    dve.wait_ge(sig_ready, T * (h + 1))
                    for t in range(T):
                        dve.wait_ge(num_mm, T * h + t + 1)
                        dve.scalar_tensor_tensor(out=hg[:, t, :], in0=ps[:, near(h) + t, :], scalar=den[:, 1, t:t + 1],
                                                 in1=hg[:, t, :], op0=ALU.mult, op1=ALU.mult).then_inc(h_gated, 1)
                        dve.wait_ge(h_gated, T * h + t + 1)
                        step(dve.bn_stats(h_stat[:, t, :], hg[:, t, :]))
                        dve.bn_aggr(h_mv[:, t, :], h_stat[:, t, :]).then_inc(h_var, 1)
                        if t >= 1:
                            standardise(h, t - 1)
                    standardise(h, T - 1)
                    if h < LAST:
                        split_lap(dve, L_PROJ[h], SOONER)
                        diagonals(h + 1)
                    dve.wait_ge(xs_ready, CT * (h + 1))
                    dve.wait_ge(hT_mm, CT * (h + 1))
                    make_y(h, 0)
                    make_y(h, 1)
                    split_y(h, 0)
                    for j in range(2, CT):
                        make_y(h, j)
                    for j in range(1, CT):
                        split_y(h, j)
                    if h < LAST:
                        split_lap(dve, L_PROJ[h], LATER)
                    if h < LAST:
                        lap = L_PROJ[h]
                        split_lap(dve, lap + 1, range(4))
                        dve.wait_ge(w_used, lap * SLOTS + 4)
                        add_half(dve, 0, near(h))
                        split_lap(dve, lap + 1, range(4, 8))
                        dve.wait_ge(w_used, lap * SLOTS + 8)
                        add_half(dve, 1, far(h))
                        weights(h + 1)
                n_added[0] += 8 * LAST
                norm_dve(dve, space, L_PROJ[LAST], [(0, near(LAST)), (1, far(LAST))])
        n_xp[0] += 8
        heads.close()
        odd.close()

        mlp_stage(1, L_MLP1, final=True)


_INS = ["x", "ev_w_in", "ev_g_w2", "ev_g_b2", "ev_g_norm", "ev_w_out", "od_w_in", "od_conv_w", "od_conv_b",
        "od_w_q", "od_w_k", "od_w_v", "od_w_gate", "od_b_gate", "od_skip", "od_norm", "od_w_out",
        "ln1_g", "ln1_b", "ln2_g", "ln2_b", "mlp_w1", "mlp_w2"]


def kernel(**inputs):
    import numpy as _np
    import concourse.bacc as _bacc
    from concourse import mybir as _mybir
    from concourse.bass_utils import run_bass_kernel_spmd as _run

    nc = _bacc.Bacc("TRN2", target_bir_lowering=False, num_devices=1)
    arrays, args = {}, []
    for name in _INS:
        a = _np.ascontiguousarray(inputs[name])
        arrays[f"in_{name}"] = a
        args.append(nc.dram_tensor(f"in_{name}", a.shape, _mybir.dt.from_np(a.dtype), kind="ExternalInput").ap())
    shape = tuple(inputs["x"].shape)
    args.append(nc.dram_tensor("out_0", shape, _mybir.dt.float32, kind="ExternalOutput").ap())
    hybrid_trunk(nc, *args)
    r = _run(nc, [arrays], core_ids=[0])
    return r.results[0]["out_0"]
```
